# Optimizing a Trainium2 kernel written in Bass

```python
import math
import jax, jax.numpy as jnp
from jax import lax
import numpy as np

"""Two layers of a hybrid diffusion / flow-matching trunk, run for a context pass and a denoising step.

Layer 0 (even): parallel head groups [Hyena order-2 gated long convolution | bidirectional mLSTM]
  sharing one combined input projection and one output projection; dense SwiGLU channel mixer.
Layer 1 (odd): windowed grouped-query attention (+-128 latent tokens plus all context keys, learned
  per-head sink logit, QK-norm, 2-D axial rotary on latent tokens); top-2-of-8 expert SwiGLU.
Every sub-layer: pre-RMSNorm then adaLN shift/scale/gate from SiLU(c) (latent) or SiLU(c_ctx) (context).

Inputs:
  x_prompt (BATCH, SEQ, D_MODEL)            context tokens of new requests
  x_sample (DEC_BATCH, DEC_SEQ, D_MODEL)    noisy latent tokens (grid rows = DEC_SEQ // GRID_W)
  state_C  (DEC_BATCH, N_EVEN, N_DIR, ML_HEADS, ML_HD, ML_HD)  final context mLSTM matrix memory (stabilised)
  state_n  (DEC_BATCH, N_EVEN, N_DIR, ML_HEADS, ML_HD)         final context normaliser
  state_m  (DEC_BATCH, N_EVEN, N_DIR, ML_HEADS)                final context running-max stabiliser
  cache_k, cache_v (DEC_BATCH, N_ODD, ATT_KV, PAST_LEN, ATT_HD) context keys (QK-normed, no rotary) / values
  c (DEC_BATCH, D_MODEL) conditioning, c_ctx (D_MODEL,) learned context modulation vector, then weights.
Output tuple:
  (y_prompt (BATCH, SEQ, D_MODEL), y_sample (DEC_BATCH, DEC_SEQ, D_MODEL),
   new_state_C (BATCH, N_EVEN, N_DIR, ML_HEADS, ML_HD, ML_HD), new_state_n (BATCH, N_EVEN, N_DIR, ML_HEADS, ML_HD),
   new_state_m (BATCH, N_EVEN, N_DIR, ML_HEADS), new_cache_k (BATCH, N_ODD, ATT_KV, SEQ, ATT_HD),
   new_cache_v (BATCH, N_ODD, ATT_KV, SEQ, ATT_HD))
"""

D_MODEL = 1024
BATCH = 1
SEQ = 128
DEPTH = 2
DEC_BATCH = 1
DEC_SEQ = 128
PAST_LEN = 128

GRID_W = 64
N_EVEN = (DEPTH + 1) // 2
N_ODD = DEPTH // 2
N_DIR = 2
HY_W = D_MODEL // 2
HY_ORDER = 2
HY_BANDS = 16
HY_EMB = 1 + 2 * HY_BANDS
HY_FF = 64
ML_W = D_MODEL // 2
ML_HEADS = 4
ML_HD = ML_W // ML_HEADS
ML_CHUNK = 64
EVEN_IN = 3 * HY_W + 4 * ML_W + N_DIR * 2 * ML_HEADS
ATT_HEADS = 16
ATT_HD = D_MODEL // ATT_HEADS
ATT_KV = 4
ATT_G = ATT_HEADS // ATT_KV
WINDOW = 128
QBLOCK = 128
ROPE_BASE = 10000.0
ODD_IN = (ATT_HEADS + 2 * ATT_KV) * ATT_HD
D_FF = 2816
N_EXPERTS = 8
TOP_K = 2
EPS = 1e-6
NEG = -1e30

kernel_name = "hyena_mlstm_swa_moe_diffusion_step"

def rmsnorm(x, g):
    xf = x.astype(jnp.float32)
    y = xf * lax.rsqrt(jnp.mean(xf * xf, axis=-1, keepdims=True) + EPS)
    return (y * g.astype(jnp.float32)).astype(x.dtype)

def adaln(cond, w_ada, b_ada):
    mod = (jax.nn.silu(cond) @ w_ada + b_ada)[..., None, :]
    return jnp.split(mod, 6, axis=-1)

def modulate(x, shift, scale):
    return x * (1 + scale) + shift

def swiglu(x, w1, w3, w2):
    return (jax.nn.silu(x @ w1) * (x @ w3)) @ w2

def short_conv3(x, w):
    L = x.shape[1]
    xp = jnp.pad(x, ((0, 0), (1, 1), (0, 0)))
    return xp[:, :L] * w[0] + xp[:, 1:L + 1] * w[1] + xp[:, 2:] * w[2]

def hyena_filters(L, w1, b1, w2, b2, w3, freq):
    f32 = jnp.float32
    t = jnp.linspace(0.0, 1.0, L, dtype=f32)[:, None]
    w = 2.0 * math.pi * jnp.arange(L, dtype=f32)[:, None] / L
    bands = jnp.linspace(1e-4, HY_BANDS - 1, HY_BANDS, dtype=f32)[None, :]
    z = jnp.concatenate([t, jnp.cos(bands * w), -jnp.sin(bands * w)], axis=-1)
    fr = freq.astype(f32)
    h = jnp.sin(fr[0] * (z @ w1.astype(f32) + b1.astype(f32)))
    h = jnp.sin(fr[1] * (h @ w2.astype(f32) + b2.astype(f32)))
    h = h @ w3.astype(f32)
    max_decay = math.log(1e-2) / 0.3
    min_decay = math.log(1e-2) / 1.5
    deltas = jnp.linspace(min_decay, max_decay, HY_W, dtype=f32)
    decay = jnp.exp(-t * jnp.abs(deltas))
    h = h.reshape(L, HY_ORDER, N_DIR, HY_W) * decay[:, None, None, :]
    h = jnp.moveaxis(h, 0, 2)
    return h / jnp.sum(jnp.abs(h), axis=(1, 2), keepdims=True)

def long_conv(z, h):
    L = z.shape[1]
    k = jnp.concatenate([h[0], jnp.zeros_like(h[0][:1]), h[1][:0:-1]], axis=0)
    zf = jnp.fft.rfft(z, n=2 * L, axis=1)
    kf = jnp.fft.rfft(k, n=2 * L, axis=0)
    return jnp.fft.irfft(zf * kf[None], n=2 * L, axis=1)[:, :L]

def hyena_mixer(u, conv_w, w1, b1, w2, b2, w3, freq, d_skip):
    L = u.shape[1]
    u = short_conv3(u, conv_w).astype(jnp.float32)
    v, x1, x2 = jnp.split(u, 3, axis=-1)
    h = hyena_filters(L, w1, b1, w2, b2, w3, freq)
    d = d_skip.astype(jnp.float32)
    z = x1 * (long_conv(v, h[0]) + d[0] * v)
    z = x2 * (long_conv(z, h[1]) + d[1] * z)
    return z

def mlstm_scan(q, k, v, li, lf, C0, n0, m0):
    B, H, L, d = q.shape
    nc = L // ML_CHUNK
    tri = jnp.tril(jnp.ones((ML_CHUNK, ML_CHUNK), dtype=bool))

    def to_chunks(a):
        a = a.reshape(a.shape[:2] + (nc, ML_CHUNK) + a.shape[3:])
        return jnp.moveaxis(a, 2, 0)

    def step(carry, xs):
        C, n, m = carry
        qc, kc, vc, lic, lfc = xs
        b = jnp.cumsum(lfc, axis=-1)
        dmat = jnp.where(tri, b[..., :, None] - b[..., None, :] + lic[..., None, :], -jnp.inf)
        inter = b + m[..., None]
        m_t = jnp.maximum(inter, jnp.max(dmat, axis=-1))
        w_intra = jnp.exp(dmat - m_t[..., None])
        w_inter = jnp.exp(inter - m_t)
        s = jnp.einsum("bhtd,bhsd->bhts", qc, kc) * w_intra
        num = jnp.einsum("bhts,bhse->bhte", s, vc) + w_inter[..., None] * jnp.einsum("bhtd,bhde->bhte", qc, C)
        den = jnp.sum(s, axis=-1) + w_inter * jnp.einsum("bhtd,bhd->bht", qc, n)
        h = num / jnp.maximum(jnp.abs(den), jnp.exp(-m_t))[..., None]
        b_end = b[..., -1]
        g = b_end[..., None] - b + lic
        m_new = jnp.maximum(b_end + m, jnp.max(g, axis=-1))
        w_tok = jnp.exp(g - m_new[..., None])
        decay = jnp.exp(b_end + m - m_new)
        C_new = decay[..., None, None] * C + jnp.einsum("bhs,bhsd,bhse->bhde", w_tok, kc, vc)
        n_new = decay[..., None] * n + jnp.einsum("bhs,bhsd->bhd", w_tok, kc)
        return (C_new, n_new, m_new), h

    xs = (to_chunks(q), to_chunks(k * (1.0 / math.sqrt(d))), to_chunks(v), to_chunks(li), to_chunks(lf))
    (C, n, m), h = lax.scan(step, (C0, n0, m0), xs)
    h = jnp.moveaxis(h, 0, 2).reshape(B, H, L, d)
    return h, C, n, m

def mlstm_bidir(q, k, v, gates, C0, n0, m0):
    f32 = jnp.float32
    h_sum = jnp.zeros(q.shape, f32)
    Cs, ns, ms = [], [], []
    for dr in range(N_DIR):
        li = jnp.moveaxis(gates[:, :, dr, 0], 1, 2)
        lf = jax.nn.log_sigmoid(jnp.moveaxis(gates[:, :, dr, 1], 1, 2))
        seq = (q, k, v, li, lf)
        if dr == 1:
            seq = tuple(jnp.flip(a, axis=2) for a in seq)
        h, C, n, m = mlstm_scan(*seq, C0[:, dr].astype(f32), n0[:, dr].astype(f32), m0[:, dr].astype(f32))
        if dr == 1:
            h = jnp.flip(h, axis=2)
        h_sum = h_sum + h
        Cs.append(C)
        ns.append(n)
        ms.append(m)
    return h_sum, jnp.stack(Cs, axis=1), jnp.stack(ns, axis=1), jnp.stack(ms, axis=1)

def even_mixer(xm, w_in, conv_w, hy_w1, hy_b1, hy_w2, hy_b2, hy_w3, hy_freq, hy_d,
               b_gate, ml_norm_g, w_out, C0, n0, m0):
    B, L, _ = xm.shape
    f32 = jnp.float32
    u = xm @ w_in
    y_hy = hyena_mixer(u[..., :3 * HY_W], conv_w, hy_w1, hy_b1, hy_w2, hy_b2, hy_w3, hy_freq, hy_d)
    base = 3 * HY_W
    q, k, v, o = (u[..., base + i * ML_W: base + (i + 1) * ML_W] for i in range(4))
    gates = u[..., base + 4 * ML_W:].astype(f32).reshape(B, L, N_DIR, 2, ML_HEADS) + b_gate.astype(f32)
    heads = lambda a: a.reshape(B, L, ML_HEADS, ML_HD).transpose(0, 2, 1, 3).astype(f32)
    h, C, n, m = mlstm_bidir(heads(q), heads(k), heads(v), gates, C0, n0, m0)
    h = rmsnorm(h.transpose(0, 2, 1, 3), ml_norm_g).reshape(B, L, ML_W) * jax.nn.sigmoid(o.astype(f32))
    y = jnp.concatenate([y_hy, h], axis=-1).astype(xm.dtype) @ w_out
    return y, C, n, m

def attn_qkv(xm, w_qkv, q_g, k_g):
    B, L, _ = xm.shape
    u = xm @ w_qkv
    q = u[..., :ATT_HEADS * ATT_HD].reshape(B, L, ATT_HEADS, ATT_HD)
    k = u[..., ATT_HEADS * ATT_HD:(ATT_HEADS + ATT_KV) * ATT_HD].reshape(B, L, ATT_KV, ATT_HD)
    v = u[..., (ATT_HEADS + ATT_KV) * ATT_HD:].reshape(B, L, ATT_KV, ATT_HD)
    return rmsnorm(q, q_g), rmsnorm(k, k_g), v

def rope_2d(x):
    f32 = jnp.float32
    L = x.shape[1]
    n_rows = L // GRID_W
    rows = jnp.repeat(jnp.arange(n_rows), GRID_W).astype(f32)
    cols = jnp.tile(jnp.arange(GRID_W), n_rows).astype(f32)
    half = ATT_HD // 2
    inv = ROPE_BASE ** (-jnp.arange(0, half, 2, dtype=f32) / half)

    def rot(xa, pos):
        ang = pos[:, None] * inv[None, :]
        cos = jnp.cos(ang)[None, :, None, :]
        sin = jnp.sin(ang)[None, :, None, :]
        a1, a2 = jnp.split(xa, 2, axis=-1)
        return jnp.concatenate([a1 * cos - a2 * sin, a1 * sin + a2 * cos], axis=-1)

    xf = x.astype(f32)
    return jnp.concatenate([rot(xf[..., :half], rows), rot(xf[..., half:], cols)], axis=-1).astype(x.dtype)

def attend(qb, K, V, mask, sink):
    logits = jnp.einsum("bqkgd,bksd->bkgqs", qb, K, preferred_element_type=jnp.float32)
    if mask is not None:
        logits = jnp.where(mask, logits, NEG)
    sink_col = jnp.broadcast_to(sink.astype(jnp.float32).reshape(1, ATT_KV, ATT_G, 1, 1), logits.shape[:-1] + (1,))
    p = jax.nn.softmax(jnp.concatenate([sink_col, logits], axis=-1), axis=-1)[..., 1:]
    return jnp.einsum("bkgqs,bksd->bqkgd", p.astype(V.dtype), V)

def q_blocks(q):
    B, L = q.shape[:2]
    qb = q.reshape(B, L // QBLOCK, QBLOCK, ATT_KV, ATT_G, ATT_HD) * (1.0 / math.sqrt(ATT_HD))
    return jnp.moveaxis(qb, 1, 0)

def merge_blocks(out, B, L):
    return jnp.moveaxis(out, 0, 1).reshape(B, L, ATT_HEADS * ATT_HD)

def ctx_attention(q, k, v, sink):
    B, L = q.shape[:2]
    out = lax.map(lambda qi: attend(qi, k, v, None, sink), q_blocks(q))
    return merge_blocks(out, B, L)

def lat_attention(q, k, v, ck, cv, sink):
    B, L = q.shape[:2]
    P = ck.shape[2]
    span = QBLOCK + 2 * WINDOW
    kp = jnp.pad(k, ((0, 0), (0, 0), (WINDOW, WINDOW), (0, 0)))
    vp = jnp.pad(v, ((0, 0), (0, 0), (WINDOW, WINDOW), (0, 0)))
    qpos = jnp.arange(QBLOCK)[:, None]
    rel = jnp.arange(span)[None, :]
    ctx_mask = jnp.ones((QBLOCK, P), dtype=bool)

    def block(args):
        j, qi = args
        start = j * QBLOCK
        kw = lax.dynamic_slice_in_dim(kp, start, span, axis=2)
        vw = lax.dynamic_slice_in_dim(vp, start, span, axis=2)
        t_pos = start + qpos
        s_pos = start - WINDOW + rel
        win = (jnp.abs(t_pos - s_pos) <= WINDOW) & (s_pos >= 0) & (s_pos < L)
        Kc = jnp.concatenate([ck.astype(kw.dtype), kw], axis=2)
        Vc = jnp.concatenate([cv.astype(vw.dtype), vw], axis=2)
        return attend(qi, Kc, Vc, jnp.concatenate([ctx_mask, win], axis=1), sink)

    out = lax.map(block, (jnp.arange(L // QBLOCK), q_blocks(q)))
    return merge_blocks(out, B, L)

def moe_swiglu(x, w_router, b_router, w1, w3, w2):
    B, L, D = x.shape
    xt = x.reshape(B * L, D)
    logits = (xt @ w_router).astype(jnp.float32) + b_router.astype(jnp.float32)
    top_v, top_i = lax.top_k(logits, TOP_K)
    top_w = jax.nn.softmax(top_v, axis=-1)
    gates = jnp.sum(jax.nn.one_hot(top_i, N_EXPERTS, dtype=jnp.float32) * top_w[..., None], axis=1)
    out = jnp.zeros(xt.shape, jnp.float32)
    for e in range(N_EXPERTS):
        out = out + gates[:, e:e + 1] * swiglu(xt, w1[e], w3[e], w2[e]).astype(jnp.float32)
    return out.astype(x.dtype).reshape(B, L, D)

def setup_inputs(seed: int = 0) -> dict:
    key = jax.random.key(seed)
    keys = iter(jax.random.split(key, 48))
    nrm = lambda shape, scale=1.0: jax.random.normal(next(keys), shape, jnp.float32) * scale
    D = D_MODEL
    b_i = nrm((N_EVEN, N_DIR, 1, ML_HEADS), 0.1)
    b_f = jnp.linspace(3.0, 6.0, ML_HEADS, dtype=jnp.float32) + nrm((N_EVEN, N_DIR, 1, ML_HEADS), 0.1)
    return {
        "x_prompt": nrm((BATCH, SEQ, D)),
        "x_sample": nrm((DEC_BATCH, DEC_SEQ, D)),
        "state_C": nrm((DEC_BATCH, N_EVEN, N_DIR, ML_HEADS, ML_HD, ML_HD), 0.05),
        "state_n": nrm((DEC_BATCH, N_EVEN, N_DIR, ML_HEADS, ML_HD), 0.1),
        "state_m": nrm((DEC_BATCH, N_EVEN, N_DIR, ML_HEADS), 0.5),
        "cache_k": nrm((DEC_BATCH, N_ODD, ATT_KV, PAST_LEN, ATT_HD)),
        "cache_v": nrm((DEC_BATCH, N_ODD, ATT_KV, PAST_LEN, ATT_HD)),
        "c": nrm((DEC_BATCH, D)),
        "c_ctx": nrm((D,)),
        "norm1_g": 1.0 + nrm((DEPTH, D), 0.05),
        "norm2_g": 1.0 + nrm((DEPTH, D), 0.05),
        "w_ada": nrm((DEPTH, D, 6 * D), D ** -0.5),
        "b_ada": nrm((DEPTH, 6 * D), 0.01),
        "ev_w_in": nrm((N_EVEN, D, EVEN_IN), D ** -0.5),
        "ev_conv": nrm((N_EVEN, 3, 3 * HY_W), 0.5),
        "hy_w1": nrm((N_EVEN, HY_EMB, HY_FF), HY_EMB ** -0.5),
        "hy_b1": nrm((N_EVEN, HY_FF), 0.1),
        "hy_w2": nrm((N_EVEN, HY_FF, HY_FF), HY_FF ** -0.5),
        "hy_b2": nrm((N_EVEN, HY_FF), 0.1),
        "hy_w3": nrm((N_EVEN, HY_FF, HY_ORDER * N_DIR * HY_W), HY_FF ** -0.5),
        "hy_freq": 1.0 + nrm((N_EVEN, 2, HY_FF), 0.1),
        "hy_d": nrm((N_EVEN, HY_ORDER, HY_W), 0.5),
        "ml_b_gate": jnp.concatenate([b_i, b_f], axis=2),
        "ml_norm_g": 1.0 + nrm((N_EVEN, ML_HEADS, ML_HD), 0.05),
        "ev_w_out": nrm((N_EVEN, HY_W + ML_W, D), (HY_W + ML_W) ** -0.5),
        "ff_w1": nrm((N_EVEN, D, D_FF), D ** -0.5),
        "ff_w3": nrm((N_EVEN, D, D_FF), D ** -0.5),
        "ff_w2": nrm((N_EVEN, D_FF, D), D_FF ** -0.5),
        "at_w_qkv": nrm((N_ODD, D, ODD_IN), D ** -0.5),
        "at_q_g": 1.0 + nrm((N_ODD, ATT_HD), 0.05),
        "at_k_g": 1.0 + nrm((N_ODD, ATT_HD), 0.05),
        "at_sink": nrm((N_ODD, ATT_HEADS), 0.5),
        "at_w_out": nrm((N_ODD, ATT_HEADS * ATT_HD, D), (ATT_HEADS * ATT_HD) ** -0.5),
        "moe_w_router": nrm((N_ODD, D, N_EXPERTS), D ** -0.5),
        "moe_b_router": nrm((N_ODD, N_EXPERTS), 0.01),
        "moe_w1": nrm((N_ODD, N_EXPERTS, D, D_FF), D ** -0.5),
        "moe_w3": nrm((N_ODD, N_EXPERTS, D, D_FF), D ** -0.5),
        "moe_w2": nrm((N_ODD, N_EXPERTS, D_FF, D), D_FF ** -0.5),
    }

def reference(x_prompt, x_sample, state_C, state_n, state_m, cache_k, cache_v, c, c_ctx,
              norm1_g, norm2_g, w_ada, b_ada,
              ev_w_in, ev_conv, hy_w1, hy_b1, hy_w2, hy_b2, hy_w3, hy_freq, hy_d, ml_b_gate, ml_norm_g, ev_w_out,
              ff_w1, ff_w3, ff_w2,
              at_w_qkv, at_q_g, at_k_g, at_sink, at_w_out,
              moe_w_router, moe_b_router, moe_w1, moe_w3, moe_w2):
    f32 = jnp.float32
    xp, xs = x_prompt, x_sample
    to_kv = lambda a: jnp.transpose(a, (0, 2, 1, 3))
    out_C, out_n, out_m, out_k, out_v = [], [], [], [], []
    for layer in range(DEPTH):
        i = layer // 2
        p_sh1, p_sc1, p_g1, p_sh2, p_sc2, p_g2 = adaln(c_ctx, w_ada[layer], b_ada[layer])
        s_sh1, s_sc1, s_g1, s_sh2, s_sc2, s_g2 = adaln(c, w_ada[layer], b_ada[layer])
        hp = modulate(rmsnorm(xp, norm1_g[layer]), p_sh1, p_sc1)
        hs = modulate(rmsnorm(xs, norm1_g[layer]), s_sh1, s_sc1)
        if layer % 2 == 0:
            ev = (ev_w_in[i], ev_conv[i], hy_w1[i], hy_b1[i], hy_w2[i], hy_b2[i], hy_w3[i], hy_freq[i],
                  hy_d[i], ml_b_gate[i], ml_norm_g[i], ev_w_out[i])
            bp = xp.shape[0]
            C0 = jnp.zeros((bp, N_DIR, ML_HEADS, ML_HD, ML_HD), f32)
            n0 = jnp.zeros((bp, N_DIR, ML_HEADS, ML_HD), f32)
            m0 = jnp.zeros((bp, N_DIR, ML_HEADS), f32)
            yp, Cp, n_p, m_p = even_mixer(hp, *ev, C0, n0, m0)
            ys, _, _, _ = even_mixer(hs, *ev, state_C[:, i], state_n[:, i], state_m[:, i])
            out_C.append(Cp)
            out_n.append(n_p)
            out_m.append(m_p)
        else:
            qp, kp, vp = attn_qkv(hp, at_w_qkv[i], at_q_g[i], at_k_g[i])
            kp, vp = to_kv(kp), to_kv(vp)
            out_k.append(kp)
            out_v.append(vp)
            yp = ctx_attention(qp, kp, vp, at_sink[i]) @ at_w_out[i]
            qs, ks_, vs = attn_qkv(hs, at_w_qkv[i], at_q_g[i], at_k_g[i])
            ys = lat_attention(rope_2d(qs), to_kv(rope_2d(ks_)), to_kv(vs), cache_k[:, i], cache_v[:, i],
                               at_sink[i]) @ at_w_out[i]
        xp = xp + p_g1 * yp
        xs = xs + s_g1 * ys
        hp = modulate(rmsnorm(xp, norm2_g[layer]), p_sh2, p_sc2)
        hs = modulate(rmsnorm(xs, norm2_g[layer]), s_sh2, s_sc2)
        if layer % 2 == 0:
            fp = swiglu(hp, ff_w1[i], ff_w3[i], ff_w2[i])
            fs = swiglu(hs, ff_w1[i], ff_w3[i], ff_w2[i])
        else:
            moe = (moe_w_router[i], moe_b_router[i], moe_w1[i], moe_w3[i], moe_w2[i])
            fp = moe_swiglu(hp, *moe)
            fs = moe_swiglu(hs, *moe)
        xp = xp + p_g2 * fp
        xs = xs + s_g2 * fs
    return (xp, xs, jnp.stack(out_C, axis=1), jnp.stack(out_n, axis=1), jnp.stack(out_m, axis=1),
            jnp.stack(out_k, axis=1), jnp.stack(out_v, axis=1))


_drawn_inputs = setup_inputs


def setup_inputs(seed=0):
    import zlib

    import numpy as np

    out = dict(_drawn_inputs(seed))
    spreads = {}
    factors = {'state_C': 3.574,
     'state_n': 3.034,
     'state_m': 3.323,
     'at_sink': 8.0,
     'moe_b_router': 3.257,
     'hy_freq': 7.232,
     'at_q_g': 3.226}
    for name, (base, spread) in spreads.items():
        noise = np.random.default_rng([zlib.crc32(name.encode()), seed]).standard_normal(out[name].shape)
        drawn = base * np.exp(spread * noise) if base else spread * noise
        out[name] = __import__('jax').numpy.asarray(drawn.astype(out[name].dtype))
    for name, factor in factors.items():
        out[name] = (out[name] * factor).astype(out[name].dtype)
    return out
```

```python
from contextlib import ExitStack

import concourse.bass as bass
import numpy as np
from concourse import mybir

ALU = mybir.AluOpType
ACT = mybir.ActivationFunctionType
F32 = mybir.dt.float32
F32R = mybir.dt.float32r
I32 = mybir.dt.int32
AX = mybir.AxisListType.X

P = 128
D = 1024
KD = D // P
G = 2
T = 128
HW = 512
NH = 4
HD = 128
NDIR = 2
FF = 2816
NE = 8
QH, KV, AHD = 16, 4, 64
ROWS = 40
TW = 256
RING = 11
RAW = 4
SPL = 3
NCH = FF // TW
NFW = 3 * NCH
HALFK = KD // 2
XB = 4
EPS = 1e-6
NEG = -1e30
TWO_PI = 2.0 * np.pi
RND = float(1.5 * 2 ** 23)

CONST_COLS = {}


def _columns():
    at = 0
    for name, n in (("ident", P), ("prefix", P), ("mask", 2 * P), ("iota", 2 * P), ("shift", 2 * P),
                    ("fc", P), ("fsn", P), ("fs0", P), ("fd", P), ("gc", P), ("gs0", P), ("gd", P),
                    ("ic", P), ("is", P), ("decay", HW), ("zt", P), ("cos", 32), ("sin", 32), ("tri", 64),
                    ("eps", 1), ("one", 1)):
        CONST_COLS[name] = (at, n)
        at += n
    return at


NCONST = _columns()


def constants():
    c = np.zeros((P, NCONST), np.float64)

    def put(name, a):
        at, n = CONST_COLS[name]
        c[:a.shape[0], at:at + n] = a.reshape(a.shape[0], n)

    i = np.arange(P)
    put("ident", np.eye(P))
    put("prefix", (i[:, None] <= i[None, :]).astype(float))
    put("mask", np.stack([np.where(i[:, None] <= i[None, :], 0, NEG),
                          np.where(i[:, None] >= i[None, :], 0, NEG)], 1))
    put("iota", np.broadcast_to(np.arange(2 * P)[None], (P, 2 * P)).copy())
    put("shift", np.stack([(i[:, None] == i[None, :] - 1), (i[:, None] == i[None, :] + 1)], 1).astype(float))
    n2 = 2 * T
    ang = 2 * np.pi * ((i[:, None] * i[None, :]) % n2) / n2
    alt = (-1.0) ** i
    cosm, sinm = np.cos(ang), -np.sin(ang)
    sin_ny, cos_ny = sinm.copy(), cosm.copy()
    sin_ny[:, 0] = alt
    cos_ny[:, 0] = alt
    put("fc", cosm)
    put("fsn", sin_ny)
    put("fs0", sinm)
    put("fd", cos_ny)
    keep = (i > 0).astype(float)[:, None]
    put("gc", cosm * keep)
    put("gs0", -sinm * keep)
    put("gd", cos_ny * keep)
    wt = np.where(i == 0, 1.0, 2.0)[:, None] / n2
    inv_s = 2 * sinm / n2
    inv_s[0, :] = alt / n2
    put("ic", cosm * wt)
    put("is", inv_s)
    f32 = np.float32
    t = np.linspace(0.0, 1.0, T, dtype=f32)[:, None]
    w = (2.0 * np.pi * np.arange(T, dtype=f32)[:, None] / T).astype(f32)
    bands = np.linspace(1e-4, 15, 16, dtype=f32)[None]
    z = np.concatenate([t, np.cos(bands * w), -np.sin(bands * w)], -1)
    put("zt", z.T)
    deltas = np.linspace(np.log(1e-2) / 1.5, np.log(1e-2) / 0.3, HW, dtype=f32)
    put("decay", np.exp(-t * np.abs(deltas)))
    inv = (10000.0 ** (-np.arange(0, 32, 2, dtype=f32) / 32)).astype(f32)
    pos = np.stack([i // 64, i % 64], 1).astype(f32)
    a = pos[:, :, None] * inv[None, None]
    put("cos", np.cos(a))
    put("sin", np.sin(a))
    j = np.arange(NE)
    put("tri", np.broadcast_to((j[None, :] < j[:, None]).astype(float)[None], (P, NE, NE)).copy())
    put("eps", np.full((P, 1), EPS))
    put("one", np.ones((P, 1)))
    return c.astype(np.float32)


def trunk(nc, a, o):
    with ExitStack() as ctx:
        ctx.enter_context(nc.allow_non_contiguous_dma(reason="vectors of at most 4 KB into columns"))

        def sb(name, shape, dt=F32):
            return ctx.enter_context(nc.sbuf_tensor(name, shape, dt))

        def sem(name):
            return ctx.enter_context(nc.semaphore(name))

        bank = [ctx.enter_context(nc.psum_tensor(f"bank{i}", [P, 512], F32)) for i in range(8)]

        raw = sb("raw", [P, RAW, 2048])
        cst = sb("cst", [P, NCONST])
        x = sb("x", [P, G, D])
        hT = sb("hT", [P, KD, G * T])
        xn = sb("xn", [P, G, D])
        Gb = sb("Gb", [P, G, D])
        stage = sb("stage", [2, 2, TW])
        condT = sb("condT", [P, KD, G])
        modb = sb("modb", [P, 2, 48])
        modc = sb("modc", [P, 2, 6, KD, G])
        ngc = sb("ngc", [P, 4, KD])
        sca = sb("sca", [P, 4, KD, G])
        ones = sb("ones", [P, P])
        ssq = sb("ssq", [P, 8])
        rt = sb("rt", [P, 8])
        rstd = sb("rstd", [P, 8])
        gzero = sb("gzero", [P, 2, G, ROWS])
        gb = sb("gb", [ROWS, 2])
        m0 = sb("m0", [ROWS, 1])
        cols = sb("cols", [P, 4, 64])
        sml = sb("sml", [P, 256])
        hyp = sb("hyp", [64, 64 + 8])
        hyw1 = sb("hyw1", [33, 64])
        nst = sb("nst", [P, 16])
        msm = sb("msm", [P, 96])
        mlx = sb("mlx", [ROWS, 2])
        flag = sb("flag", [1, 1], I32)
        SPARE = (RING - RAW - 2 * SPL) * 2048
        with nc.sbuf_tensor("raw_more", [P, RING - RAW, 2048], F32) as raw_more, \
                nc.sbuf_tensor("arena", [P, 16896], F32) as arena:
            pass
        w_hi = sb("w_hi", [P, SPL, 2048], F32R)
        w_lo = sb("w_lo", [P, SPL, 2048], F32R)
        sb("spare", [P, SPARE])
        x_hi = sb("x_hi", [P, KD, G * T], F32R)
        x_lo = sb("x_lo", [P, KD, G * T], F32R)
        sb("arena_low", [P, 12800 - 4096])
        g_hi = sb("g_hi", [P, 2, TW], F32R)
        g_lo = sb("g_lo", [P, 2, TW], F32R)
        sb("arena_high", [P, 16896 - 12800 - 4 * TW])

        def C(name, rows=P):
            at, n = CONST_COLS[name]
            return cst[0:rows, at:at + n]

        ident = C("ident")

        def ar(at, n):
            return arena[:, at:at + n]

        u = ar(0, 3072).rearrange("p (g n) -> p g n", g=G)
        convw = ar(3072, 4608).rearrange("p (w n) -> p w n", w=3)
        spec = ar(7680, 3072).rearrange("p (o i n) -> p o i n", o=2, i=3)
        vrow = ar(10752, 1024).rearrange("p (g n) -> p g n", g=G)
        sigo = ar(11776, 1024).rearrange("p (g n) -> p g n", g=G)
        qT = ar(12800, 1024).rearrange("p (h n) -> p h n", h=NH)
        kT = ar(13824, 1024).rearrange("p (h n) -> p h n", h=NH)
        hy1 = ar(14848, 2048).rearrange("p (i n) -> p i n", i=4)
        hyT = [Gb[:, :, :].rearrange("p g (i n) -> p (g i) n", i=2), hy1]
        taps = ar(10752, 2048).rearrange("p (i n) -> p i n", i=4)
        mags = ar(12800, 2048).rearrange("p (i n) -> p i n", i=4)
        hyhw3 = arena[0:64, 14848:16896]
        skip = Gb[0:1, 0, 0:1024]
        sinb = ar(0, 1024).rearrange("p (i n) -> p i n", i=8)
        rowq = hy1[0:ROWS, :, :].rearrange("p i n -> p (i n)").rearrange("p (i n) -> p i n", i=16)
        WT = ar(3072, 2048).rearrange("p (c n) -> p c n", c=16)
        ST = ar(5120, 2048).rearrange("p (c n) -> p c n", c=16)
        selr = xn[0:ROWS, :, :].rearrange("p g n -> p (g n)").rearrange("p (c n) -> p c n", c=16)
        kw = hy1[:, 0:2, :].rearrange("p i n -> p (i n)").rearrange("p (d h n) -> p d h n", d=NDIR, h=NH)
        cout = ar(13824, 1024).rearrange("p (d n) -> p d n", d=NDIR)
        stateC = ar(3072, 1024).rearrange("p (d h n) -> p d h n", d=NDIR, h=NH)
        mgain = ar(4096, 512)

        qkv = ar(0, 3072).rearrange("p (g n) -> p g n", g=G)
        rtmp = ar(3072, 2560).rearrange("p (i n) -> p i n", i=4)
        aqT = ar(5632, 2048).rearrange("p (j n) -> p j n", j=8)
        akT = [ar(c, 1024).rearrange("p (v n) -> p v n", v=KV) for c in (7680, 4096)]
        ckd = ar(8704, 512).rearrange("p (v d n) -> p v d n", v=KV, d=2)
        ckT = [ar(c, 512).rearrange("p (v n) -> p v n", v=KV) for c in (9216, 5120)]
        kd = ar(3072, 1024).rearrange("p (g v d n) -> p g v d n", g=G, v=KV, d=2)
        cv = ar(9728, 256)
        Pb = [ar(9984, 1536), ar(11520, 1536)]
        PTb = [ar(13056, 1536), ar(14592, 1536)]
        qkg = ar(16128, 128)
        sinkb = ar(16256, 16)
        Psel = [ar(4096 + 256 * i, 256).rearrange("p (g n) -> p g n", g=G) for i in range(2)]
        PselT = [ar(5120 + 256 * i, 256) for i in range(2)]
        ys = ar(6144, 1024)
        acc = ar(8192, 2048).rearrange("p (g n) -> p g n", g=G)
        sa = [ar(10240 + 256 * i, 256) for i in range(2)]
        grow = [ar(10752 + 256 * i, 256) for i in range(2)]
        tmpf = ar(11264, 1024).rearrange("p (i n) -> p i n", i=2)
        rw = ar(12288, 512)
        tmpr = ar(14848, 1024).rearrange("p (i n) -> p i n", i=2)

        slot = [sem(f"slot{i}_filled") for i in range(RING)]
        tile_used = sem("tile_used")
        ld_c = sem("ld_cond")
        ld_k = sem("ld_constants")
        ld_x = sem("ld_x")
        ld_a = sem("ld_adaln")
        ld_h = sem("ld_hyena")
        ld_h2 = sem("ld_hyena_skip")
        ld_g = sem("ld_gate_rows")
        ld_cw = sem("ld_conv")
        ld_n = sem("ld_states")
        ld_C = sem("ld_state_C")
        ld_mg = sem("ld_mlstm_gain")
        ld_at = sem("ld_attention")
        ld_r = sem("ld_router")
        pz = sem("pool_zeroed")
        dve = sem("dve_chain")
        act = sem("act_chain")
        stored = sem("outputs_stored")
        stored_st = sem("states_stored")
        stored_kv = sem("keys_values_stored")
        cond_ok = sem("cond_silu")
        ada_stg = sem("ada_rows_staged")
        ada_col = sem("ada_columns_made")
        modc_ok = sem("modc_ready")
        f_mm = sem("filter_products")
        f_arg = sem("filter_sine_args")
        f_sin = sem("filter_sines")
        f_tap = sem("filter_taps")
        f_abs = sem("filter_magnitudes")
        f_nrm = sem("filter_normalised")
        f_spec = sem("filter_spectra")
        f_spt = sem("filter_spectra_taken")
        n_rt = sem("norm_root")
        resid = sem("residual_updated")
        rows_ok = sem("rows_ready")
        turned = sem("rows_turned")
        hT_a = sem("hT_by_act")
        hT_d = sem("hT_by_dve")
        tj_t = sem("projection_taken")
        g_rows = sem("gate_rows_ready")
        g_in = sem("gate_rows_taken")
        g_f = sem("forget_exp_log")
        g_mu = sem("gate_scans")
        g_ex = sem("gate_exps")
        g_col = sem("gate_columns")
        g_colt = sem("gate_columns_taken")
        sel_ok = sem("row_selectors")
        qk_ok = sem("qk_ready")
        kr_ok = sem("k_rows_turned")
        kw_ok = sem("k_weighted")
        wt_mm = sem("weight_logs")
        wt_ok = sem("weights_exp")
        st_ok = sem("scores_ready")
        nu_ok = sem("numerator_ready")
        nu_t = sem("numerator_taken")
        cs_ok = sem("states_ready")
        cs_t = sem("states_taken")
        hs_q = sem("head_squares")
        hs_r = sem("head_roots")
        so_ok = sem("sigmoid_o")
        cw_ok = sem("conv_taps_applied")
        cv_mm = sem("conv_shifted")
        cv_ok = sem("conv_done")
        fz_mm = sem("dft_ready")
        fz_ok = sem("spectrum_product")
        iz_mm = sem("inverse_ready")
        iz_ok = sem("hyena_gated")
        gbs = sem("gate_broadcast_source")
        gbm = sem("gate_broadcast_made")
        gbt = sem("gate_broadcast_taken")
        ro_t = sem("out_projection_taken")
        q_sq = sem("qk_squares")
        q_rt = sem("qk_roots")
        q_ok = sem("qk_normed")
        k_dup = sem("k_doubled")
        at_t = sem("attention_turned")
        at_ta = sem("attention_turned_by_act")
        at_td = sem("attention_turned_by_dve")
        sc_mm = sem("logits_ready")
        sc_m = sem("logits_max")
        sc_e = sem("probs_ready")
        sk_e = sem("sink_exp")
        pt_mm = sem("probs_turned")
        pt_t = sem("probs_turned_taken")
        pv_mm = sem("values_mixed")
        pv_t = sem("values_taken")
        r_mm = sem("router_logits")
        r_l = sem("router_shifted")
        r_e = sem("router_exp")
        r_sel = sem("router_selected")
        r_pos = sem("router_positions")
        r_ok = sem("router_tables")
        hr_mm = sem("token_rows_turned")
        hr_t = sem("token_rows_taken")
        p_ok = sem("selector_built")
        gj = sem("gather_ready")
        gj_t = sem("selector_turned_taken")
        x_h = sem("input_high_parts")
        x_l = sem("input_low_parts")
        cb = sem("combine_ready")
        cb_t = sem("combine_taken")
        hi_ok = sem("weight_high_parts")
        lo_ok = sem("weight_low_parts")
        split_used = sem("split_tile_used")
        h_sa = sem("hidden_silu")
        h_g = sem("hidden_gated")
        h_t = sem("hidden_turned")
        gh_ok = sem("hidden_high_parts")
        gl_ok = sem("hidden_low_parts")
        y_a = sem("ffn_taken_by_act")
        y_d = sem("ffn_taken_by_dve")
        fin = sem("output_rows")

        w_in = a["ev_w_in"][0]

        def kmaj(w, c0, n=TW):
            return w[:, c0:c0 + n].rearrange("(k p) n -> p k n", p=P)

        base_q, base_v, base_o, base_g = 3 * HW, 3 * HW + 2 * HW, 3 * HW + 3 * HW, 3 * HW + 4 * HW
        stream = [kmaj(a["w_ada"][0], TW * i) for i in range(24)]
        stream += [kmaj(w_in, base_g, 16)]
        stream += [kmaj(w_in, base_q + TW * i) for i in range(4)]
        stream += [kmaj(w_in, base_v + TW * i) for i in range(2)]
        stream += [kmaj(w_in, base_o + TW * i) for i in range(2)]
        stream += [kmaj(w_in, TW * i) for i in range(6)]
        stream += [kmaj(a["w_ada"][1], TW * i) for i in range(24)]
        stream += [kmaj(a["ev_w_out"][0], TW * i) for i in range(4)]
        NA = len(stream)
        late = [kmaj(a["at_w_qkv"][0], TW * i) for i in range(6)]
        late += [kmaj(a["at_w_out"][0], TW * i) for i in range(4)]
        IN0, ADA1, WOUT = 24, 39, 63
        QKV0, AOUT = NA, NA + 6
        GATHERS = NE + 1
        MOE0 = NFW + len(late)
        assert XB * NFW % RAW == 0 and XB * NFW % SPL == 0 and NFW % SPL == 0 and NE % XB == 0

        def place_of(n):
            if n < NA:
                s, more = n % RING, 16 * (n // RING + 1)
            else:
                s, more = late_at(n - NA + NFW)
            return (raw[:, s, :] if s < RAW else raw_more[:, s - RAW, :]), slot[s], more

        def late_at(j):
            s = j % RAW
            return s, 16 * len(range(s, NA, RING)) + 32 * (j // RAW + 1)

        def tile(n, k=KD):
            return place_of(n)[0].rearrange("p (k n) -> p k n", k=k)

        def ada_bank(i):
            return i % 2 if i < 24 else 0

        FFN0 = (G, None, 0, 0, 0)

        def expert(p, i, r):
            e = r * NE + i
            return (1, p, G * NCH + NCH * e, NFW * (1 + e), MOE0 + NFW * e)

        def plus(p, step, n):
            return n if p is None else p * step + n

        def n_unit(f, c, g=0):
            return plus(f[1], XB * NCH, f[2] + f[0] * c + g + 1)

        def n_split(f, i):
            return plus(f[1], XB * NFW, f[3] + i + 1)

        def at_a(c):
            return 3 * c - (c > 0)

        def at_b(c):
            return 3 * c + (c == 0)

        def at_w(c):
            return min(3 * c + 4, NFW - 1)

        def order():
            for c in range(NCH):
                yield "A", c
                yield "B", c
                if c:
                    yield "W", c - 1
            yield "W", NCH - 1

        for n_, (kind_, c_) in enumerate(order()):
            assert n_ == {"A": at_a, "B": at_b, "W": at_w}[kind_](c_)

        def unit_at(f, c, g):
            b = g if f[0] == G else c % 2
            return b, bank[b], bank[2 + g] if f[0] == G else bank[6 + b]

        STATE_STORES = 16 * (NDIR + 2)

        block = ctx.enter_context(nc.Block())

        @block.sync
        def _(sp):
            for n, src in enumerate(stream):
                if n >= RING:
                    sp.wait_ge(tile_used, n - RING + 1)
                k, w = src.shape[1], src.shape[2]
                dst, filled, _ = place_of(n)
                sp.dma_start(dst[:, 0:k * w].rearrange("p (k n) -> p k n", k=k), src).then_inc(filled, 16)

            def load(j, kind, c, w1, w3, w2):
                s = j % RAW
                cols_, rows_ = slice(TW * c, TW * c + TW), slice(HALFK * (kind == "B"), HALFK * (kind == "B") + HALFK)
                if kind == "W":
                    for i in range(2):
                        sp.dma_start(raw[:, s, D * i:D * i + D], w2(2 * c + i)).then_inc(slot[s], 16)
                else:
                    t = raw[:, s, :].rearrange("p (k n) -> p k n", k=HALFK)
                    sp.dma_start(t[:, :, 0:TW], w1(rows_, cols_)).then_inc(slot[s], 16)
                    sp.dma_start(t[:, :, TW:2 * TW], w3(rows_, cols_)).then_inc(slot[s], 16)

            w1 = a["ff_w1"][0].rearrange("(k p) n -> p k n", p=P)
            w3 = a["ff_w3"][0].rearrange("(k p) n -> p k n", p=P)
            w2 = a["ff_w2"][0].rearrange("(j p) n -> p j n", p=P)
            for j, (kind, c) in enumerate(order()):
                if j < RAW:
                    sp.wait_ge(tile_used, range(j, NA, RING)[-1] + 1)
                else:
                    sp.wait_ge(lo_ok, j - RAW + 1)
                load(j, kind, c, lambda r, n: w1[:, r, n], lambda r, n: w3[:, r, n], lambda i: w2[:, i, :])
            for i, src in enumerate(late):
                j = NFW + i
                if i < RAW:
                    sp.wait_ge(lo_ok, j - RAW + 1)
                else:
                    sp.wait_ge(tile_used, QKV0 + i - RAW + 1)
                for h in range(2):
                    t = raw[:, j % RAW, D * h:D * h + D].rearrange("p (k n) -> p k n", k=HALFK)
                    sp.dma_start(t, src[:, HALFK * h:HALFK * h + HALFK, :]).then_inc(slot[j % RAW], 16)
            e1 = a["moe_w1"][0].rearrange("e (k p) n -> e p k n", p=P)
            e3 = a["moe_w3"][0].rearrange("e (k p) n -> e p k n", p=P)
            e2 = a["moe_w2"][0].rearrange("e (j p) n -> e p j n", p=P)

            def experts(r):
                with sp.Fori(0, NE // XB) as p:
                    for i in range(XB):
                        f = expert(p, i, r)
                        e = bass.ds(p * XB + i, 1)
                        for n, (kind, c) in enumerate(order()):
                            if r == 0 and i == 0 and n < RAW:
                                sp.wait_ge(tile_used, QKV0 + len(late) - RAW + n + 1)
                            sp.wait_ge(lo_ok, n_split(f, n - RAW))
                            load(f[4] + n, kind, c,
                                 lambda rr, nn: e1[e, :, rr, nn].rearrange("a p k n -> p (a k) n"),
                                 lambda rr, nn: e3[e, :, rr, nn].rearrange("a p k n -> p (a k) n"),
                                 lambda jj: e2[e, :, jj, :].rearrange("a p n -> p (a n)"))

            experts(0)
            sp.wait_ge(r_ok, 1)
            crowded = sp.value_load(flag[0:1, 0:1], min_val=0, max_val=1)
            with sp.If(crowded > 0):
                experts(1)
            sp.wait_ge(stored_st, STATE_STORES)
            sp.wait_ge(stored_kv, 32)
            sp.wait_ge(stored, 32)


        @block.gpsimd
        def _(pool):
            gp = nc.gpsimd
            gp.memset(gzero[:], 0.0).then_inc(pz, 1)
            gp.memset(gb[:], 0.0).then_inc(pz, 1)
            gp.memset(m0[:], 0.0).then_inc(pz, 1)
            gp.memset(ones[:], 1.0).then_inc(pz, 1)
            gp.dma_start(hyw1[:], a["hy_w1"][0]).then_inc(ld_h, 16)
            gp.dma_start(hyp[:, 0:64], a["hy_w2"][0]).then_inc(ld_h, 16)
            gp.dma_start(hyp[:, 64:65], a["hy_b1"].rearrange("a n -> n a")).then_inc(ld_h, 16)
            gp.dma_start(hyp[:, 65:66], a["hy_b2"].rearrange("a n -> n a")).then_inc(ld_h, 16)
            gp.dma_start(hyp[:, 66:68], a["hy_freq"][0].rearrange("a n -> n a")).then_inc(ld_h, 16)
            gp.dma_start(hyhw3, a["hy_w3"][0]).then_inc(ld_h, 16)
            gp.dma_start(skip, a["hy_d"].rearrange("a o n -> a (o n)")).then_inc(ld_h2, 16)
            gp.dma_start(modb[:], a["b_ada"].rearrange("l (j p) -> p l j", p=P)).then_inc(ld_a, 16)
            gp.dma_start(ngc[:, 0:2, :], a["norm1_g"].rearrange("l (k p) -> p l k", p=P)).then_inc(ld_a, 16)
            gp.dma_start(ngc[:, 2:4, :], a["norm2_g"].rearrange("l (k p) -> p l k", p=P)).then_inc(ld_a, 16)
            gp.dma_start(convw, a["ev_conv"][0].rearrange("(a w) n -> a w n", a=1).to_broadcast([P, 3, 3 * HW])
                         ).then_inc(ld_cw, 16)
            pool.wait_ge(pz, 4)
            for d in range(NDIR):
                for g in range(G):
                    r = 32 * d + 4 * g
                    gp.dma_start(gb[r:r + 4, :], a["ml_b_gate"][0, d].rearrange("f h -> h f")).then_inc(ld_g, 16)
                gp.dma_start(m0[32 * d + 4:32 * d + 8, :],
                             a["state_m"][0, 0, d].rearrange("(h a) -> h a", a=1)).then_inc(ld_g, 16)
                gp.dma_start(nst[:, 4 * d:4 * d + 4], a["state_n"][0, 0, d].rearrange("h n -> n h")
                             ).then_inc(ld_n, 16)
            gp.dma_start(msm[:, 0:64].rearrange("p (k n) -> p k n", k=KD),
                         a["moe_w_router"][0].rearrange("(k p) n -> p k n", p=P)).then_inc(ld_r, 16)
            gp.dma_start(msm[:, 64:72], a["moe_b_router"].to_broadcast([P, NE])).then_inc(ld_r, 16)
            pool.wait_ge(st_ok, 4)
            gp.dma_start(stateC.rearrange("p d h n -> p (d h) n"), a["state_C"][0, 0].rearrange("d h i j -> i (d h) j")).then_inc(ld_C, 16)
            gp.dma_start(mgain, a["ml_norm_g"].rearrange("a h n -> a (h n)").to_broadcast([P, HW])
                         ).then_inc(ld_mg, 16)
            pool.wait_ge(resid, 2)
            for d in range(2):
                gp.dma_start(ckd[:, :, d, :], a["cache_k"][0, 0].rearrange("v s n -> s v n")).then_inc(ld_at, 16)
            gp.dma_start(cv.rearrange("p (v n) -> p v n", v=KV), a["cache_v"][0, 0].rearrange("v s n -> s v n")
                         ).then_inc(ld_at, 16)
            gp.dma_start(qkg[:, 0:64], a["at_q_g"].to_broadcast([P, AHD])).then_inc(ld_at, 16)
            gp.dma_start(qkg[:, 64:128], a["at_k_g"].to_broadcast([P, AHD])).then_inc(ld_at, 16)
            gp.dma_start(sinkb, a["at_sink"].to_broadcast([P, QH])).then_inc(ld_at, 16)

        @block.scalar
        def _(eng):
            sc = nc.scalar
            n_chain = [0]

            def link(ins):
                n_chain[0] += 1
                ins.then_inc(act, 1)
                eng.wait_ge(act, n_chain[0])

            eng.dma_start(condT[:, :, 0:1], a["c_ctx"].rearrange("(k p a) -> p k a", p=P, a=1)).then_inc(ld_c, 16)
            eng.dma_start(condT[:, :, 1:2], a["c"].rearrange("a (k p) -> p k a", p=P)).then_inc(ld_c, 16)
            eng.dma_start(cst[:], a["constants"]).then_inc(ld_k, 16)
            eng.dma_start(x[:, 0, :], a["x_prompt"][0]).then_inc(ld_x, 16)
            eng.dma_start(x[:, 1, :], a["x_sample"][0]).then_inc(ld_x, 16)
            eng.wait_ge(ld_c, 32)
            sc.activation(condT[:], condT[:], ACT.Silu).then_inc(cond_ok, 1)

            def stage_row(i):
                eng.wait_ge(tile_used, (i if i < 24 else ADA1 + i - 24) + 1)
                if i >= 2:
                    eng.wait_ge(ada_col, i - 1)
                sc.copy(stage[:, i % 2, :], bank[ada_bank(i)][0:2, 0:TW]).then_inc(ada_stg, 1)

            def norm_root(i):
                if i == 0:
                    eng.wait_ge(ld_x, 32)
                    eng.wait_ge(ld_k, 16)
                else:
                    eng.wait_ge(resid, i)
                for g in range(G):
                    link(sc.activation(xn[:, g, :], x[:, g, :], ACT.Square, accum_out=ssq[:, 2 * i + g:2 * i + g + 1]))
                sc.activation(rt[:, 2 * i:2 * i + 2], ssq[:, 2 * i:2 * i + 2], ACT.Sqrt, bias=C("eps"),
                              scale=1.0 / D).then_inc(n_rt, 1)

            def take_turned(s, norm):
                for half in range(2):
                    eng.wait_ge(turned, 4 * s + half + 1)
                    if norm is not None:
                        l, part = norm % 2, 3 * (norm // 2)
                        eng.wait_ge(modc_ok, l + 1)
                    for j in range(4):
                        k = 4 * half + j
                        src = bank[4 + half][:, P * j:P * j + P]
                        if norm is None:
                            if j == 0:
                                ins = sc.copy(hT[:, 4 * half:4 * half + 4, 0:T],
                                              bank[4 + half][:, :].rearrange("p (j n) -> p j n", j=4))
                        else:
                            ins = sc.activation(hT[:, k, 0:T], src, ACT.Identity,
                                                bias=modc[:, l, part, k, 0:1], scale=sca[:, norm, k, 0:1])
                    ins.then_inc(hT_a, 1)

            def gate_rows_out(s):
                for q in range(4):
                    eng.wait_ge(gbm, 4 * s + q + 1)
                    sc.copy(Gb[:, q // 2, 512 * (q % 2):512 * (q % 2) + 512], bank[4 + q][:, :]).then_inc(gbt, 1)

            def high(f, i):
                s, count = late_at(f[4] + i)
                eng.wait_ge(slot[s], plus(f[1], XB * NFW // RAW * 32, count))
                if f is FFN0 and i < SPL:
                    eng.wait_ge(tile_used, NA)
                else:
                    eng.wait_ge(split_used, n_split(f, i - SPL))
                sc.copy(w_hi[:, (f[3] + i) % SPL, :], raw[:, s, :]).then_inc(hi_ok, 1)

            def silu(f, c):
                eng.wait_ge(split_used, n_split(f, at_b(c)))
                for g in range(f[0]):
                    b, up, _ = unit_at(f, c, g)
                    if f is not FFN0 or c > 0:
                        eng.wait_ge(h_g, n_unit(f, c - (1 if f is FFN0 else 2), g))
                    sc.activation(sa[b], up[:, 0:TW], ACT.Silu).then_inc(h_sa, 1)

            def hidden_high(f, c):
                for g in range(f[0]):
                    b, _, turn = unit_at(f, c, g)
                    eng.wait_ge(h_t, n_unit(f, c, g))
                    sc.copy(g_hi[:, b, :], turn[:, 0:TW]).then_inc(gh_ok, 1)

            def chunk(f, c):
                if c:
                    hidden_high(f, c - 1)
                high(f, at_a(c + 1) if c < NCH - 1 else at_w(c))
                silu(f, c)
                if c < NCH - 1:
                    high(f, at_b(c + 1))
                    high(f, at_w(c))

            for i in range(24):
                stage_row(i)
                if i in (5, 9):
                    n = 0 if i == 5 else 1
                    eng.wait_ge(f_arg, n + 1)
                    sc.activation(sinb[0:64, 4 + n, :], sinb[0:64, 3, :], ACT.Sin).then_inc(f_sin, 1)
                if i == 13:
                    eng.wait_ge(f_tap, 1)
                    for q in range(4):
                        ins = sc.activation(mags[:, q, :], taps[:, q, :], ACT.Abs)
                    ins.then_inc(f_abs, 1)
                if i >= 18:
                    q = i - 18
                    eng.wait_ge(f_spec, q + 1)
                    sc.copy(spec[:, q // 3, q % 3, :], bank[4 + q % 2][:, :]).then_inc(f_spt, 1)
                if i == 10:
                    norm_root(0)
            take_turned(0, 0)


            def take_proj(j, fn):
                eng.wait_ge(tile_used, (IN0 + j if j < 15 else QKV0 + j - 15) + 1)
                fn(bank[j % 3]).then_inc(tj_t, 1)

            def spread_gates(b):
                eng.wait_ge(pz, 4)
                v = b[:, 0:32].rearrange("p (g d f h) -> p g d f h", g=G, d=2, f=2)
                for g in range(G):
                    for d in range(NDIR):
                        r = 32 * d + 4 * g
                        ins = sc.copy(gzero[:, :, g, r:r + 4], v[:, g, d, :, :])
                return ins

            def two_heads(dst, i):
                return lambda b: sc.copy(dst[:, 2 * i:2 * i + 2, :], b[:, :].rearrange("p (h n) -> p h n", h=2))

            def cols_of(dst, c0):
                return lambda b: sc.copy(dst[:, :, c0:c0 + TW], b[:, :].rearrange("p (g n) -> p g n", g=G))

            take_proj(0, spread_gates)
            take_proj(1, two_heads(qT, 0))
            take_proj(2, two_heads(qT, 1))
            eng.wait_ge(g_in, 1)
            link(sc.activation(rowq[:, 2, :], rowq[:, 1, :], ACT.Abs))
            link(sc.activation(rowq[:, 3, :], rowq[:, 2, :], ACT.Exp, scale=-1.0))
            sc.activation(rowq[:, 8, :], rowq[:, 3, :], ACT.Ln, bias=C("one", ROWS)).then_inc(g_f, 1)
            take_proj(3, two_heads(kT, 0))
            take_proj(4, two_heads(kT, 1))
            eng.wait_ge(g_mu, 1)
            sc.activation(rowq[:, 9, :], rowq[:, 6, :], ACT.Exp, bias=m0[:, 0:1], scale=-1.0)
            sc.activation(rowq[:, 10, :], rowq[:, 7, :], ACT.Exp, scale=-1.0)
            sc.activation(rowq[:, 11, :], rowq[:, 5, :], ACT.Exp, bias=mlx[:, 1:2]).then_inc(g_ex, 1)
            for d in range(NDIR):
                eng.dma_start(o["m"][0, 0, d].rearrange("(h a) -> h a", a=1), mlx[32 * d:32 * d + 4, 0:1]
                              ).then_inc(stored_st, 16)
            take_proj(5, cols_of(vrow, 0))
            take_proj(6, cols_of(vrow, TW))
            for i in range(2):
                take_proj(7 + i, lambda b: sc.activation(sigo[:, :, TW * i:TW * i + TW],
                                                         b[:, :].rearrange("p (g n) -> p g n", g=G), ACT.Sigmoid))
            for i in range(6):
                take_proj(9 + i, cols_of(u, TW * i))

            for i in range(24, 30):
                stage_row(i)
            for q in range(4):
                eng.wait_ge(g_colt, 1)
                eng.wait_ge(cv_ok, 6)
                eng.wait_ge(wt_mm, q + 1)
                d, g = q // 2, q % 2
                for h in range(NH):
                    r = 32 * d + 4 * g + h
                    ins = sc.activation(WT[:, 4 * q + h, :], bank[4 + q % 2][:, P * h:P * h + P], ACT.Exp,
                                        bias=cols[:, 0, r:r + 1])
                ins.then_inc(wt_ok, 1)
                if q % 2:
                    stage_row(30 + q // 2)
            for i in range(32, 36):
                stage_row(i)
            for d in range(NDIR):
                eng.wait_ge(cs_ok, d + 1)
                sc.copy(cout[:, d, :], bank[4 + d][:, :]).then_inc(cs_t, 1)
            sc.copy(sml[:, 240:248], bank[3][:, 288:296]).then_inc(cs_t, 1)
            eng.wait_ge(hs_q, 1)
            sc.activation(sml[:, 40:48], sml[:, 32:40], ACT.Sqrt, bias=C("eps"), scale=1.0 / HD).then_inc(hs_r, 1)
            eng.wait_ge(cs_t, 3)
            eng.dma_start(o["C"][0, 0].rearrange("d h i j -> i (d h) j"),
                          cout.rearrange("p d (h j) -> p (d h) j", h=NH)).then_inc(stored_st, 16)
            eng.dma_start(o["n"][0, 0].rearrange("d h i -> i (d h)"), sml[:, 240:248]).then_inc(stored_st, 16)
            for i in range(36, 48):
                stage_row(i)
            take_turned(1, None)
            gate_rows_out(0)

            norm_root(1)
            high(FFN0, 0)
            take_turned(2, 2)
            high(FFN0, 1)
            eng.wait_ge(hT_a, 6)
            eng.wait_ge(hT_d, 6)
            for g in range(G):
                sc.copy(x_hi[:, :, T * g:T * g + T], hT[:, :, T * g:T * g + T]).then_inc(x_h, 1)
            for c in range(NCH):
                chunk(FFN0, c)
                if c == 0:
                    gate_rows_out(1)
            hidden_high(FFN0, NCH - 1)

            eng.wait_ge(stored_st, STATE_STORES)
            norm_root(2)
            take_turned(3, 1)
            for i in range(6):
                take_proj(15 + i, cols_of(qkv, TW * i))
            eng.wait_ge(tj_t, 21)
            eng.dma_start(o["v"][0, 0].rearrange("v s n -> s v n"),
                          qkv[:, 0, 1280:1536].rearrange("p (v n) -> p v n", v=KV)).then_inc(stored_kv, 16)
            for g in range(G):
                eng.wait_ge(q_sq, g + 1)
                sc.activation(sml[:, 24 * g:24 * g + 20], sml[:, 24 * g:24 * g + 20], ACT.Sqrt, bias=C("eps"),
                              scale=1.0 / AHD).then_inc(q_rt, 1)
            eng.wait_ge(q_ok, 1)
            eng.dma_start(o["k"][0, 0].rearrange("v s n -> s v n"),
                          qkv[:, 0, 1024:1280].rearrange("p (v n) -> p v n", v=KV)).then_inc(stored_kv, 16)
            for q in range(4):
                eng.wait_ge(at_t, q + 1)
                sc.copy(aqT[:, 4 * (q % 2):4 * (q % 2) + 4, T * (q // 2):T * (q // 2) + T],
                        bank[4 + q][:, :].rearrange("p (j n) -> p j n", j=4)).then_inc(at_ta, 1)
            gate_rows_out(2)
            for v in range(KV):
                b = 3 * (v % 2)
                eng.wait_ge(sc_m, v + 1)
                if v >= 2:
                    eng.wait_ge(pt_mm, 3 * (v - 1))
                for i in range(12):
                    part, h = i // 4, i % 4
                    at = 8 * v + 4 * (part > 0) + h
                    ins = sc.activation(Pb[v % 2][:, P * i:P * i + P], bank[b + part][:, P * h:P * h + P], ACT.Exp,
                                        bias=sml[:, 64 + at:65 + at], scale=AHD ** -0.5,
                                        accum_out=sml[:, 96 + 12 * v + i:97 + 12 * v + i])
                sc.activation(sml[:, 144 + 8 * v:152 + 8 * v], sml[:, 176 + 8 * v:184 + 8 * v], ACT.Exp
                              ).then_inc(sc_e, 1)
            take_turned(4, None)

            eng.wait_ge(stored_kv, 32)
            norm_root(3)
            take_turned(5, 3)
            eng.wait_ge(r_l, 1)
            sc.activation(rw[:, 16:32], rw[:, 16:32], ACT.Exp).then_inc(r_e, 1)
            for q in range(4):
                eng.wait_ge(hr_mm, q + 1)
                sc.copy(xn[:, q // 2, 512 * (q % 2):512 * (q % 2) + 512], bank[4 + q][:, :]).then_inc(hr_t, 1)
            gate_rows_out(3)

            def gather(n0, par, p=None, step=0):
                for q in range(2):
                    eng.wait_ge(gj, plus(p, 3 * step, 3 * n0 + q + 1))
                    sc.copy(x_hi[:, 4 * q:4 * q + 4, T * par:T * par + T],
                            bank[2 + q][:, :].rearrange("p (k n) -> p k n", k=4)).then_inc(x_h, 1)
                eng.wait_ge(gj, plus(p, 3 * step, 3 * n0 + 3))
                sc.copy(PselT[par], bank[7][:, 0:G * T]).then_inc(gj_t, 1)

            def experts(r):
                gather(GATHERS * r, 0)
                with eng.Fori(0, NE // XB) as p:
                    for i in range(XB):
                        f = expert(p, i, r)
                        if i == 0:
                            high(f, 0)
                            high(f, 1)
                        for c in range(NCH):
                            chunk(f, c)
                        if i < XB - 1:
                            high(f, NFW)
                        gather(GATHERS * r + i + 1, 1 - i % 2, p, XB)
                        hidden_high(f, NCH - 1)
                        if i < XB - 1:
                            high(f, NFW + 1)
                        eng.wait_ge(split_used, n_split(f, NFW - 1))
                        sc.copy(ys[:, 0:512], bank[4][:, :]).then_inc(y_a, 1)

            eng.wait_ge(r_ok, 1)
            experts(0)
            crowded = eng.value_load(flag[0:1, 0:1], min_val=0, max_val=1)
            with eng.If(crowded > 0):
                experts(1)
            eng.wait_ge(fin, 1)
            for g, name in enumerate(("y_prompt", "y_sample")):
                eng.dma_start(o[name][0], x[:, g, :]).then_inc(stored, 16)

        @block.vector
        def _(eng):
            v_ = nc.vector
            n_chain = [0]

            def link(ins):
                n_chain[0] += 1
                ins.then_inc(dve, 1)
                eng.wait_ge(dve, n_chain[0])

            def bc(ap, n):
                return ap.unsqueeze(len(ap.shape)).to_broadcast([*ap.shape, n])

            link(v_.memset(mlx[:], 0.0))

            def range_reduce(n):
                s = sinb[0:64, :, :]
                link(v_.tensor_scalar(s[:, 1, :], s[:, 0, :], 1.0 / TWO_PI, RND, ALU.mult, ALU.add))
                link(v_.tensor_scalar(s[:, 1, :], s[:, 1, :], RND, None, ALU.subtract))
                c1 = float(np.float32(6.28125))
                c2 = float(np.float32(1.9350051879882812e-03))
                c3 = float(TWO_PI - 6.28125 - 1.9350051879882812e-03)
                link(v_.scalar_tensor_tensor(s[:, 2, :], s[:, 1, :], -c1, s[:, 0, :], ALU.mult, ALU.add))
                link(v_.scalar_tensor_tensor(s[:, 0, :], s[:, 1, :], -c2, s[:, 2, :], ALU.mult, ALU.add))
                link(v_.scalar_tensor_tensor(s[:, 2, :], s[:, 1, :], -c3, s[:, 0, :], ALU.mult, ALU.add))
                v_.tensor_scalar(s[:, 3, :], s[:, 2, :], -3.1415925, 3.1415925, ALU.max, ALU.min).then_inc(f_arg, 1)

            eng.wait_ge(ld_h, 16 * 6)
            for n in range(2):
                eng.wait_ge(f_mm, n + 1)
                if n:
                    eng.wait_ge(f_sin, n)
                link(v_.tensor_scalar(sinb[0:64, 0, :], bank[3][0:64, P * n:P * n + P], hyp[:, 64 + n:65 + n],
                                      hyp[:, 66 + n:67 + n], ALU.add, ALU.mult))
                range_reduce(n)
            eng.wait_ge(f_mm, 3)
            for q in range(4):
                ins = v_.tensor_tensor(taps[:, q, :], bank[4 + q][:, :], C("decay"), ALU.mult)
            ins.then_inc(f_tap, 1)
            link(v_.memset(rowq[:, 4:8, :], 0.0))
            eng.wait_ge(ld_h2, 16)
            for r in range(2):
                eng.wait_ge(f_mm, 4 + r)
                link(v_.reciprocal(Gb[:, 1, 512 * r:512 * r + 512], bank[6 + r][:, :]))
                for d in range(NDIR):
                    link(v_.tensor_tensor(taps[:, 2 * r + d, :], taps[:, 2 * r + d, :],
                                          Gb[:, 1, 512 * r:512 * r + 512], ALU.mult))
                v_.tensor_tensor(taps[0:1, 2 * r, :], taps[0:1, 2 * r, :], skip[:, 512 * r:512 * r + 512], ALU.add
                                 ).then_inc(f_nrm, 1)

            def mod_columns(l):
                eng.wait_ge(ld_a, 48)
                eng.wait_ge(ada_col, 24 * (l + 1))
                link(v_.tensor_tensor(modc[:, l].rearrange("p a k g -> p (a k) g"),
                                      bank[2][:, P * l:P * l + 96].rearrange("p (m g) -> p m g", g=G),
                                      bc(modb[:, l, :], G), ALU.add))
                for i in range(2):
                    ins = v_.scalar_tensor_tensor(sca[:, l + 2 * i], modc[:, l, 1 + 3 * i], 1.0,
                                                  bc(ngc[:, l + 2 * i, :], G), ALU.add, ALU.mult)
                ins.then_inc(modc_ok, 1)

            def norm_rows(i):
                eng.wait_ge(n_rt, i + 1)
                link(v_.reciprocal(rstd[:, 2 * i:2 * i + 2], rt[:, 2 * i:2 * i + 2]))
                for g in range(G):
                    v_.tensor_scalar(xn[:, g, :], x[:, g, :], rstd[:, 2 * i + g:2 * i + g + 1], None, ALU.mult
                                     ).then_inc(rows_ok, 1)

            def take_turned(s, norm):
                for half in range(2):
                    eng.wait_ge(turned, 4 * s + 2 + half + 1)
                    if norm is None:
                        ins = v_.tensor_copy(hT[:, 4 * half:4 * half + 4, T:2 * T],
                                             bank[6 + half][:, :].rearrange("p (j n) -> p j n", j=4))
                    else:
                        if half == 0:
                            eng.wait_ge(modc_ok, norm % 2 + 1)
                        l, part = norm % 2, 3 * (norm // 2)
                        for j in range(4):
                            k = 4 * half + j
                            ins = v_.tensor_scalar(hT[:, k, T:2 * T], bank[6 + half][:, P * j:P * j + P],
                                                   sca[:, norm, k, 1:2], modc[:, l, part, k, 1:2],
                                                   ALU.mult, ALU.add)
                    ins.then_inc(hT_d, 1)

            def gate_source(s):
                l, part = s // 2, 2 + 3 * (s % 2)
                for g in range(G):
                    ins = v_.tensor_copy(Gb[:, g, :].rearrange("p (k n) -> p k n", k=KD),
                                         bc(modc[:, l, part, :, g], P))
                ins.then_inc(gbs, 1)

            def add_projection(n0, s):
                eng.wait_ge(gbt, 4 * (s + 1))
                for i in range(4):
                    n = n0 + i
                    eng.wait_ge(tile_used, (WOUT if s == 0 else AOUT) + i + 1)
                    t_ = tmpr[:, n % 2].rearrange("p (g n) -> p g n", g=G)
                    c = slice(TW * i, TW * i + TW)
                    n_chain[0] += 1
                    v_.tensor_tensor(t_, bank[n % 2][:, :].rearrange("p (g n) -> p g n", g=G), Gb[:, :, c],
                                     ALU.mult).then_inc(dve, 1)
                    eng.wait_ge(dve, n_chain[0])
                    v_.tensor_tensor(x[:, :, c], x[:, :, c], t_, ALU.add).then_inc(ro_t, 1)
                eng.wait_ge(ro_t, n0 + 4)
                eng.sem_inc(resid, 1)

            mod_columns(0)
            norm_rows(0)
            take_turned(0, 0)

            eng.wait_ge(turned, 4)
            for d in range(NDIR):
                v_.tensor_copy(selr[:, 8 * d:8 * d + 8, :], bc(ident[0:ROWS, 32 * d:32 * d + 8], P)
                               ).then_inc(sel_ok, 1)
            eng.wait_ge(ld_g, 16 * 6)
            eng.wait_ge(g_rows, 1)
            v_.tensor_scalar(rowq[:, 0, :], bank[4][0:ROWS, 0:P], gb[:, 0:1], None, ALU.add)
            v_.tensor_scalar(rowq[:, 1, :], bank[4][0:ROWS, P:2 * P], gb[:, 1:2], None, ALU.add).then_inc(g_in, 1)
            eng.wait_ge(g_f, 1)
            link(v_.scalar_tensor_tensor(rowq[:, 2, :], rowq[:, 1, :], 0.0, rowq[:, 8, :], ALU.min, ALU.subtract))
            fwd, bwd = slice(0, 8), slice(32, 40)
            v_.tensor_tensor_scan(rowq[fwd, 4, :], ones[fwd, :], rowq[fwd, 2, :], 0.0, ALU.mult, ALU.add)
            link(v_.tensor_tensor_scan(rowq[bwd, 4, ::-1], ones[bwd, :], rowq[bwd, 2, ::-1], 0.0, ALU.mult, ALU.add))
            link(v_.tensor_tensor(rowq[:, 5, :], rowq[:, 0, :], rowq[:, 4, :], ALU.subtract))
            v_.tensor_tensor_scan(rowq[fwd, 6, :], ones[fwd, :], rowq[fwd, 5, :], m0[fwd, 0:1], ALU.mult, ALU.max)
            link(v_.tensor_tensor_scan(rowq[bwd, 6, ::-1], ones[bwd, :], rowq[bwd, 5, ::-1], m0[bwd, 0:1],
                                       ALU.mult, ALU.max))
            link(v_.tensor_tensor(rowq[:, 7, :], rowq[:, 4, :], rowq[:, 6, :], ALU.add))
            v_.tensor_copy(mlx[fwd, 0:1], rowq[fwd, 7, P - 1:P])
            v_.tensor_copy(mlx[bwd, 0:1], rowq[bwd, 7, 0:1])
            v_.tensor_scalar(mlx[fwd, 1:2], rowq[fwd, 6, P - 1:P], -1.0, None, ALU.mult)
            v_.tensor_scalar(mlx[bwd, 1:2], rowq[bwd, 6, 0:1], -1.0, None, ALU.mult)
            v_.tensor_scalar(rowq[:, 8, :], rowq[:, 6, :], -1.0, None, ALU.mult).then_inc(g_mu, 1)
            eng.wait_ge(g_col, 1)
            v_.tensor_copy(cols[:, :, 0:ROWS], bank[3][:, 0:256].rearrange("p (i n) -> p i n", i=4)[:, :, 0:ROWS]
                           ).then_inc(g_colt, 1)

            eng.wait_ge(ld_cw, 16)

            def conv_taps(c):
                w, g = c // 2, c % 2
                uc = u[:, g, HW * w:HW * w + HW]
                eng.wait_ge(tj_t, 9 + 2 * w + 2)
                if c >= 2:
                    eng.wait_ge(cv_mm, c - 1)
                for i in range(2):
                    ins = v_.tensor_tensor(hyT[0][:, 2 * (c % 2) + i, :], uc, convw[:, 2 * i, HW * w:HW * w + HW],
                                           ALU.mult)
                ins.then_inc(cw_ok, 1)
                eng.wait_ge(cw_ok, c + 1)
                link(v_.tensor_tensor(uc, uc, convw[:, 1, HW * w:HW * w + HW], ALU.mult))

            def conv_sum(c):
                w, g = c // 2, c % 2
                uc = u[:, g, HW * w:HW * w + HW]
                eng.wait_ge(cv_mm, c + 1)
                v_.tensor_tensor(uc, uc, bank[1][:, :], ALU.add).then_inc(cv_ok, 1)

            for c in range(6):
                conv_taps(c)
                if c:
                    conv_sum(c - 1)
            conv_sum(5)

            for q in range(4):
                g = q % 2
                eng.wait_ge(wt_ok, q + 1)
                eng.wait_ge(qk_ok, 2)
                v_.scalar_tensor_tensor(ST[:, 4 * q:4 * q + 4, :],
                                        bank[6 + g][:, :].rearrange("p (h n) -> p h n", h=NH), HD ** -0.5,
                                        WT[:, 4 * q:4 * q + 4, :], ALU.mult, ALU.mult).then_inc(st_ok, 1)
            den, rd, tiny = sml[:, 0:4], sml[:, 4:8], sml[:, 8:12]

            def heads(ap):
                return ap.rearrange("p (h n) -> p h n", h=NH)

            T0, T1 = heads(hyT[0][:, 0, :]), heads(hyT[0][:, 1, :])
            for q in range(4):
                d, g = q // 2, q % 2
                r = 32 * d + 4 * g
                w_inter, floor = cols[:, 1, r:r + 4], cols[:, 2, r:r + 4]
                eng.wait_ge(nu_ok, q + 1)
                pden = bank[1 if g else 3][:, 256 + 4 * q:260 + 4 * q]
                if g:
                    link(v_.tensor_tensor(tiny, bank[1][:, 272 + 4 * d:276 + 4 * d], w_inter, ALU.mult))
                    link(v_.tensor_tensor(den, pden, tiny, ALU.add))
                    pden = den
                link(v_.scalar_tensor_tensor(tiny, pden, -1.0, floor, ALU.mult, ALU.max))
                link(v_.tensor_tensor(den, pden, tiny, ALU.max))
                link(v_.reciprocal(rd, den))
                num = heads(bank[4 + q % 2][:, :])
                hs = heads(xn[:, g, HW:2 * HW])
                dst = T1 if d else hs
                if g:
                    link(v_.tensor_tensor(T0, heads(bank[6 + d][:, :]), bc(w_inter, HD), ALU.mult))
                    link(v_.tensor_tensor(T0, T0, num, ALU.add))
                    link(v_.tensor_tensor(dst, T0, bc(rd, HD), ALU.mult))
                else:
                    link(v_.tensor_tensor(dst, num, bc(rd, HD), ALU.mult))
                eng.sem_inc(nu_t, 1)
                if d:
                    link(v_.tensor_tensor(hs, hs, T1, ALU.add))
            eng.wait_ge(kr_ok, 1)
            for d in range(NDIR):
                ins = v_.scalar_tensor_tensor(kw[:, d], heads(bank[6][:, :]), HD ** -0.5,
                                              bc(cols[:, 3, 32 * d:32 * d + 4], HD), ALU.mult, ALU.mult)
            ins.then_inc(kw_ok, 1)
            hall = xn[:, :, HW:2 * HW]
            sq = hyT[0][:, 0:2, :]
            link(v_.tensor_tensor(sq, hall, hall, ALU.mult))
            v_.tensor_reduce(sml[:, 32:40], sq.rearrange("p g (h n) -> p (g h) n", h=NH), AX, ALU.add
                             ).then_inc(hs_q, 1)
            eng.wait_ge(ld_mg, 16)
            link(v_.tensor_tensor(sigo, sigo, mgain.unsqueeze(1).to_broadcast([P, G, HW]), ALU.mult))
            link(v_.tensor_tensor(hall, hall, sigo, ALU.mult))
            eng.wait_ge(hs_r, 1)
            link(v_.reciprocal(sml[:, 48:56], sml[:, 40:48]))
            for g in range(G):
                hg = heads(xn[:, g, HW:2 * HW])
                link(v_.tensor_tensor(hg, hg, bc(sml[:, 48 + 4 * g:52 + 4 * g], HD), ALU.mult))

            eng.wait_ge(cs_ok, 2)
            for r in range(2):
                A, B, Dd = spec[:, r, 0, :], spec[:, r, 1, :], spec[:, r, 2, :]
                for g in range(G):
                    n = 2 * r + g
                    eng.wait_ge(fz_mm, n + 1)
                    if n >= 2:
                        eng.wait_ge(iz_mm, n - 1)
                    Pz, Qz, t_ = bank[4 + 2 * g], bank[5 + 2 * g], hyT[g]
                    v_.tensor_tensor(t_[:, 0, :], Pz[:, :], A, ALU.mult)
                    v_.tensor_tensor(t_[:, 1, :], Qz[:, :], B, ALU.mult)
                    v_.tensor_tensor(t_[:, 2, :], Pz[:, :], B, ALU.mult)
                    link(v_.tensor_tensor(t_[:, 3, :], Qz[:, :], Dd, ALU.mult))
                    v_.tensor_tensor(t_[:, 0, :], t_[:, 0, :], t_[:, 1, :], ALU.subtract)
                    v_.tensor_tensor(t_[:, 2, :], t_[:, 2, :], t_[:, 3, :], ALU.add).then_inc(fz_ok, 1)
                for g in range(G):
                    eng.wait_ge(iz_mm, 2 * r + g + 1)
                    dst = xn[:, g, 0:HW] if r else u[:, g, 0:HW]
                    v_.tensor_tensor(dst, u[:, g, HW * (1 + r):HW * (2 + r)], bank[1 + 2 * g][:, :], ALU.mult
                                     ).then_inc(iz_ok, 1)
            eng.wait_ge(iz_ok, 4)
            for g in range(G):
                eng.sem_inc(rows_ok, 1)
            take_turned(1, None)
            eng.wait_ge(iz_mm, 4)
            gate_source(0)
            add_projection(0, 0)
            mod_columns(1)

            def low(f, i):
                s, _ = late_at(f[4] + i)
                n = (f[3] + i) % SPL
                eng.wait_ge(hi_ok, n_split(f, i))
                v_.tensor_tensor(w_lo[:, n, :], raw[:, s, :], w_hi[:, n, :].bitcast(F32), ALU.subtract
                                 ).then_inc(lo_ok, 1)

            def gated(f, c):
                for g in range(f[0]):
                    b, up, _ = unit_at(f, c, g)
                    eng.wait_ge(h_sa, n_unit(f, c, g))
                    v_.tensor_tensor(grow[b], sa[b], up[:, TW:2 * TW], ALU.mult).then_inc(h_g, 1)

            def hidden_low(f, c):
                for g in range(f[0]):
                    b, _, turn = unit_at(f, c, g)
                    eng.wait_ge(gh_ok, n_unit(f, c, g))
                    v_.tensor_tensor(g_lo[:, b, :], turn[:, 0:TW], g_hi[:, b, :].bitcast(F32), ALU.subtract
                                     ).then_inc(gl_ok, 1)

            def chunk(f, c):
                if c:
                    hidden_low(f, c - 1)
                low(f, at_a(c + 1) if c < NCH - 1 else at_w(c))
                gated(f, c)
                if c < NCH - 1:
                    low(f, at_b(c + 1))
                    low(f, at_w(c))

            norm_rows(1)
            low(FFN0, 0)
            take_turned(2, 2)
            for g in range(G):
                eng.wait_ge(x_h, g + 1)
                v_.tensor_tensor(x_lo[:, :, T * g:T * g + T], hT[:, :, T * g:T * g + T],
                                 x_hi[:, :, T * g:T * g + T].bitcast(F32), ALU.subtract).then_inc(x_l, 1)
            low(FFN0, 1)
            gate_source(1)
            for c in range(NCH):
                chunk(FFN0, c)
            hidden_low(FFN0, NCH - 1)
            eng.wait_ge(split_used, NFW)
            eng.wait_ge(gbt, 8)
            for q in range(4):
                g, c = q // 2, slice(512 * (q % 2), 512 * (q % 2) + 512)
                link(v_.tensor_tensor(tmpf[:, q % 2, :], bank[4 + q][:, :], Gb[:, g, c], ALU.mult))
                link(v_.tensor_tensor(x[:, g, c], x[:, g, c], tmpf[:, q % 2, :], ALU.add))
            eng.sem_inc(resid, 1)

            norm_rows(2)
            take_turned(3, 1)
            gate_source(2)
            eng.wait_ge(ld_at, 16 * 6)
            eng.wait_ge(tj_t, 21)
            wide = ar(3072, 1280)
            for g in range(G):
                qk = qkv[:, g, 0:1280]
                link(v_.tensor_tensor(wide, qk, qk, ALU.mult))
                v_.tensor_reduce(sml[:, 24 * g:24 * g + 20], wide.rearrange("p (h n) -> p h n", n=AHD), AX, ALU.add
                                 ).then_inc(q_sq, 1)
                eng.wait_ge(q_sq, g + 1)
            for g in range(G):
                qk = qkv[:, g, 0:1280].rearrange("p (h n) -> p h n", n=AHD)
                eng.wait_ge(q_rt, g + 1)
                link(v_.reciprocal(sml[:, 24 * g:24 * g + 20], sml[:, 24 * g:24 * g + 20]))
                link(v_.tensor_tensor(qk, qk, bc(sml[:, 24 * g:24 * g + 20], AHD), ALU.mult))
                v_.tensor_tensor(qk[:, 0:QH, :], qk[:, 0:QH, :],
                                 qkg[:, 0:64].unsqueeze(1).to_broadcast([P, QH, AHD]), ALU.mult)
                link(v_.tensor_tensor(qk[:, QH:, :], qk[:, QH:, :],
                                      qkg[:, 64:128].unsqueeze(1).to_broadcast([P, KV, AHD]), ALU.mult))
                if g:
                    half = qkv[:, 1, 0:1280].rearrange("p (h a b n) -> p h a b n", a=2, b=2, n=16)
                    a1, a2 = half[:, :, :, 0, :], half[:, :, :, 1, :]
                    cos, sin = (C(n).rearrange("p (a n) -> p a n", a=2).unsqueeze(1).to_broadcast([P, 20, 2, 16])
                                for n in ("cos", "sin"))
                    tt = [rtmp[:, i, :].rearrange("p (h a n) -> p h a n", a=2, n=16) for i in range(4)]
                    v_.tensor_tensor(tt[0], a1, cos, ALU.mult)
                    v_.tensor_tensor(tt[1], a2, sin, ALU.mult)
                    v_.tensor_tensor(tt[2], a1, sin, ALU.mult)
                    link(v_.tensor_tensor(tt[3], a2, cos, ALU.mult))
                    v_.tensor_tensor(a1, tt[0], tt[1], ALU.subtract)
                    link(v_.tensor_tensor(a2, tt[2], tt[3], ALU.add))
                eng.sem_inc(q_ok, 1)
            for d in range(2):
                ins = v_.tensor_copy(kd[:, :, :, d, :],
                                     qkv[:, :, 1024:1280].rearrange("p g (v n) -> p g v n", v=KV))
            ins.then_inc(k_dup, 1)
            for odd in range(2):
                other = slice(0, 64) if odd else slice(64, 128)
                v_.memset(akT[odd][other], 0.0)
                v_.memset(ckT[odd][other], 0.0)
            for q in range(3):
                eng.wait_ge(at_t, 4 + q + 1)
                for odd in range(2):
                    half = slice(64 * odd, 64 * odd + 64)
                    src = bank[q][half, :].rearrange("p (v n) -> p v n", v=KV)
                    dst = akT[odd][half, :, T * q:T * q + T] if q < 2 else ckT[odd][half]
                    ins = v_.tensor_copy(dst, src)
                ins.then_inc(at_td, 1)

            def maxima(v):
                b = 3 * (v % 2)
                eng.wait_ge(sc_mm, v + 1)
                mx = sml[:, 208:220]
                for part in range(3):
                    ins = v_.tensor_reduce(mx[:, 4 * part:4 * part + 4],
                                           bank[b + part][:, :].rearrange("p (h n) -> p h n", h=4), AX, ALU.max)
                link(ins)
                link(v_.tensor_tensor(mx[:, 4:8], mx[:, 4:8], mx[:, 8:12], ALU.max))
                s4 = sinkb[:, 4 * v:4 * v + 4].unsqueeze(1).to_broadcast([P, 2, 4])
                m8 = mx[:, 0:8].rearrange("p (g h) -> p g h", g=2)
                neg = sml[:, 64 + 8 * v:72 + 8 * v]
                link(v_.scalar_tensor_tensor(m8, m8, AHD ** -0.5, s4, ALU.mult, ALU.max))
                link(v_.tensor_scalar(neg, mx[:, 0:8], -1.0, None, ALU.mult))
                link(v_.tensor_tensor(sml[:, 176 + 8 * v:184 + 8 * v].rearrange("p (g h) -> p g h", g=2),
                                      neg.rearrange("p (g h) -> p g h", g=2), s4, ALU.add))
                eng.sem_inc(sc_m, 1)

            def values(v):
                b = 3 * (v % 2)
                for q in range(3):
                    n = 3 * v + q
                    eng.wait_ge(pt_mm, n + 1)
                    if v >= 2 and q == 0:
                        eng.wait_ge(pv_mm, v - 1)
                    v_.tensor_copy(PTb[v % 2][:, 512 * q:512 * q + 512], bank[6 + n % 2][:, :]).then_inc(pt_t, 1)
                sums, sk = sml[:, 96 + 12 * v:108 + 12 * v], sml[:, 144 + 8 * v:152 + 8 * v]
                link(v_.tensor_tensor(sk, sk, sums[:, 0:8], ALU.add))
                link(v_.tensor_tensor(sk[:, 4:8], sk[:, 4:8], sums[:, 8:12], ALU.add))
                link(v_.reciprocal(sk, sk))
                eng.wait_ge(pv_mm, v + 1)
                for g in range(G):
                    ins = v_.tensor_tensor(xn[:, g, TW * v:TW * v + TW].rearrange("p (h n) -> p h n", h=4),
                                           bank[b][:, TW * g:TW * g + TW].rearrange("p (h n) -> p h n", h=4),
                                           bc(sk[:, 4 * g:4 * g + 4], AHD), ALU.mult)
                ins.then_inc(pv_t, 1)

            maxima(0)
            for v in range(KV):
                if v + 1 < KV:
                    maxima(v + 1)
                values(v)
            eng.wait_ge(pv_t, KV)
            for g in range(G):
                eng.sem_inc(rows_ok, 1)
            take_turned(4, None)
            add_projection(4, 2)

            norm_rows(3)
            take_turned(5, 3)
            L, E = rw[:, 0:16].rearrange("p (g e) -> p g e", g=G), rw[:, 16:32].rearrange("p (g e) -> p g e", g=G)
            sel = rw[:, 32:48].rearrange("p (g e) -> p g e", g=G)
            rank = rw[:, 48:64].rearrange("p (g e) -> p g e", g=G)
            top, dsum = rw[:, 64:66], rw[:, 66:68]
            gates = rw[:, 68:88].rearrange("p (g e) -> p g e", g=G)
            place = rw[:, 88:108].rearrange("p (g e) -> p g e", g=G)
            cnt = rw[:, 108:110]
            cmp1 = rw[:, 128:256].rearrange("p (g i j) -> p g i j", g=G, i=NE)
            cmp2 = rw[:, 256:384].rearrange("p (g i j) -> p g i j", g=G, i=NE)
            eng.wait_ge(ld_r, 32)
            eng.wait_ge(r_mm, 1)
            link(v_.tensor_tensor(L, bank[0][:, 0:16].rearrange("p (g e) -> p g e", g=G),
                                  msm[:, 64:72].unsqueeze(1).to_broadcast([P, G, NE]), ALU.add))
            link(v_.tensor_reduce(top, L, AX, ALU.max))
            v_.tensor_tensor(E, L, bc(top, NE), ALU.subtract).then_inc(r_l, 1)
            for g in range(G):
                Li = L[:, g, :].unsqueeze(2).to_broadcast([P, NE, NE])
                Lj = L[:, g, :].unsqueeze(1).to_broadcast([P, NE, NE])
                v_.tensor_tensor(cmp1[:, g], Lj, Li, ALU.is_gt)
                link(v_.tensor_tensor(cmp2[:, g], Lj, Li, ALU.is_equal))
                link(v_.tensor_tensor(cmp2[:, g], cmp2[:, g], C("tri").rearrange("p (i j) -> p i j", i=NE), ALU.mult))
                link(v_.tensor_tensor(cmp1[:, g], cmp1[:, g], cmp2[:, g], ALU.add))
            link(v_.tensor_reduce(rank, cmp1, AX, ALU.add))
            link(v_.tensor_scalar(sel, rank, 1.5, None, ALU.is_lt))
            v_.memset(gates, 0.0)
            link(v_.memset(place, -1.0))
            eng.sem_inc(r_sel, 1)
            eng.wait_ge(r_e, 1)
            link(v_.tensor_tensor(E, E, sel, ALU.mult))
            link(v_.tensor_reduce(dsum, E, AX, ALU.add))
            link(v_.reciprocal(dsum, dsum))
            link(v_.tensor_tensor(gates[:, :, 1:9], E, bc(dsum, NE), ALU.mult))
            eng.wait_ge(r_pos, 1)
            link(v_.tensor_tensor(place[:, :, 1:9], bank[1][:, 0:16].rearrange("p (g e) -> p g e", g=G), sel, ALU.mult))
            link(v_.tensor_scalar(place[:, :, 1:9], place[:, :, 1:9], 1.0, None, ALU.subtract))
            link(v_.tensor_reduce(cnt[:, 0:1], bank[1][:, 16:24], AX, ALU.max))
            link(v_.tensor_scalar(cnt[:, 1:2], cnt[:, 0:1], float(P) + 0.5, None, ALU.is_gt))
            link(v_.tensor_copy(flag[0:1, 0:1], cnt[0:1, 1:2]))
            v_.memset(acc, 0.0)
            v_.memset(ys, 0.0)
            link(v_.memset(PselT[1], 0.0))
            eng.sem_inc(y_a, 1)
            eng.sem_inc(y_d, 1)
            eng.sem_inc(r_ok, 1)
            eng.wait_ge(hr_t, 4)
            gate_source(3)

            def selector(par, r, e):
                for g in range(G):
                    ins = v_.tensor_scalar(Psel[par][:, g, :], C("iota")[:, P * r:P * r + P],
                                           place[:, g, bass.ds(e + 1, 1)], None, ALU.is_equal)
                ins.then_inc(p_ok, 1)

            def gather(n0, par, p=None, step=0):
                for q in range(2):
                    eng.wait_ge(x_h, plus(p, 2 * step, G + 2 * n0 + q + 1))
                    dst = slice(4 * q, 4 * q + 4), slice(T * par, T * par + T)
                    v_.tensor_tensor(x_lo[:, dst[0], dst[1]], bank[2 + q][:, :].rearrange("p (k n) -> p k n", k=4),
                                     x_hi[:, dst[0], dst[1]].bitcast(F32), ALU.subtract).then_inc(x_l, 1)

            def combined(n0, p, step, e, h):
                for q in (2 * h, 2 * h + 1):
                    c = slice(512 * (q % 2), 512 * (q % 2) + 512)
                    eng.wait_ge(cb, plus(p, 4 * step, 4 * n0 + q + 1))
                    v_.scalar_tensor_tensor(acc[:, h, c], bank[2 + q % 2][:, :], gates[:, h, bass.ds(e, 1)],
                                            acc[:, h, c], ALU.mult, ALU.add).then_inc(cb_t, 1)

            def experts(r):
                if r:
                    eng.wait_ge(gj, 3 * GATHERS * r)
                selector(0, r, 0)
                gather(GATHERS * r, 0)
                with eng.Fori(0, NE // XB) as p:
                    for i in range(XB):
                        f = expert(p, i, r)
                        if i == 0:
                            low(f, 0)
                            low(f, 1)
                        for c in range(NCH):
                            chunk(f, c)
                            if c in (1, 3):
                                combined(GATHERS * r + i, p, XB, p * XB + i, c // 2)
                            if c == 6:
                                eng.wait_ge(gj, p * (3 * XB) + 3 * (GATHERS * r + i + 1))
                                selector(1 - i % 2, r, p * XB + (i + 1))
                        if i < XB - 1:
                            low(f, NFW)
                        gather(GATHERS * r + i + 1, 1 - i % 2, p, XB)
                        hidden_low(f, NCH - 1)
                        if i < XB - 1:
                            low(f, NFW + 1)
                        eng.wait_ge(split_used, n_split(f, NFW - 1))
                        v_.tensor_copy(ys[:, 512:1024], bank[5][:, :]).then_inc(y_d, 1)
                for h in range(G):
                    combined(GATHERS * r + NE, None, 0, NE, h)

            experts(0)
            crowded = eng.value_load(flag[0:1, 0:1], min_val=0, max_val=1)
            with eng.If(crowded > 0):
                experts(1)
            eng.wait_ge(gbt, 16)
            eng.wait_ge(cb_t, 4 * GATHERS)
            for q in range(4):
                g, c = q // 2, slice(512 * (q % 2), 512 * (q % 2) + 512)
                link(v_.tensor_tensor(acc[:, g, c], acc[:, g, c], Gb[:, g, c], ALU.mult))
                link(v_.tensor_tensor(x[:, g, c], x[:, g, c], acc[:, g, c], ALU.add))
            eng.sem_inc(fin, 1)

        @block.tensor
        def _(eng):
            pe = nc.tensor

            def landed(n):
                _, filled, count = place_of(n)
                eng.wait_ge(filled, count)

            def mm(out, lhsT, rhs, start, stop):
                return pe.matmul(out, lhsT, rhs, start=start, stop=stop)

            def ada_main(i):
                n = i if i < 24 else ADA1 + i - 24
                landed(n)
                if i >= 24:
                    eng.wait_ge(ada_stg, i)
                elif i >= 2:
                    eng.wait_ge(ada_stg, i - 1)
                for k in range(KD):
                    ins = mm(bank[ada_bank(i)][0:2, 0:TW], condT[:, k, :], tile(n)[:, k, :],
                             k == 0, k == KD - 1)
                ins.then_inc(tile_used, 1)

            def ada_cols(i):
                l, at = i // 24, i % 24
                eng.wait_ge(ada_stg, i + 1)
                for j in range(2):
                    c = P * l + 2 * (2 * at + j)
                    ins = mm(bank[2][:, c:c + 2], stage[0:2, i % 2, P * j:P * j + P], ident[0:2, 0:2], True, True)
                ins.then_inc(ada_col, 1)

            eng.wait_ge(cond_ok, 1)
            for i in range(24):
                ada_main(i)
                if i == 0:
                    eng.wait_ge(ld_k, 16)
                else:
                    ada_cols(i - 1)
                if i == 3:
                    eng.wait_ge(ld_h, 16 * 6)
                    mm(bank[3][0:64, 0:P], hyw1[:], C("zt", 33), True, True).then_inc(f_mm, 1)
                if i == 7:
                    eng.wait_ge(f_sin, 1)
                    mm(bank[3][0:64, P:2 * P], hyp[:, 0:64], sinb[0:64, 4, :], True, True).then_inc(f_mm, 1)
                if i == 11:
                    eng.wait_ge(f_sin, 2)
                    for q in range(4):
                        ins = mm(bank[4 + q][:, :], sinb[0:64, 5, :], hyhw3[:, HW * q:HW * q + HW], True, True)
                    ins.then_inc(f_mm, 1)
                if i == 15:
                    eng.wait_ge(f_abs, 1)
                    eng.wait_ge(pz, 4)
                    for r in range(2):
                        mm(bank[6 + r][:, :], ones[:, :], mags[:, 2 * r, :], True, False)
                        mm(bank[6 + r][:, :], ones[:, :], mags[:, 2 * r + 1, :], False, True).then_inc(f_mm, 1)
                if i >= 18:
                    q = i - 18
                    r, k = q // 3, q % 3
                    eng.wait_ge(f_nrm, r + 1)
                    if q >= 2:
                        eng.wait_ge(f_spt, q - 1)
                    mm(bank[4 + q % 2][:, :], C(("fc", "fs0", "fd")[k]), taps[:, 2 * r, :], True, False)
                    mm(bank[4 + q % 2][:, :], C(("gc", "gs0", "gd")[k]), taps[:, 2 * r + 1, :], False, True
                       ).then_inc(f_spec, 1)
            ada_cols(23)

            def turn_rows(s):
                for q in range(4):
                    g, half = q // 2, q % 2
                    if half == 0:
                        eng.wait_ge(rows_ok, 2 * s + g + 1)
                    for j in range(4):
                        c = 512 * half + P * j
                        ins = pe.transpose(bank[4 + q][:, P * j:P * j + P], xn[:, g, c:c + P], ident)
                    ins.then_inc(turned, 1)

            def wait_hT(s):
                eng.wait_ge(hT_a, 2 * (s + 1))
                eng.wait_ge(hT_d, 2 * (s + 1))

            def rows_of(dst, n, width=TW, k8=None):
                for g in range(G):
                    for k in range(KD):
                        w = tile(n)[:, k, :] if k8 is None else k8[:, k, :]
                        ins = mm(dst[:, width * g:width * g + width], hT[:, k, T * g:T * g + T], w, k == 0, k == KD - 1)
                return ins

            def proj(j, n, kind):
                landed(n)
                if j >= 3:
                    eng.wait_ge(tj_t, j - 2)
                b = bank[j % 3]
                if kind == "cols":
                    for h in range(2):
                        for k in range(KD):
                            ins = mm(b[:, TW * h:TW * h + TW], tile(n)[:, k, P * h:P * h + P], hT[:, k, :],
                                     k == 0, k == KD - 1)
                elif kind == "gates":
                    ins = rows_of(b, n, 16, place_of(n)[0][:, 0:128].rearrange("p (k n) -> p k n", k=KD))
                else:
                    ins = rows_of(b, n)
                ins.then_inc(tile_used, 1)

            eng.wait_ge(f_spt, 6)
            turn_rows(0)
            eng.wait_ge(modc_ok, 1)
            wait_hT(0)
            kinds = ["gates"] + ["cols"] * 4 + ["rows"] * 10

            def ip(j):
                proj(j, IN0 + j, kinds[j])

            ip(0)
            ip(1)
            ip(2)
            eng.wait_ge(tj_t, 1)
            for f in range(2):
                for g in range(G):
                    ins = mm(bank[4][0:ROWS, P * f:P * f + P], gzero[:, f, g, :], ident, g == 0, g == 1)
            ins.then_inc(g_rows, 1)
            ip(3)
            ip(4)
            ip(5)
            eng.wait_ge(tj_t, 5)
            for g in range(G):
                for h in range(NH):
                    ins = mm(bank[6 + g][:, P * h:P * h + P], kT[:, h, T * g:T * g + T], qT[:, h, T * g:T * g + T],
                             True, True)
                ins.then_inc(qk_ok, 1)
            ip(6)
            ip(7)
            eng.wait_ge(g_ex, 1)
            for i, r in enumerate((5, 9, 10, 11)):
                ins = mm(bank[3][:, 64 * i:64 * i + ROWS], rowq[:, r, :], ident[0:ROWS, 0:ROWS], True, True)
            ins.then_inc(g_col, 1)
            for j in range(8, 15):
                ip(j)

            def fill(i):
                if i == 24:
                    eng.wait_ge(tj_t, 15)
                    eng.wait_ge(modc_ok, 1)
                ada_main(i)
                if i > 24:
                    ada_cols(i - 1)

            eng.wait_ge(tj_t, 15)
            for c in range(6):
                eng.wait_ge(cw_ok, c + 1)
                if c:
                    eng.wait_ge(cv_ok, c)
                for i in range(2):
                    ins = mm(bank[1][:, :], C("shift")[:, P * i:P * i + P], hyT[0][:, 2 * (c % 2) + i, :],
                             i == 0, i == 1)
                ins.then_inc(cv_mm, 1)
                fill(24 + c)
            eng.wait_ge(sel_ok, 2)
            eng.wait_ge(g_mu, 1)
            for q in range(4):
                if q >= 2:
                    eng.wait_ge(wt_ok, q - 1)
                d, g = q // 2, q % 2
                for h in range(NH):
                    out = bank[4 + q % 2][:, P * h:P * h + P]
                    mm(out, selr[:, 8 * d + 4 * g + h, :], rowq[:, 8, :], True, False)
                    ins = mm(out, ident, C("mask")[:, P * d:P * d + P], False, True)
                ins.then_inc(wt_mm, 1)
                if q % 2:
                    fill(30 + q // 2)
            eng.wait_ge(ld_n, 32)
            eng.wait_ge(ld_C, 16)
            for q in range(4):
                d, g = q // 2, q % 2
                eng.wait_ge(st_ok, 4)
                if q >= 2:
                    eng.wait_ge(nu_t, q - 1)
                for h in range(NH):
                    s_, v = ST[:, 4 * q + h, :], vrow[:, g, P * h:P * h + P]
                    mm(bank[4 + q % 2][:, P * h:P * h + P], s_, v, True, True)
                    ins = mm(bank[1 if g else 3][:, 256 + 4 * q + h:257 + 4 * q + h], s_, ones[:, 0:1], True, True)
                    if g:
                        qt = qT[:, h, T:2 * T]
                        mm(bank[6 + d][:, P * h:P * h + P], qt, stateC[:, d, h, :], True, True)
                        ins = mm(bank[1][:, 272 + 4 * d + h:273 + 4 * d + h], qt, nst[:, 4 * d + h:4 * d + h + 1],
                                 True, True)
                ins.then_inc(nu_ok, 1)
                fill(32 + q)
            eng.wait_ge(nu_t, 4)
            for h in range(NH):
                ins = pe.transpose(bank[6][:, P * h:P * h + P], kT[:, h, 0:T], ident)
            ins.then_inc(kr_ok, 1)
            eng.wait_ge(kw_ok, 1)
            for d in range(NDIR):
                for h in range(NH):
                    k_ = kw[:, d, h, :]
                    mm(bank[4 + d][:, P * h:P * h + P], k_, vrow[:, 0, P * h:P * h + P], True, True)
                    ins = mm(bank[3][:, 288 + 4 * d + h:289 + 4 * d + h], k_, ones[:, 0:1], True, True)
                ins.then_inc(cs_ok, 1)

            eng.wait_ge(cs_t, 3)
            for r in range(2):
                for g in range(G):
                    if r:
                        eng.wait_ge(iz_ok, g + 1)
                    mm(bank[4 + 2 * g][:, :], C("fc"), u[:, g, 0:HW], True, True)
                    mm(bank[5 + 2 * g][:, :], C("fsn"), u[:, g, 0:HW], True, True).then_inc(fz_mm, 1)
                    fill(36 + 6 * r + g)
                for g in range(G):
                    eng.wait_ge(fz_ok, 2 * r + g + 1)
                    mm(bank[1 + 2 * g][:, :], C("ic"), hyT[g][:, 0, :], True, False)
                    mm(bank[1 + 2 * g][:, :], C("is"), hyT[g][:, 2, :], False, True).then_inc(iz_mm, 1)
                    fill(38 + 6 * r + 2 * g)
                    fill(39 + 6 * r + 2 * g)
            ada_cols(47)
            turn_rows(1)

            def gate_rows(s):
                eng.wait_ge(gbs, s + 1)
                for q in range(4):
                    for j in range(4):
                        c = 512 * (q % 2) + P * j
                        ins = mm(bank[4 + q][:, P * j:P * j + P], Gb[:, q // 2, c:c + P], ident, True, True)
                    ins.then_inc(gbm, 1)

            def out_proj(n0, s, w0):
                wait_hT(s)
                for i in range(4):
                    n = n0 + i
                    landed(w0 + i)
                    if n >= 2 and i >= 2:
                        eng.wait_ge(ro_t, n - 1)
                    rows_of(bank[n % 2], w0 + i).then_inc(tile_used, 1)

            wait_hT(1)
            gate_rows(0)
            out_proj(0, 1, WOUT)

            def wide(f, c, i):
                n = at_b(c) if i else at_a(c)
                w = (f[3] + n) % SPL
                hi, lo = (t[:, w, :].rearrange("p (k n) -> p k n", k=HALFK) for t in (w_hi, w_lo))
                eng.wait_ge(lo_ok, n_split(f, n))
                for g in range(f[0]):
                    b, up, _ = unit_at(f, c, g)
                    at = g if f is FFN0 else f[2] // NCH % 2
                    if i == 0 and (f is not FFN0 or c > 0):
                        eng.wait_ge(h_g, n_unit(f, c - (1 if f is FFN0 else 2), g))
                    for kk in range(HALFK):
                        k = HALFK * i + kk
                        xh, xl = (t[:, k, T * at:T * at + T] for t in (x_hi, x_lo))
                        mm(up[:, :], xh, hi[:, kk, :], k == 0, False)
                        mm(up[:, :], xh, lo[:, kk, :], False, False)
                        ins = mm(up[:, :], xl, hi[:, kk, :], False, k == KD - 1)
                ins.then_inc(split_used, 1)

            def turn_hidden(f, c):
                for g in range(f[0]):
                    b, _, turn = unit_at(f, c, g)
                    eng.wait_ge(h_g, n_unit(f, c, g))
                    for j in range(2):
                        ins = pe.transpose(turn[:, P * j:P * j + P], grow[b][:, P * j:P * j + P], ident)
                    ins.then_inc(h_t, 1)

            def down(f, c):
                n = at_w(c)
                w = (f[3] + n) % SPL
                hi, lo = (t[:, w, :].rearrange("p (j n) -> p j n", j=2) for t in (w_hi, w_lo))
                eng.wait_ge(lo_ok, n_split(f, n))
                for g in range(f[0]):
                    b, _, _ = unit_at(f, c, g)
                    eng.wait_ge(gl_ok, n_unit(f, c, g))
                    for j in range(2):
                        gh, gl = (t[:, b, P * j:P * j + P] for t in (g_hi, g_lo))
                        first, last = c == 0 and j == 0, c == NCH - 1 and j == 1
                        outs = [(bank[4 + 2 * g + h][:, :], slice(512 * h, 512 * h + 512)) for h in range(2)]
                        for out, cc in outs:
                            mm(out, gh, hi[:, j, cc], first, False)
                            mm(out, gh, lo[:, j, cc], False, False)
                        for out, cc in outs:
                            ins = mm(out, gl, hi[:, j, cc], False, last)
                ins.then_inc(split_used, 1)

            turn_rows(2)
            wait_hT(2)
            eng.wait_ge(ro_t, 4)
            eng.wait_ge(x_l, 2)
            for c in range(NCH):
                wide(FFN0, c, 0)
                if c:
                    turn_hidden(FFN0, c - 1)
                wide(FFN0, c, 1)
                if c == 0:
                    gate_rows(1)
                    eng.wait_ge(gbt, 8)
                if c:
                    down(FFN0, c - 1)
            turn_hidden(FFN0, NCH - 1)
            down(FFN0, NCH - 1)

            turn_rows(3)
            wait_hT(3)
            for i in range(6):
                proj(15 + i, QKV0 + i, "rows")
            for q in range(4):
                g = q // 2
                eng.wait_ge(q_ok, g + 1)
                for j in range(4):
                    c = P * (4 * (q % 2) + j)
                    ins = pe.transpose(bank[4 + q][:, P * j:P * j + P], qkv[:, g, c:c + P], ident)
                ins.then_inc(at_t, 1)
            eng.wait_ge(k_dup, 1)
            eng.wait_ge(ld_at, 16 * 6)
            eng.wait_ge(tj_t, 21)
            for q in range(3):
                for v in range(KV):
                    src = (kd[:, q, v] if q < 2 else ckd[:, v]).rearrange("p d n -> p (d n)")
                    ins = pe.transpose(bank[q][:, P * v:P * v + P], src, ident)
                ins.then_inc(at_t, 1)
            eng.wait_ge(at_ta, 4)
            gate_rows(2)
            eng.wait_ge(at_td, 3)

            def scores(v):
                b = 3 * (v % 2)
                if v >= 2:
                    eng.wait_ge(pv_t, v - 1)
                    eng.wait_ge(sc_e, v - 1)
                for part, g in enumerate((0, 1, 1)):
                    for i in range(4):
                        h = 4 * v + i
                        keys = ckT[h % 2][:, v, :] if part == 1 else akT[h % 2][:, v, T * g:T * g + T]
                        ins = mm(bank[b + part][:, P * i:P * i + P], aqT[:, h // 2, T * g:T * g + T], keys, True, True)
                ins.then_inc(sc_mm, 1)

            eng.wait_ge(gbt, 12)
            scores(0)
            for v in range(KV):
                if v + 1 < KV:
                    scores(v + 1)
                b = 3 * (v % 2)
                eng.wait_ge(sc_e, v + 1)
                for q in range(3):
                    n = 3 * v + q
                    if n >= 2:
                        eng.wait_ge(pt_t, n - 1)
                    for j in range(4):
                        i = 4 * q + j
                        ins = pe.transpose(bank[6 + n % 2][:, P * j:P * j + P], Pb[v % 2][:, P * i:P * i + P], ident)
                    ins.then_inc(pt_mm, 1)
                eng.wait_ge(pt_t, 3 * v + 3)
                for h in range(4):
                    own = slice(1280 + AHD * v, 1280 + AHD * v + AHD)
                    PT = [PTb[v % 2][:, P * (4 * q + h):P * (4 * q + h) + P] for q in range(3)]
                    mm(bank[b][:, AHD * h:AHD * h + AHD], PT[0], qkv[:, 0, own], True, True)
                    out = bank[b][:, TW + AHD * h:TW + AHD * h + AHD]
                    mm(out, PT[1], cv[:, AHD * v:AHD * v + AHD], True, False)
                    ins = mm(out, PT[2], qkv[:, 1, own], False, True)
                ins.then_inc(pv_mm, 1)
            turn_rows(4)
            eng.wait_ge(pv_t, 4)
            out_proj(4, 4, AOUT)

            turn_rows(5)
            wait_hT(5)
            eng.wait_ge(ro_t, 8)
            eng.wait_ge(ld_r, 32)
            rows_of(bank[0], None, NE, msm[:, 0:64].rearrange("p (k n) -> p k n", k=KD)).then_inc(r_mm, 1)
            for q in range(4):
                g = q // 2
                for j in range(4):
                    k = 4 * (q % 2) + j
                    ins = pe.transpose(bank[4 + q][:, P * j:P * j + P], hT[:, k, T * g:T * g + T], ident)
                ins.then_inc(hr_mm, 1)
            eng.wait_ge(r_sel, 1)
            sel = rw[:, 32:48].rearrange("p (g e) -> p g e", g=G)
            mm(bank[1][:, 0:8], C("prefix"), sel[:, 0, :], True, True)
            mm(bank[1][:, 8:16], C("prefix"), sel[:, 1, :], True, False)
            mm(bank[1][:, 8:16], ones[:, :], sel[:, 0, :], False, True)
            mm(bank[1][:, 16:24], ones[:, :], sel[:, 0, :], True, False)
            mm(bank[1][:, 16:24], ones[:, :], sel[:, 1, :], False, True).then_inc(r_pos, 1)
            eng.wait_ge(hr_t, 4)
            gate_rows(3)

            def gather(n0, par, p=None, step=0):
                eng.wait_ge(p_ok, plus(p, step, n0 + 1))
                if n0:
                    eng.wait_ge(cb_t, plus(p, 4 * step, 4 * n0))
                for q in range(2):
                    for kk in range(4):
                        k = 4 * q + kk
                        for g in range(G):
                            ins = mm(bank[2 + q][:, P * kk:P * kk + P], xn[:, g, P * k:P * k + P],
                                     Psel[par][:, g, :], g == 0, g == 1)
                    ins.then_inc(gj, 1)
                for g in range(G):
                    ins = pe.transpose(bank[7][:, T * g:T * g + T], Psel[par][:, g, :], ident)
                ins.then_inc(gj, 1)

            def combine(n0, p, step, r, par, h):
                if h == 0:
                    eng.wait_ge(gj_t, plus(p, step, (n0 + 1)))
                    eng.wait_ge(x_l, plus(p, 2 * step, G + 2 * (n0 + 1)))
                    eng.wait_ge(y_a, plus(p, step, n0 - r + 1))
                    eng.wait_ge(y_d, plus(p, step, n0 - r + 1))
                else:
                    eng.wait_ge(cb_t, plus(p, 4 * step, 4 * n0 + 2))
                for i in range(2):
                    mm(bank[2 + i][:, :], PselT[par][:, T * h:T * h + T], ys[:, 512 * i:512 * i + 512], True, True
                       ).then_inc(cb, 1)

            def experts(r):
                gather(GATHERS * r, 0)
                with eng.Fori(0, NE // XB) as p:
                    for i in range(XB):
                        f = expert(p, i, r)
                        n0 = GATHERS * r + i
                        eng.wait_ge(x_l, p * (2 * XB) + (G + 2 * (n0 + 1)))
                        for c in range(NCH):
                            wide(f, c, 0)
                            if c:
                                turn_hidden(f, c - 1)
                            wide(f, c, 1)
                            if c == 1:
                                eng.wait_ge(y_a, p * XB + (n0 - r + 1))
                                eng.wait_ge(y_d, p * XB + (n0 - r + 1))
                            if c:
                                down(f, c - 1)
                            if c in (1, 3):
                                combine(n0, p, XB, r, 1 - i % 2, c // 2)
                        gather(n0 + 1, 1 - i % 2, p, XB)
                        turn_hidden(f, NCH - 1)
                        down(f, NCH - 1)
                for h in range(G):
                    combine(GATHERS * r + NE, None, 0, r, 1, h)

            eng.wait_ge(gbt, 16)
            eng.wait_ge(r_ok, 1)
            experts(0)
            crowded = eng.value_load(flag[0:1, 0:1], min_val=0, max_val=1)
            with eng.If(crowded > 0):
                experts(1)


_INS = ["x_prompt", "x_sample", "state_C", "state_n", "state_m", "cache_k", "cache_v", "c", "c_ctx",
        "norm1_g", "norm2_g", "w_ada", "b_ada", "ev_w_in", "ev_conv", "hy_w1", "hy_b1", "hy_w2", "hy_b2", "hy_w3",
        "hy_freq", "hy_d", "ml_b_gate", "ml_norm_g", "ev_w_out", "ff_w1", "ff_w3", "ff_w2", "at_w_qkv", "at_q_g",
        "at_k_g", "at_sink", "at_w_out", "moe_w_router", "moe_b_router", "moe_w1", "moe_w3", "moe_w2"]
_OUTS = [("y_prompt", (1, T, D)), ("y_sample", (1, T, D)), ("C", (1, 1, NDIR, NH, HD, HD)), ("n", (1, 1, NDIR, NH, HD)),
         ("m", (1, 1, NDIR, NH)), ("k", (1, 1, KV, T, AHD)), ("v", (1, 1, KV, T, AHD))]


def kernel(**inputs):
    import concourse.bacc as bacc
    from concourse.bass_utils import run_bass_kernel_spmd

    nc = bacc.Bacc("TRN2", target_bir_lowering=False, num_devices=1)
    arrays, ins, outs = {}, {}, {}
    for name in _INS + ["constants"]:
        arr = np.ascontiguousarray(inputs[name]) if name != "constants" else constants()
        arrays[f"in_{name}"] = arr
        ins[name] = nc.dram_tensor(f"in_{name}", arr.shape, mybir.dt.from_np(arr.dtype), kind="ExternalInput").ap()
    for name, shape in _OUTS:
        outs[name] = nc.dram_tensor(f"out_{name}", shape, F32, kind="ExternalOutput").ap()
    trunk(nc, ins, outs)
    r = run_bass_kernel_spmd(nc, [arrays], core_ids=[0])
    return tuple(r.results[0][f"out_{name}"] for name, _ in _OUTS)
```

```python
from contextlib import ExitStack, nullcontext

import concourse.bass as bass
import numpy as np
from concourse import mybir

ALU = mybir.AluOpType
ACT = mybir.ActivationFunctionType
F32 = mybir.dt.float32
F32R = mybir.dt.float32r
I32 = mybir.dt.int32
AX = mybir.AxisListType.X

P = 128
D = 1024
KD = D // P
G = 2
T = 128
HW = 512
NH = 4
HD = 128
NDIR = 2
FF = 2816
NE = 8
QH, KV, AHD = 16, 4, 64
ROWS = 40
TW = 256
RAW = 4
RAWX = 6
SPL = 3
NCH = FF // TW
NFW = 3 * NCH
HALFK = KD // 2
XB = 4
EPS = 1e-6
NEG = -1e30
TWO_PI = 2.0 * np.pi
RND = float(1.5 * 2 ** 23)

CONST_COLS = {}


def _columns():
    at = 0
    for name, n in (("ident", P), ("prefix", P), ("mask", 2 * P), ("iota", 2 * P), ("shift", 2 * P),
                    ("fc", P), ("fsn", P), ("fs0", P), ("fd", P), ("gc", P), ("gs0", P), ("gd", P),
                    ("ic", P), ("is", P), ("decay", HW), ("zt", P), ("cos", 32), ("sin", 32), ("tri", 64),
                    ("eps", 1), ("one", 1), ("pair", G), ("spread", 2 * G * ROWS)):
        CONST_COLS[name] = (at, n)
        at += n
    return at


NCONST = _columns()


def constants():
    c = np.zeros((P, NCONST), np.float64)

    def put(name, a):
        at, n = CONST_COLS[name]
        c[:a.shape[0], at:at + n] = a.reshape(a.shape[0], n)

    i = np.arange(P)
    put("ident", np.eye(P))
    put("prefix", (i[:, None] <= i[None, :]).astype(float))
    put("mask", np.stack([np.where(i[:, None] <= i[None, :], 0, NEG),
                          np.where(i[:, None] >= i[None, :], 0, NEG)], 1))
    put("iota", np.broadcast_to(np.arange(2 * P)[None], (P, 2 * P)).copy())
    put("shift", np.stack([(i[:, None] == i[None, :] - 1), (i[:, None] == i[None, :] + 1)], 1).astype(float))
    n2 = 2 * T
    ang = 2 * np.pi * ((i[:, None] * i[None, :]) % n2) / n2
    alt = (-1.0) ** i
    cosm, sinm = np.cos(ang), -np.sin(ang)
    sin_ny, cos_ny = sinm.copy(), cosm.copy()
    sin_ny[:, 0] = alt
    cos_ny[:, 0] = alt
    put("fc", cosm)
    put("fsn", sin_ny)
    put("fs0", sinm)
    put("fd", cos_ny)
    keep = (i > 0).astype(float)[:, None]
    put("gc", cosm * keep)
    put("gs0", -sinm * keep)
    put("gd", cos_ny * keep)
    wt = np.where(i == 0, 1.0, 2.0)[:, None] / n2
    inv_s = 2 * sinm / n2
    inv_s[0, :] = alt / n2
    put("ic", cosm * wt)
    put("is", inv_s)
    f32 = np.float32
    t = np.linspace(0.0, 1.0, T, dtype=f32)[:, None]
    w = (2.0 * np.pi * np.arange(T, dtype=f32)[:, None] / T).astype(f32)
    bands = np.linspace(1e-4, 15, 16, dtype=f32)[None]
    z = np.concatenate([t, np.cos(bands * w), -np.sin(bands * w)], -1)
    put("zt", z.T)
    deltas = np.linspace(np.log(1e-2) / 1.5, np.log(1e-2) / 0.3, HW, dtype=f32)
    put("decay", np.exp(-t * np.abs(deltas)))
    inv = (10000.0 ** (-np.arange(0, 32, 2, dtype=f32) / 32)).astype(f32)
    pos = np.stack([i // 64, i % 64], 1).astype(f32)
    a = pos[:, :, None] * inv[None, None]
    put("cos", np.cos(a))
    put("sin", np.sin(a))
    j = np.arange(NE)
    put("tri", np.broadcast_to((j[None, :] < j[:, None]).astype(float)[None], (P, NE, NE)).copy())
    put("eps", np.full((P, 1), EPS))
    put("one", np.ones((P, 1)))
    put("pair", np.stack([i % G == g for g in range(G)], 1).astype(float))
    spread = np.zeros((16, 2, G, ROWS))
    for d in range(NDIR):
        for f in range(2):
            for g in range(G):
                for h in range(NH):
                    spread[8 * d + 4 * f + h, f, g, 32 * d + 4 * g + h] = 1
    put("spread", spread)
    return c.astype(np.float32)


def trunk(nc, a, o):
    with ExitStack() as ctx:
        ctx.enter_context(nc.allow_non_contiguous_dma(reason="vectors of at most 4 KB into columns"))

        def sb(name, shape, dt=F32):
            return ctx.enter_context(nc.sbuf_tensor(name, shape, dt))

        def sem(name):
            return ctx.enter_context(nc.semaphore(name))

        bank = [ctx.enter_context(nc.psum_tensor(f"bank{i}", [P, 512], F32)) for i in range(8)]

        raw = sb("raw", [P, RAW, 2048])
        cst = sb("cst", [P, NCONST])
        x = sb("x", [P, G, D])
        x_hi = sb("x_hi", [P, KD, G * T], F32R)
        x_lo = sb("x_lo", [P, KD, G * T], F32R)
        w_hi = sb("w_hi", [P, SPL, 2048], F32R)
        w_lo = sb("w_lo", [P, SPL, 2048], F32R)
        xn = sb("xn", [P, G, D])
        Gb = sb("Gb", [P, G, D])
        stage = sb("stage", [2 * G, 2, 512])
        condT = sb("condT", [P, KD, G])
        cond_hl = sb("cond_hl", [P, KD, 2 * G], F32R)
        cond_h0 = sb("cond_h0", [P, KD, 2 * G], F32R)
        warmed = sb("warmed", [P, 8])
        adac = sb("adac", [P, P])
        modc = sb("modc", [P, 2, 6, KD, G])
        sca = sb("sca", [P, 4, KD, G])
        ones = sb("ones", [P, P])
        ssq = sb("ssq", [P, 8])
        rt = sb("rt", [P, 8])
        rstd = sb("rstd", [P, 8])
        gb = sb("gb", [ROWS, 2])
        m0 = sb("m0", [ROWS, 1])
        cols = sb("cols", [P, 4, 64])
        sml = sb("sml", [P, 256])
        hyp = sb("hyp", [64, 64 + 8])
        hyw1 = sb("hyw1", [33, 64])
        nst = sb("nst", [P, 16])
        msm = sb("msm", [P, 96])
        mlx = sb("mlx", [ROWS, 2])
        flag = sb("flag", [1, 1], I32)
        with nc.sbuf_tensor("arena", [P, 16896], F32) as arena:
            pass
        sb("arena_0", [P, 5120])
        PselT = [sb(f"selT{i}", [P, G * T], F32R) for i in range(2)]
        sb("arena_1", [P, 6144 - 5120 - 2 * G * T])
        y_hi = sb("y_hi", [P, D], F32R)
        y_lo = sb("y_lo", [P, D], F32R)
        sb("arena_2", [P, 12800 - 6144 - 2 * D])
        g_hi = sb("g_hi", [P, 2, TW], F32R)
        g_lo = sb("g_lo", [P, 2, TW], F32R)
        sb("arena_high", [P, 16896 - 12800 - 4 * TW])
        hF = Gb[:, :, :].rearrange("p g n -> p (g n)").rearrange("p (k n) -> p k n", k=KD)

        def C(name, rows=P):
            at, n = CONST_COLS[name]
            return cst[0:rows, at:at + n]

        ident = C("ident")
        modb = adac[:, 0:96].rearrange("p (l j) -> p l j", l=2)
        ngc = adac[:, 96:P].rearrange("p (n k) -> p n k", n=4)

        def ar(at, n):
            return arena[:, at:at + n]

        u = ar(0, 3072).rearrange("p (g n) -> p g n", g=G)
        convw = ar(3072, 4608).rearrange("p (w n) -> p w n", w=3)
        spec = ar(7680, 3072).rearrange("p (o i n) -> p o i n", o=2, i=3)
        vrow = ar(10752, 1024).rearrange("p (g n) -> p g n", g=G)
        sigo = ar(11776, 1024).rearrange("p (g n) -> p g n", g=G)
        qT = ar(12800, 1024).rearrange("p (h n) -> p h n", h=NH)
        kT = ar(13824, 1024).rearrange("p (h n) -> p h n", h=NH)
        hy1 = ar(14848, 2048).rearrange("p (i n) -> p i n", i=4)
        hyT = [Gb[:, :, :].rearrange("p g (i n) -> p (g i) n", i=2), hy1]
        taps = ar(10752, 2048).rearrange("p (i n) -> p i n", i=4)
        mags = ar(12800, 2048).rearrange("p (i n) -> p i n", i=4)
        hyhw3 = arena[0:64, 14848:16896]
        skip = Gb[0:1, 0, 0:1024]
        ada_rows = ar(7680, P)
        gcol = arena[0:16, 0:G * T]
        sinb = ar(0, 1024).rearrange("p (i n) -> p i n", i=8)
        rowq = hy1[0:ROWS, :, :].rearrange("p i n -> p (i n)").rearrange("p (i n) -> p i n", i=16)
        WT = ar(3072, 2048).rearrange("p (c n) -> p c n", c=16)
        ST = ar(5120, 2048).rearrange("p (c n) -> p c n", c=16)
        selr = xn[0:ROWS, :, :].rearrange("p g n -> p (g n)").rearrange("p (c n) -> p c n", c=16)
        kw = hy1[:, 0:2, :].rearrange("p i n -> p (i n)").rearrange("p (d h n) -> p d h n", d=NDIR, h=NH)
        cout = ar(13824, 1024).rearrange("p (d n) -> p d n", d=NDIR)
        stateC = [ar(c, 512).rearrange("p (h n) -> p h n", h=NH) for c in (7168, 3072)]
        mgain = ar(4096, 512)

        qkv = ar(0, 3072).rearrange("p (g n) -> p g n", g=G)
        sqs = ar(9984, 2560).rearrange("p (g n) -> p g n", g=G)
        rtmp = ar(13056, 1024).rearrange("p (i n) -> p i n", i=4)
        aqT = ar(5632, 2048).rearrange("p (j n) -> p j n", j=8)
        akT = [ar(c, 1024).rearrange("p (v n) -> p v n", v=KV) for c in (7680, 4096)]
        ckd = ar(8704, 512).rearrange("p (v d n) -> p v d n", v=KV, d=2)
        ckT = [ar(c, 512).rearrange("p (v n) -> p v n", v=KV) for c in (9216, 5120)]
        kd = ar(3072, 1024).rearrange("p (g v d n) -> p g v d n", g=G, v=KV, d=2)
        cv = ar(9728, 256)
        Pb = [ar(9984, 1536), ar(11520, 1536)]
        PTb = [ar(13056, 1536), ar(14592, 1536)]
        qkg = ar(16128, 128)
        sinkb = ar(16256, 16)
        Psel = [ar(4096 + 256 * i, 256).rearrange("p (g n) -> p g n", g=G) for i in range(2)]
        acc = ar(8192, 2048).rearrange("p (g n) -> p g n", g=G)
        sa = [ar(10240 + 256 * i, 256) for i in range(2)]
        grow = [ar(10752 + 256 * i, 256) for i in range(2)]
        tmpf = ar(11264, 1024).rearrange("p (i n) -> p i n", i=2)
        rw = ar(12288, 512)
        tmpr = ar(14848, 1024).rearrange("p (i n) -> p i n", i=2)

        slot = [sem(f"slot{i}_filled") for i in range(RAWX)]
        ld_c = sem("ld_cond")
        ld_k = sem("ld_constants")
        ld_x = sem("ld_x")
        ld_a = sem("ld_adaln")
        ac_mm = sem("adaln_constants_turned")
        ac_t = sem("adaln_constants_taken")
        ld_h = sem("ld_hyena")
        ld_h2 = sem("ld_hyena_skip")
        ld_g = sem("ld_gate_rows")
        ld_cw = sem("ld_conv")
        ld_n = sem("ld_states")
        ld_C = [sem("ld_state_C_forward"), sem("ld_state_C_backward")]
        ld_mg = sem("ld_mlstm_gain")
        ld_at = sem("ld_attention")
        ld_r = sem("ld_router")
        pz = sem("pool_zeroed")
        dve = sem("dve_chain")
        act = sem("act_chain")
        stored = sem("outputs_stored")
        stored_st = sem("states_stored")
        stored_kv = sem("keys_values_stored")
        cond_ok = sem("cond_silu")
        ada_stg = sem("ada_rows_staged")
        ada_col = sem("ada_columns_made")
        modc_ok = sem("modc_ready")
        f_mm = sem("filter_products")
        f_arg = sem("filter_sine_args")
        f_sin = sem("filter_sines")
        f_tap = sem("filter_taps")
        f_abs = sem("filter_magnitudes")
        f_nrm = sem("filter_normalised")
        f_spec = sem("filter_spectra")
        f_spt = sem("filter_spectra_taken")
        n_rt = sem("norm_root")
        ff_g0 = sem("prompt_ffn_summed")
        resid = sem("ffn_residual_updated")
        rows_ok = sem("rows_ready")
        turned = sem("rows_turned")
        hT_a = sem("modulated_by_act")
        hT_d = sem("modulated_by_dve")
        cond_s = sem("cond_split")
        tj_t = sem("projection_taken")
        g_rows = sem("gate_rows_ready")
        g_in = sem("gate_rows_taken")
        g_f = sem("forget_exp_log")
        g_mu = sem("gate_scans")
        g_ex = sem("gate_exps")
        g_col = sem("gate_columns")
        g_colt = sem("gate_columns_taken")
        sel_ok = sem("row_selectors")
        qk_ok = sem("qk_ready")
        kr_ok = sem("k_rows_turned")
        kw_ok = sem("k_weighted")
        wt_mm = sem("weight_logs")
        wt_ok = sem("weights_exp")
        st_ok = sem("scores_ready")
        nu_ok = sem("numerator_ready")
        nu_t = sem("numerator_taken")
        cs_ok = sem("states_ready")
        cs_t = sem("states_taken")
        hs_q = sem("head_squares")
        hs_r = sem("head_roots")
        so_ok = sem("sigmoid_o")
        cw_ok = sem("conv_taps_applied")
        cv_mm = sem("conv_shifted")
        cv_ok = sem("conv_done")
        fz_mm = sem("dft_ready")
        fz_ok = sem("spectrum_product")
        iz_mm = sem("inverse_ready")
        iz_ok = sem("hyena_gated")
        gbs = sem("gate_broadcast_source")
        gbm = sem("gate_broadcast_made")
        gbt = sem("gate_broadcast_taken")
        ro_t = sem("out_projection_taken")
        az = sem("attention_zeroed")
        q_sq = sem("qk_squares")
        q_rt = sem("qk_roots")
        q_ok = sem("qk_normed")
        k_dup = sem("k_doubled")
        at_t = sem("attention_turned")
        at_ta = sem("attention_turned_by_act")
        at_td = sem("attention_turned_by_dve")
        sc_mm = sem("logits_ready")
        sc_m = sem("logits_max")
        sc_e = sem("probs_ready")
        sk_e = sem("sink_exp")
        pt_mm = sem("probs_turned")
        pt_t = sem("probs_turned_taken")
        pv_mm = sem("values_mixed")
        pv_t = sem("values_taken")
        r_mm = sem("router_logits")
        r_l = sem("router_shifted")
        r_e = sem("router_exp")
        r_sel = sem("router_selected")
        r_pos = sem("router_positions")
        r_ok = sem("router_tables")
        hr_mm = sem("token_rows_turned")
        hr_t = sem("token_rows_taken")
        p_ok = sem("selector_built")
        gj = sem("gather_ready")
        gj_t = sem("selector_turned_taken")
        x_h = sem("input_high_parts")
        x_l = sem("input_low_parts")
        cb = sem("combine_ready")
        cb_t = sem("combine_taken")
        hi_ok = sem("weight_high_parts")
        lo_ok = sem("weight_low_parts")
        used = sem("tile_used")
        h_sa = sem("hidden_silu")
        h_g = sem("hidden_gated")
        h_t = sem("hidden_turned")
        gh_ok = sem("hidden_high_parts")
        gl_ok = sem("hidden_low_parts")
        y_a = sem("ffn_taken_by_act")
        y_d = sem("ffn_taken_by_dve")
        fin = sem("output_rows")

        w_in = a["ev_w_in"][0]

        def columns(w, c0, n):
            return [w[:, c0:c0 + n].rearrange("(k p) n -> p k n", p=P)]

        def halves(w, c0, n=512):
            t = columns(w, c0, n)[0]
            return [t[:, 0:HALFK, :], t[:, HALFK:KD, :]]

        base_q, base_v, base_o, base_g = 3 * HW, 3 * HW + 2 * HW, 3 * HW + 3 * HW, 3 * HW + 4 * HW
        NB = 6 * D // 512
        stream = []
        for i in range(NB):
            stream += halves(a["w_ada"][0], 512 * i)
        IN0 = len(stream)
        stream += columns(w_in, base_g, 16)
        for i in range(4):
            stream += columns(w_in, base_q + TW * i, TW)
        stream += halves(w_in, base_v) + halves(w_in, base_o)
        for i in range(3):
            stream += halves(w_in, HW * i)
        ADA1 = len(stream)
        for i in range(NB):
            stream += halves(a["w_ada"][1], 512 * i)
        WOUT = len(stream)
        stream += halves(a["ev_w_out"][0], 0) + halves(a["ev_w_out"][0], 512)
        FF0 = len(stream)
        late = []
        QKV_BLOCKS = (2, 0, 1)
        for w in QKV_BLOCKS:
            late += halves(a["at_w_qkv"][0], 512 * w)
        late += halves(a["at_w_out"][0], 0) + halves(a["at_w_out"][0], 512)
        QKV0 = FF0 + NFW
        AOUT = QKV0 + 6
        MOE0 = QKV0 + len(late)
        GATHERS = NE + 1
        assert XB * NFW % RAWX == 0 and NE * NFW % RAWX == 0 and XB * NFW % SPL == 0 and NE % XB == 0

        def split_tile(n, k):
            return [t[:, n % SPL, :].rearrange("p (k n) -> p k n", k=k) for t in (w_hi, w_lo)]

        def raw_slot(n, p=None):
            if n < MOE0:
                s, fills = n % RAW, n // RAW + 1
            else:
                s = (n - MOE0) % RAWX
                fills = (n - MOE0) // RAWX + 1
                if s < RAW:
                    s = (MOE0 + s) % RAW
                    fills += len(range(s, MOE0, RAW))
            place = raw[:, s, :] if s < RAW else ar(2048 * (s - RAW), 2048)
            return place, slot[s], plus(p, XB * NFW // RAWX * 32, 32 * fills)

        def tile_columns(n):
            return 16 * KD if n == IN0 else 2048

        def high_of(eng, n, p=None):
            place, filled, count = raw_slot(n, p)
            eng.wait_ge(filled, count)
            if n >= SPL:
                eng.wait_ge(used, plus(p, XB * NFW, n - SPL + 1))
            c = slice(0, tile_columns(n))
            nc.scalar.copy(w_hi[:, n % SPL, c], place[:, c]).then_inc(hi_ok, 1)

        def low_of(eng, n, p=None):
            eng.wait_ge(hi_ok, plus(p, XB * NFW, n + 1))
            c = slice(0, tile_columns(n))
            nc.vector.tensor_tensor(w_lo[:, n % SPL, c], raw_slot(n)[0][:, c], w_hi[:, n % SPL, c].bitcast(F32),
                                    ALU.subtract).then_inc(lo_ok, 1)

        MODULATED = (0, 2, 3, 5)

        def inputs_split(s):
            return 4 * min(s + 1, 5)

        X0 = inputs_split(5)

        def last_tile(t):
            if t < 5:
                return IN0 + t
            return IN0 + 6 + 2 * ((t - 5) // 2) if t < 15 else QKV0 + 1 + 2 * ((t - 15) // 2)

        def out_bank(n):
            return bank[n % 4]

        def ada_bank(m):
            return bank[m % 2 if m < NB else 0]

        FFN0 = (G, None, 0, FF0)

        def expert(p, i, r):
            e = r * NE + i
            return (1, p, G * NCH + NCH * e, MOE0 + NFW * e)

        def plus(p, step, n):
            return n if p is None else p * step + n

        def next_expert(eng, p, i):
            return eng.If(p < NE // XB - 1) if i == XB - 1 else nullcontext()

        def n_unit(f, c, g=0):
            return plus(f[1], XB * NCH, f[2] + f[0] * c + g + 1)

        def n_split(f, i):
            return plus(f[1], XB * NFW, f[3] + i + 1)

        def at_a(c):
            return 3 * c - (c > 0)

        def at_b(c):
            return 3 * c + (c == 0)

        def at_w(c):
            return min(3 * c + 4, NFW - 1)

        def order():
            for c in range(NCH):
                yield "A", c
                yield "B", c
                if c:
                    yield "W", c - 1
            yield "W", NCH - 1

        for n_, (kind_, c_) in enumerate(order()):
            assert n_ == {"A": at_a, "B": at_b, "W": at_w}[kind_](c_)

        def unit_at(f, c, g):
            b = g if f[0] == G else c % 2
            return b, bank[b], bank[2 + g] if f[0] == G else bank[6 + b]

        STATE_STORES = 16 * (NDIR + 2)

        block = ctx.enter_context(nc.Block())

        @block.sync
        def _(sp):
            def load_rows(n, src):
                if n >= RAW:
                    sp.wait_ge(lo_ok, n - RAW + 1)
                k, w = src.shape[1] // 2, src.shape[2]
                place, filled, _ = raw_slot(n)
                for h in range(2):
                    sp.dma_start(place[:, k * w * h:k * w * (h + 1)].rearrange("p (k n) -> p k n", k=k),
                                 src[:, k * h:k * (h + 1), :]).then_inc(filled, 16)

            def load(n, kind, c, w1, w3, w2):
                place, filled, _ = raw_slot(n)
                cols_, rows_ = slice(TW * c, TW * c + TW), slice(HALFK * (kind == "B"), HALFK * (kind == "B") + HALFK)
                if kind == "W":
                    for i in range(2):
                        sp.dma_start(place[:, D * i:D * i + D], w2(2 * c + i)).then_inc(filled, 16)
                else:
                    t = place.rearrange("p (k n) -> p k n", k=HALFK)
                    sp.dma_start(t[:, :, 0:TW], w1(rows_, cols_)).then_inc(filled, 16)
                    sp.dma_start(t[:, :, TW:2 * TW], w3(rows_, cols_)).then_inc(filled, 16)

            for n, src in enumerate(stream):
                load_rows(n, src)
            w1 = a["ff_w1"][0].rearrange("(k p) n -> p k n", p=P)
            w3 = a["ff_w3"][0].rearrange("(k p) n -> p k n", p=P)
            w2 = a["ff_w2"][0].rearrange("(j p) n -> p j n", p=P)
            for j, (kind, c) in enumerate(order()):
                sp.wait_ge(lo_ok, FF0 + j - RAW + 1)
                load(FF0 + j, kind, c, lambda r, n: w1[:, r, n], lambda r, n: w3[:, r, n], lambda i: w2[:, i, :])
            for i, src in enumerate(late):
                load_rows(QKV0 + i, src)
            e1 = a["moe_w1"][0].rearrange("e (k p) n -> e p k n", p=P)
            e3 = a["moe_w3"][0].rearrange("e (k p) n -> e p k n", p=P)
            e2 = a["moe_w2"][0].rearrange("e (j p) n -> e p j n", p=P)

            def experts(r):
                with sp.Fori(0, NE // XB) as p:
                    for i in range(XB):
                        f = expert(p, i, r)
                        e = bass.ds(p * XB + i, 1)
                        for n, (kind, c) in enumerate(order()):
                            if r == 0 and i == 0 and n < RAW:
                                sp.wait_ge(lo_ok, MOE0 + n - RAW + 1)
                            elif r == 0 and i == 0 and n < RAWX:
                                sp.wait_ge(used, AOUT + 1)
                                sp.wait_ge(stored_kv, 32)
                            sp.wait_ge(lo_ok, n_split(f, n - RAWX))
                            load(f[3] + n, kind, c,
                                 lambda rr, nn: e1[e, :, rr, nn].rearrange("a p k n -> p (a k) n"),
                                 lambda rr, nn: e3[e, :, rr, nn].rearrange("a p k n -> p (a k) n"),
                                 lambda jj: e2[e, :, jj, :].rearrange("a p n -> p (a n)"))

            experts(0)
            sp.wait_ge(r_ok, 1)
            crowded = sp.value_load(flag[0:1, 0:1], min_val=0, max_val=1)
            with sp.If(crowded > 0):
                experts(1)
            sp.wait_ge(stored_st, STATE_STORES)
            sp.wait_ge(stored_kv, 32)
            sp.wait_ge(stored, 32)


        @block.gpsimd
        def _(pool):
            gp = nc.gpsimd
            gp.memset(cond_h0[:, :, G:2 * G].bitcast(F32), 0.0).then_inc(cond_s, 1)
            gp.dma_start(hyw1[:], a["hy_w1"][0]).then_inc(ld_h, 16)
            gp.dma_start(hyp[:, 0:64], a["hy_w2"][0]).then_inc(ld_h, 16)
            gp.dma_start(hyp[:, 64:65], a["hy_b1"].rearrange("a n -> n a")).then_inc(ld_h, 16)
            gp.dma_start(hyp[:, 65:66], a["hy_b2"].rearrange("a n -> n a")).then_inc(ld_h, 16)
            gp.dma_start(hyp[:, 66:68], a["hy_freq"][0].rearrange("a n -> n a")).then_inc(ld_h, 16)
            gp.dma_start(hyhw3, a["hy_w3"][0]).then_inc(ld_h, 16)
            gp.dma_start(ada_rows[0:96, :], a["b_ada"].rearrange("l (j p) -> (l j) p", p=P)).then_inc(ld_a, 16)
            gp.dma_start(ada_rows[96:112, :], a["norm1_g"].rearrange("l (k p) -> (l k) p", p=P)).then_inc(ld_a, 16)
            gp.dma_start(ada_rows[112:128, :], a["norm2_g"].rearrange("l (k p) -> (l k) p", p=P)).then_inc(ld_a, 16)
            gp.dma_start(skip, a["hy_d"].rearrange("a o n -> a (o n)")).then_inc(ld_h2, 16)
            gp.memset(ones[:], 1.0).then_inc(pz, 1)
            gp.memset(gb[:], 0.0).then_inc(pz, 1)
            gp.memset(m0[:], 0.0).then_inc(pz, 1)
            pool.wait_ge(pz, 3)
            for d in range(NDIR):
                for g in range(G):
                    r = 32 * d + 4 * g
                    gp.dma_start(gb[r:r + 4, :], a["ml_b_gate"][0, d].rearrange("f h -> h f")).then_inc(ld_g, 16)
                gp.dma_start(m0[32 * d + 4:32 * d + 8, :],
                             a["state_m"][0, 0, d].rearrange("(h a) -> h a", a=1)).then_inc(ld_g, 16)
                gp.dma_start(nst[:, 4 * d:4 * d + 4], a["state_n"][0, 0, d].rearrange("h n -> n h")
                             ).then_inc(ld_n, 16)
            gp.dma_start(msm[:, 0:64].rearrange("p (k n) -> p k n", k=KD),
                         a["moe_w_router"][0].rearrange("(k p) n -> p k n", p=P)).then_inc(ld_r, 16)
            gp.dma_start(msm[:, 64:72], a["moe_b_router"].to_broadcast([P, NE])).then_inc(ld_r, 16)
            pool.wait_ge(used, 20)
            gp.dma_start(convw, a["ev_conv"][0].rearrange("(a w) n -> a w n", a=1).to_broadcast([P, 3, 3 * HW])
                         ).then_inc(ld_cw, 16)
            for d in range(NDIR):
                if d == 0:
                    pool.wait_ge(cv_ok, 6)
                else:
                    pool.wait_ge(st_ok, 4)
                gp.dma_start(stateC[d], a["state_C"][0, 0, d].rearrange("h i j -> i h j")).then_inc(ld_C[d], 16)
            gp.dma_start(mgain, a["ml_norm_g"].rearrange("a h n -> a (h n)").to_broadcast([P, HW])
                         ).then_inc(ld_mg, 16)
            pool.wait_ge(resid, 2)
            for odd in range(2):
                other = slice(0, 64) if odd else slice(64, 128)
                gp.memset(akT[odd][other], 0.0).then_inc(az, 1)
                gp.memset(ckT[odd][other], 0.0).then_inc(az, 1)
            for d in range(2):
                gp.dma_start(ckd[:, :, d, :], a["cache_k"][0, 0].rearrange("v s n -> s v n")).then_inc(ld_at, 16)
            gp.dma_start(cv.rearrange("p (v n) -> p v n", v=KV), a["cache_v"][0, 0].rearrange("v s n -> s v n")
                         ).then_inc(ld_at, 16)
            gp.dma_start(qkg[:, 0:64], a["at_q_g"].to_broadcast([P, AHD])).then_inc(ld_at, 16)
            gp.dma_start(qkg[:, 64:128], a["at_k_g"].to_broadcast([P, AHD])).then_inc(ld_at, 16)
            gp.dma_start(sinkb, a["at_sink"].to_broadcast([P, QH])).then_inc(ld_at, 16)

        @block.scalar
        def _(eng):
            sc = nc.scalar
            n_chain = [0]

            def link(ins):
                n_chain[0] += 1
                ins.then_inc(act, 1)
                eng.wait_ge(act, n_chain[0])

            eng.dma_start(condT[:, :, 0:1], a["c_ctx"].rearrange("(k p a) -> p k a", p=P, a=1)).then_inc(ld_c, 16)
            eng.dma_start(condT[:, :, 1:2], a["c"].rearrange("a (k p) -> p k a", p=P)).then_inc(ld_c, 16)
            eng.wait_ge(ld_c, 32)
            link(sc.activation(condT[:], condT[:], ACT.Silu))
            sc.copy(cond_hl[:, :, 0:G], condT[:]).then_inc(cond_ok, 1)
            sc.copy(cond_h0[:, :, 0:G], condT[:]).then_inc(cond_s, 1)

            def high(n):
                high_of(eng, n)

            def stage_row(m):
                eng.wait_ge(used, (2 * m if m < NB else ADA1 + 2 * (m - NB)) + 2)
                if m >= 2:
                    eng.wait_ge(ada_col, m - 1)
                sc.copy(stage[:, m % 2, :], ada_bank(m)[0:2 * G, :]).then_inc(ada_stg, 1)

            def after_fill(i):
                if i % 2:
                    stage_row(NB + i // 2)
                high(ADA1 + i + SPL)

            n_warm = [0]

            def warm(fn):
                n_warm[0] += 1
                sc.activation(warmed[:, n_warm[0]:n_warm[0] + 1], C("one"), fn)

            def norm_root(i):
                if i:
                    warm(ACT.Sqrt)
                if i == 0:
                    eng.wait_ge(ld_x, 32)
                    eng.wait_ge(ld_k, 16)
                for g in range(G):
                    if i == 2:
                        eng.wait_ge(resid, g + 1)
                    elif i:
                        eng.wait_ge(ro_t, 2 * i + 1 + g)
                    c = slice(2 * i + g, 2 * i + g + 1)
                    link(sc.activation(xn[:, g, :], x[:, g, :], ACT.Square, accum_out=ssq[:, c]))
                    sc.activation(rt[:, c], ssq[:, c], ACT.Sqrt, bias=C("eps"), scale=1.0 / D).then_inc(n_rt, 1)

            def take_turned(s, norm):
                if norm is None:
                    for q in range(4):
                        g, h = q // 2, q % 2
                        eng.wait_ge(turned, 4 * s + q + 1)
                        sc.copy(x_hi[:, 4 * h:4 * h + 4, T * g:T * g + T],
                                bank[4 + q][:, :].rearrange("p (j n) -> p j n", j=4)).then_inc(x_h, 1)
                    return
                l, part = norm % 2, 3 * (norm // 2)
                eng.wait_ge(modc_ok, l + 1)
                n = 2 * MODULATED.index(s)
                for h in range(2):
                    eng.wait_ge(turned, 4 * s + h + 1)
                    for j in range(4):
                        k = 4 * h + j
                        ins = sc.activation(hF[:, k, 0:T], bank[4 + h][:, P * j:P * j + P], ACT.Identity,
                                            bias=modc[:, l, part, k, 0:1], scale=sca[:, norm, k, 0:1])
                    ins.then_inc(hT_a, 1)
                    if s < 5:
                        k4 = slice(4 * h, 4 * h + 4)
                        eng.wait_ge(hT_a, n + h + 1)
                        sc.copy(x_hi[:, k4, 0:T], hF[:, k4, 0:T]).then_inc(x_h, 1)
                        eng.wait_ge(hT_d, n + h + 1)
                        sc.copy(x_hi[:, k4, T:2 * T], hF[:, k4, T:2 * T]).then_inc(x_h, 1)

            def gate_rows_out(s):
                for q in range(4):
                    eng.wait_ge(gbm, 4 * s + q + 1)
                    sc.copy(Gb[:, q // 2, 512 * (q % 2):512 * (q % 2) + 512], bank[4 + q][:, :]).then_inc(gbt, 1)

            def ffn_high(f, i):
                high_of(eng, f[3] + i, f[1])

            def silu(f, c):
                eng.wait_ge(used, n_split(f, at_b(c)))
                for g in range(f[0]):
                    b, up, _ = unit_at(f, c, g)
                    if f is not FFN0 or c > 0:
                        eng.wait_ge(h_g, n_unit(f, c - (1 if f is FFN0 else 2), g))
                    sc.activation(sa[b], up[:, 0:TW], ACT.Silu).then_inc(h_sa, 1)

            def hidden_high(f, c):
                for g in range(f[0]):
                    b, _, turn = unit_at(f, c, g)
                    eng.wait_ge(h_t, n_unit(f, c, g))
                    sc.copy(g_hi[:, b, :], turn[:, 0:TW]).then_inc(gh_ok, 1)

            def chunk(f, c):
                if c:
                    hidden_high(f, c - 1)
                if c:
                    ffn_high(f, 3 * c + 2)
                if c == 0:
                    ffn_high(f, 3)
                silu(f, c)
                if 0 < c < NCH - 1:
                    ffn_high(f, 3 * c + 3)
                if c < NCH - 1:
                    ffn_high(f, 3 * c + 4)

            high(0)
            eng.dma_start(cst[:], a["constants"]).then_inc(ld_k, 16)
            high(1)
            high(2)
            for m in range(NB):
                high(2 * m + 3)
                if m == 0:
                    eng.dma_start(x[:, 0, :], a["x_prompt"][0]).then_inc(ld_x, 16)
                    eng.dma_start(x[:, 1, :], a["x_sample"][0]).then_inc(ld_x, 16)
                stage_row(m)
                high(2 * m + 4)
                if m == 4:
                    norm_root(0)
                if m in (5, 6):
                    n = m - 5
                    eng.wait_ge(f_arg, n + 1)
                    sc.activation(sinb[0:64, 4 + n, :], sinb[0:64, 3, :], ACT.Sin).then_inc(f_sin, 1)
                if m == 7:
                    eng.wait_ge(f_tap, 1)
                    for q in range(4):
                        ins = sc.activation(mags[:, q, :], taps[:, q, :], ACT.Abs)
                    ins.then_inc(f_abs, 1)
                if m >= NB - 2:
                    for q in ((0, 1) if m == NB - 2 else (2, 3, 4, 5)):
                        eng.wait_ge(f_spec, q + 1)
                        sc.copy(spec[:, q // 3, q % 3, :], bank[4 + q % 2][:, :]).then_inc(f_spt, 1)
            eng.wait_ge(f_nrm, 2)
            take_turned(0, 0)

            def take_proj(j, fn):
                eng.wait_ge(used, last_tile(j) + 1)
                fn(bank[j % 3]).then_inc(tj_t, 1)

            def take_gates(b):
                return sc.copy(gcol, b[0:16, 0:G * T])

            def two_heads(dst, i):
                return lambda b: sc.copy(dst[:, 2 * i:2 * i + 2, :], b[:, :].rearrange("p (h n) -> p h n", h=2))

            def pair(t, n, fn):
                high(n + SPL)
                take_proj(t, lambda b: fn(0, b))
                take_proj(t + 1, lambda b: fn(1, b))
                high(n + SPL + 1)

            def block_of(dst, c0):
                return lambda g, b: sc.copy(dst[:, g, c0:c0 + 512], b[:, :])

            take_proj(0, take_gates)
            high(IN0 + 3)
            take_proj(1, two_heads(qT, 0))
            high(IN0 + 4)
            take_proj(2, two_heads(qT, 1))
            high(IN0 + 5)
            eng.wait_ge(g_in, 1)
            link(sc.activation(rowq[:, 2, :], rowq[:, 1, :], ACT.Abs))
            link(sc.activation(rowq[:, 3, :], rowq[:, 2, :], ACT.Exp, scale=-1.0))
            sc.activation(rowq[:, 8, :], rowq[:, 3, :], ACT.Ln, bias=C("one", ROWS)).then_inc(g_f, 1)
            take_proj(3, two_heads(kT, 0))
            high(IN0 + 6)
            take_proj(4, two_heads(kT, 1))
            high(IN0 + 7)
            eng.wait_ge(g_mu, 1)
            sc.activation(rowq[:, 9, :], rowq[:, 6, :], ACT.Exp, bias=m0[:, 0:1], scale=-1.0)
            sc.activation(rowq[:, 10, :], rowq[:, 7, :], ACT.Exp, scale=-1.0)
            sc.activation(rowq[:, 11, :], rowq[:, 5, :], ACT.Exp, bias=mlx[:, 1:2]).then_inc(g_ex, 1)
            for d in range(NDIR):
                eng.dma_start(o["m"][0, 0, d].rearrange("(h a) -> h a", a=1), mlx[32 * d:32 * d + 4, 0:1]
                              ).then_inc(stored_st, 16)
            pair(5, IN0 + 5, block_of(vrow, 0))
            pair(7, IN0 + 7, lambda g, b: sc.activation(sigo[:, g, :], b[:, :], ACT.Sigmoid))
            for w in range(3):
                pair(9 + 2 * w, IN0 + 9 + 2 * w, block_of(u, HW * w))

            for i in range(6):
                after_fill(i)
            for q in range(4):
                eng.wait_ge(g_colt, 1)
                eng.wait_ge(cv_ok, 6)
                eng.wait_ge(wt_mm, q + 1)
                d, g = q // 2, q % 2
                for h in range(NH):
                    r = 32 * d + 4 * g + h
                    ins = sc.activation(WT[:, 4 * q + h, :], bank[4 + q % 2][:, P * h:P * h + P], ACT.Exp,
                                        bias=cols[:, 0, r:r + 1])
                ins.then_inc(wt_ok, 1)
                if q % 2:
                    after_fill(6 + q // 2)
            for i in range(8, 12):
                after_fill(i)
            for d in range(NDIR):
                eng.wait_ge(cs_ok, d + 1)
                sc.copy(cout[:, d, :], bank[4 + d][:, :]).then_inc(cs_t, 1)
            sc.copy(sml[:, 240:248], bank[3][:, 288:296]).then_inc(cs_t, 1)
            eng.wait_ge(hs_q, 1)
            sc.activation(sml[:, 40:48], sml[:, 32:40], ACT.Sqrt, bias=C("eps"), scale=1.0 / HD).then_inc(hs_r, 1)
            eng.wait_ge(cs_t, 3)
            eng.dma_start(o["C"][0, 0].rearrange("d h i j -> i (d h) j"),
                          cout.rearrange("p d (h j) -> p (d h) j", h=NH)).then_inc(stored_st, 16)
            eng.dma_start(o["n"][0, 0].rearrange("d h i -> i (d h)"), sml[:, 240:248]).then_inc(stored_st, 16)
            for i in range(12, 24):
                after_fill(i)
            take_turned(1, None)
            gate_rows_out(0)
            for n in range(WOUT + 3, FF0 + 2):
                high(n)

            norm_root(1)
            high(FF0 + 2)
            take_turned(2, 2)
            for c in range(NCH):
                chunk(FFN0, c)
                if c == 0:
                    gate_rows_out(1)
            high(QKV0)
            hidden_high(FFN0, NCH - 1)
            high(QKV0 + 1)

            eng.wait_ge(stored_st, STATE_STORES)
            norm_root(2)
            high(QKV0 + 2)
            take_turned(3, 1)
            def take_qkv(w):
                def take(g, b):
                    n = 512 if w < 2 else 256
                    sc.activation(sqs[:, g, 512 * w:512 * w + n], b[:, 0:n], ACT.Square)
                    return sc.copy(qkv[:, g, 512 * w:512 * w + 512], b[:, :])
                return take

            def take_queries(w):
                for g in range(G):
                    eng.wait_ge(at_t, 3 + 2 * w + g + 1)
                    sc.copy(aqT[:, 4 * w:4 * w + 4, T * g:T * g + T],
                            bank[4 + 2 * g + w][:, :].rearrange("p (j n) -> p j n", j=4)).then_inc(at_ta, 1)

            stats = sml[:, 0:48].rearrange("p (g n) -> p g n", g=G)
            for b, w in enumerate(QKV_BLOCKS):
                pair(15 + 2 * b, QKV0 + 2 * b, take_qkv(w))
                if b == 2:
                    take_queries(0)
                eng.wait_ge(q_sq, b + 1)
                c = stats[:, :, 8 * w:min(8 * w + 8, QH + KV)]
                sc.activation(c, c, ACT.Sqrt, bias=C("eps"), scale=1.0 / AHD).then_inc(q_rt, 1)
                if b == 0:
                    gate_rows_out(2)
                    eng.wait_ge(tj_t, 17)
                    eng.dma_start(o["v"][0, 0].rearrange("v s n -> s v n"),
                                  qkv[:, 0, 1280:1536].rearrange("p (v n) -> p v n", v=KV)).then_inc(stored_kv, 16)
                if b == 1:
                    eng.wait_ge(q_ok, 1)
                    eng.dma_start(o["k"][0, 0].rearrange("v s n -> s v n"),
                                  qkv[:, 0, 1024:1280].rearrange("p (v n) -> p v n", v=KV)).then_inc(stored_kv, 16)
            take_queries(1)
            warm(ACT.Exp)
            for v in range(KV):
                b = 3 * (v % 2)
                eng.wait_ge(sc_m, v + 1)
                if v >= 2:
                    eng.wait_ge(pt_mm, 3 * (v - 1))
                for i in range(12):
                    part, h = i // 4, i % 4
                    at = 8 * v + 4 * (part > 0) + h
                    ins = sc.activation(Pb[v % 2][:, P * i:P * i + P], bank[b + part][:, P * h:P * h + P], ACT.Exp,
                                        bias=sml[:, 64 + at:65 + at], scale=AHD ** -0.5,
                                        accum_out=sml[:, 96 + 12 * v + i:97 + 12 * v + i])
                sc.activation(sml[:, 144 + 8 * v:152 + 8 * v], sml[:, 176 + 8 * v:184 + 8 * v], ACT.Exp
                              ).then_inc(sc_e, 1)
                for q in range(3):
                    n = 3 * v + q
                    eng.wait_ge(pt_mm, n + 1)
                    if v >= 2 and q == 0:
                        eng.wait_ge(pv_mm, v - 1)
                    sc.copy(PTb[v % 2][:, 512 * q:512 * q + 512], bank[6 + n % 2][:, :]).then_inc(pt_t, 1)
            take_turned(4, None)
            for n in range(AOUT + 3, AOUT + 6):
                high(n)

            eng.wait_ge(stored_kv, 32)
            norm_root(3)
            high(MOE0 + 2)
            take_turned(5, 3)
            warm(ACT.Exp)
            for q in range(4):
                eng.wait_ge(hr_mm, q + 1)
                sc.copy(xn[:, q // 2, 512 * (q % 2):512 * (q % 2) + 512], bank[4 + q][:, :]).then_inc(hr_t, 1)
            eng.wait_ge(r_l, 1)
            sc.activation(rw[:, 16:32], rw[:, 16:32], ACT.Exp).then_inc(r_e, 1)
            warm(ACT.Silu)
            gate_rows_out(3)

            def gather(n0, par, p=None, step=0):
                for q in range(2):
                    eng.wait_ge(gj, plus(p, 3 * step, 3 * n0 + q + 1))
                    sc.copy(x_hi[:, 4 * q:4 * q + 4, T * par:T * par + T],
                            bank[2 + q][:, :].rearrange("p (k n) -> p k n", k=4)).then_inc(x_h, 1)
                eng.wait_ge(gj, plus(p, 3 * step, 3 * n0 + 3))
                sc.copy(PselT[par][:], bank[7][:, 0:G * T]).then_inc(gj_t, 1)

            def experts(r):
                if r:
                    for n in range(SPL):
                        ffn_high(expert(None, 0, r), n)
                gather(GATHERS * r, 0)
                with eng.Fori(0, NE // XB) as p:
                    for i in range(XB):
                        f = expert(p, i, r)
                        for c in range(NCH):
                            chunk(f, c)
                        with next_expert(eng, p, i):
                            ffn_high(f, NFW)
                        gather(GATHERS * r + i + 1, 1 - i % 2, p, XB)
                        hidden_high(f, NCH - 1)
                        with next_expert(eng, p, i):
                            ffn_high(f, NFW + 1)
                        eng.wait_ge(used, n_split(f, NFW - 1))
                        sc.copy(y_hi[:, 0:512], bank[4][:, :])
                        sc.copy(y_hi[:, 512:D], bank[5][:, :]).then_inc(y_a, 1)
                        with next_expert(eng, p, i):
                            ffn_high(f, NFW + 2)

            eng.wait_ge(r_ok, 1)
            experts(0)
            crowded = eng.value_load(flag[0:1, 0:1], min_val=0, max_val=1)
            with eng.If(crowded > 0):
                experts(1)
            eng.wait_ge(fin, 1)
            for g, name in enumerate(("y_prompt", "y_sample")):
                eng.dma_start(o[name][0], x[:, g, :]).then_inc(stored, 16)

        @block.vector
        def _(eng):
            v_ = nc.vector
            n_chain = [0]

            def link(ins):
                n_chain[0] += 1
                ins.then_inc(dve, 1)
                eng.wait_ge(dve, n_chain[0])

            def bc(ap, n):
                return ap.unsqueeze(len(ap.shape)).to_broadcast([*ap.shape, n])

            link(v_.memset(mlx[:], 0.0))

            def low(n0, n1=None):
                for n in range(n0, n0 + 1 if n1 is None else n1):
                    low_of(eng, n)

            eng.wait_ge(cond_ok, 1)
            v_.tensor_tensor(cond_hl[:, :, G:2 * G], condT[:], cond_hl[:, :, 0:G].bitcast(F32), ALU.subtract
                             ).then_inc(cond_s, 1)

            def range_reduce(n):
                s = sinb[0:64, :, :]
                link(v_.tensor_scalar(s[:, 1, :], s[:, 0, :], 1.0 / TWO_PI, RND, ALU.mult, ALU.add))
                link(v_.tensor_scalar(s[:, 1, :], s[:, 1, :], RND, None, ALU.subtract))
                c1 = float(np.float32(6.28125))
                c2 = float(np.float32(1.9350051879882812e-03))
                c3 = float(TWO_PI - 6.28125 - 1.9350051879882812e-03)
                link(v_.scalar_tensor_tensor(s[:, 2, :], s[:, 1, :], -c1, s[:, 0, :], ALU.mult, ALU.add))
                link(v_.scalar_tensor_tensor(s[:, 0, :], s[:, 1, :], -c2, s[:, 2, :], ALU.mult, ALU.add))
                link(v_.scalar_tensor_tensor(s[:, 2, :], s[:, 1, :], -c3, s[:, 0, :], ALU.mult, ALU.add))
                v_.tensor_scalar(s[:, 3, :], s[:, 2, :], -3.1415925, 3.1415925, ALU.max, ALU.min).then_inc(f_arg, 1)

            low(0, 9)
            eng.wait_ge(ac_mm, 1)
            v_.tensor_copy(adac[:], bank[3][:, 3 * P:4 * P]).then_inc(ac_t, 1)
            low(9, 12)
            eng.wait_ge(ld_h, 16 * 6)
            for n in range(2):
                eng.wait_ge(f_mm, n + 1)
                if n:
                    eng.wait_ge(f_sin, n)
                link(v_.tensor_scalar(sinb[0:64, 0, :], bank[3][0:64, P * n:P * n + P], hyp[:, 64 + n:65 + n],
                                      hyp[:, 66 + n:67 + n], ALU.add, ALU.mult))
                range_reduce(n)
                low(12 + 3 * n, 15 + 3 * n)
            eng.wait_ge(f_mm, 3)
            for q in range(4):
                ins = v_.tensor_tensor(taps[:, q, :], bank[4 + q][:, :], C("decay"), ALU.mult)
            ins.then_inc(f_tap, 1)
            link(v_.memset(rowq[:, 4:8, :], 0.0))
            low(18, 21)
            eng.wait_ge(ld_h2, 16)
            for r in range(2):
                if r:
                    low(21)
                eng.wait_ge(f_mm, 4 + r)
                link(v_.reciprocal(Gb[:, 1, 512 * r:512 * r + 512], bank[6 + r][:, :]))
                if r:
                    low(22)
                for d in range(NDIR):
                    link(v_.tensor_tensor(taps[:, 2 * r + d, :], taps[:, 2 * r + d, :],
                                          Gb[:, 1, 512 * r:512 * r + 512], ALU.mult))
                v_.tensor_tensor(taps[0:1, 2 * r, :], taps[0:1, 2 * r, :], skip[:, 512 * r:512 * r + 512], ALU.add
                                 ).then_inc(f_nrm, 1)

            def mod_columns(l):
                eng.wait_ge(ada_col, NB * (l + 1))
                link(v_.tensor_tensor(modc[:, l].rearrange("p a k g -> p (a k) g"),
                                      bank[2][:, P * l:P * l + 96].rearrange("p (m g) -> p m g", g=G),
                                      bc(modb[:, l, :], G), ALU.add))
                for i in range(2):
                    ins = v_.scalar_tensor_tensor(sca[:, l + 2 * i], modc[:, l, 1 + 3 * i], 1.0,
                                                  bc(ngc[:, l + 2 * i, :], G), ALU.add, ALU.mult)
                ins.then_inc(modc_ok, 1)

            def norm_rows(i):
                for g in range(G):
                    c = slice(2 * i + g, 2 * i + g + 1)
                    eng.wait_ge(n_rt, 2 * i + g + 1)
                    link(v_.reciprocal(rstd[:, c], rt[:, c]))
                    v_.tensor_scalar(xn[:, g, :], x[:, g, :], rstd[:, c], None, ALU.mult).then_inc(rows_ok, 1)

            def take_turned(s, norm):
                if norm is None:
                    for q in range(4):
                        g, h = q // 2, q % 2
                        part = slice(4 * h, 4 * h + 4), slice(T * g, T * g + T)
                        eng.wait_ge(x_h, inputs_split(s) - 3 + q)
                        v_.tensor_tensor(x_lo[:, part[0], part[1]], bank[4 + q][:, :].rearrange("p (j n) -> p j n", j=4),
                                         x_hi[:, part[0], part[1]].bitcast(F32), ALU.subtract).then_inc(x_l, 1)
                    return
                l, part = norm % 2, 3 * (norm // 2)
                for h in range(2):
                    eng.wait_ge(turned, 4 * s + 2 + h + 1)
                    if h == 0:
                        eng.wait_ge(modc_ok, l + 1)
                    for j in range(4):
                        k = 4 * h + j
                        ins = v_.tensor_scalar(hF[:, k, T:2 * T], bank[6 + h][:, P * j:P * j + P],
                                               sca[:, norm, k, 1:2], modc[:, l, part, k, 1:2], ALU.mult, ALU.add)
                    ins.then_inc(hT_d, 1)
                    if s < 5:
                        k4 = slice(4 * h, 4 * h + 4)
                        for g in range(G):
                            c = slice(T * g, T * g + T)
                            eng.wait_ge(x_h, inputs_split(s) - 3 + 2 * h + g)
                            v_.tensor_tensor(x_lo[:, k4, c], hF[:, k4, c], x_hi[:, k4, c].bitcast(F32), ALU.subtract
                                             ).then_inc(x_l, 1)
                if s < 5:
                    eng.wait_ge(x_l, inputs_split(s))

            def gate_source(s):
                l, part = s // 2, 2 + 3 * (s % 2)
                for g in range(G):
                    ins = v_.tensor_copy(Gb[:, g, :].rearrange("p (k n) -> p k n", k=KD),
                                         bc(modc[:, l, part, :, g], P))
                ins.then_inc(gbs, 1)

            def add_projection(n0, s):
                eng.wait_ge(gbt, 4 * (s + 1))
                w0 = WOUT if s == 0 else AOUT
                low(w0 + 3, w0 + 5)
                for i in range(4):
                    n, g, c = n0 + i, i % 2, slice(512 * (i // 2), 512 * (i // 2) + 512)
                    eng.wait_ge(used, w0 + 2 * (i // 2) + 2)
                    link(v_.tensor_tensor(tmpr[:, g, :], out_bank(n)[:, :], Gb[:, g, c], ALU.mult))
                    v_.tensor_tensor(x[:, g, c], x[:, g, c], tmpr[:, g, :], ALU.add).then_inc(ro_t, 1)
                    if i == 1:
                        low(w0 + 5)

            low(23)
            norm_rows(0)
            mod_columns(0)
            low(24)
            take_turned(0, 0)
            low(25, 28)

            eng.wait_ge(turned, 4)
            for d in range(NDIR):
                v_.tensor_copy(selr[:, 8 * d:8 * d + 8, :], bc(ident[0:ROWS, 32 * d:32 * d + 8], P)
                               ).then_inc(sel_ok, 1)
            eng.wait_ge(ld_g, 16 * 6)
            eng.wait_ge(g_rows, 1)
            v_.tensor_scalar(rowq[:, 0, :], bank[4][0:ROWS, 0:P], gb[:, 0:1], None, ALU.add)
            v_.tensor_scalar(rowq[:, 1, :], bank[4][0:ROWS, P:2 * P], gb[:, 1:2], None, ALU.add).then_inc(g_in, 1)
            low(28)
            eng.wait_ge(g_f, 1)
            link(v_.scalar_tensor_tensor(rowq[:, 2, :], rowq[:, 1, :], 0.0, rowq[:, 8, :], ALU.min, ALU.subtract))
            fwd, bwd = slice(0, 8), slice(32, 40)
            v_.tensor_tensor_scan(rowq[fwd, 4, :], ones[fwd, :], rowq[fwd, 2, :], 0.0, ALU.mult, ALU.add)
            link(v_.tensor_tensor_scan(rowq[bwd, 4, ::-1], ones[bwd, :], rowq[bwd, 2, ::-1], 0.0, ALU.mult, ALU.add))
            link(v_.tensor_tensor(rowq[:, 5, :], rowq[:, 0, :], rowq[:, 4, :], ALU.subtract))
            v_.tensor_tensor_scan(rowq[fwd, 6, :], ones[fwd, :], rowq[fwd, 5, :], m0[fwd, 0:1], ALU.mult, ALU.max)
            link(v_.tensor_tensor_scan(rowq[bwd, 6, ::-1], ones[bwd, :], rowq[bwd, 5, ::-1], m0[bwd, 0:1],
                                       ALU.mult, ALU.max))
            link(v_.tensor_tensor(rowq[:, 7, :], rowq[:, 4, :], rowq[:, 6, :], ALU.add))
            v_.tensor_copy(mlx[fwd, 0:1], rowq[fwd, 7, P - 1:P])
            v_.tensor_copy(mlx[bwd, 0:1], rowq[bwd, 7, 0:1])
            v_.tensor_scalar(mlx[fwd, 1:2], rowq[fwd, 6, P - 1:P], -1.0, None, ALU.mult)
            v_.tensor_scalar(mlx[bwd, 1:2], rowq[bwd, 6, 0:1], -1.0, None, ALU.mult)
            v_.tensor_scalar(rowq[:, 8, :], rowq[:, 6, :], -1.0, None, ALU.mult).then_inc(g_mu, 1)
            low(29, 36)
            eng.wait_ge(g_col, 1)
            v_.tensor_copy(cols[:, :, 0:ROWS], bank[3][:, 0:256].rearrange("p (i n) -> p i n", i=4)[:, :, 0:ROWS]
                           ).then_inc(g_colt, 1)

            eng.wait_ge(ld_cw, 16)

            def conv_taps(c):
                w, g = c // 2, c % 2
                uc = u[:, g, HW * w:HW * w + HW]
                eng.wait_ge(tj_t, 9 + c + 1)
                if c >= 2:
                    eng.wait_ge(cv_mm, c - 1)
                for i in range(2):
                    ins = v_.tensor_tensor(hyT[0][:, 2 * (c % 2) + i, :], uc, convw[:, 2 * i, HW * w:HW * w + HW],
                                           ALU.mult)
                ins.then_inc(cw_ok, 1)
                eng.wait_ge(cw_ok, c + 1)
                link(v_.tensor_tensor(uc, uc, convw[:, 1, HW * w:HW * w + HW], ALU.mult))

            def conv_sum(c):
                w, g = c // 2, c % 2
                uc = u[:, g, HW * w:HW * w + HW]
                eng.wait_ge(cv_mm, c + 1)
                v_.tensor_tensor(uc, uc, bank[1][:, :], ALU.add).then_inc(cv_ok, 1)

            low(36, 38)
            for c in range(6):
                conv_taps(c)
                if c == 1:
                    low(38, 42)
                if c:
                    conv_sum(c - 1)
                    low(41 + c)
            conv_sum(5)
            low(47)

            for q in range(4):
                g = q % 2
                eng.wait_ge(wt_ok, q + 1)
                eng.wait_ge(qk_ok, 2)
                v_.scalar_tensor_tensor(ST[:, 4 * q:4 * q + 4, :],
                                        bank[6 + g][:, :].rearrange("p (h n) -> p h n", h=NH), HD ** -0.5,
                                        WT[:, 4 * q:4 * q + 4, :], ALU.mult, ALU.mult).then_inc(st_ok, 1)
                if g:
                    low(48 + q // 2)
            den, rd, tiny = sml[:, 0:4], sml[:, 4:8], sml[:, 8:12]

            def heads(ap):
                return ap.rearrange("p (h n) -> p h n", h=NH)

            T0, T1 = heads(hyT[0][:, 0, :]), heads(hyT[0][:, 1, :])
            for q in range(4):
                d, g = q // 2, q % 2
                r = 32 * d + 4 * g
                if q == 3:
                    eng.wait_ge(kr_ok, 1)
                    for d in range(NDIR):
                        ins = v_.scalar_tensor_tensor(kw[:, d], heads(bank[6][:, :]), HD ** -0.5,
                                                      bc(cols[:, 3, 32 * d:32 * d + 4], HD), ALU.mult, ALU.mult)
                    ins.then_inc(kw_ok, 1)
                w_inter, floor = cols[:, 1, r:r + 4], cols[:, 2, r:r + 4]
                eng.wait_ge(nu_ok, q + 1)
                pden = bank[1 if g else 3][:, 256 + 4 * q:260 + 4 * q]
                if g:
                    link(v_.tensor_tensor(tiny, bank[1][:, 272 + 4 * d:276 + 4 * d], w_inter, ALU.mult))
                    link(v_.tensor_tensor(den, pden, tiny, ALU.add))
                    pden = den
                link(v_.scalar_tensor_tensor(tiny, pden, -1.0, floor, ALU.mult, ALU.max))
                link(v_.tensor_tensor(den, pden, tiny, ALU.max))
                link(v_.reciprocal(rd, den))
                num = heads(bank[4 + q % 2][:, :])
                hs = heads(xn[:, g, HW:2 * HW])
                dst = T1 if d else hs
                if g:
                    link(v_.tensor_tensor(T0, heads(bank[6 + d][:, :]), bc(w_inter, HD), ALU.mult))
                    link(v_.tensor_tensor(T0, T0, num, ALU.add))
                    link(v_.tensor_tensor(dst, T0, bc(rd, HD), ALU.mult))
                else:
                    link(v_.tensor_tensor(dst, num, bc(rd, HD), ALU.mult))
                eng.sem_inc(nu_t, 1)
                if d:
                    link(v_.tensor_tensor(hs, hs, T1, ALU.add))
                low(50 + q)
            hall = xn[:, :, HW:2 * HW]
            sq = hyT[0][:, 0:2, :]
            link(v_.tensor_tensor(sq, hall, hall, ALU.mult))
            v_.tensor_reduce(sml[:, 32:40], sq.rearrange("p g (h n) -> p (g h) n", h=NH), AX, ALU.add
                             ).then_inc(hs_q, 1)
            eng.wait_ge(ld_mg, 16)
            link(v_.tensor_tensor(sigo, sigo, mgain.unsqueeze(1).to_broadcast([P, G, HW]), ALU.mult))
            link(v_.tensor_tensor(hall, hall, sigo, ALU.mult))
            eng.wait_ge(hs_r, 1)
            link(v_.reciprocal(sml[:, 48:56], sml[:, 40:48]))
            for g in range(G):
                hg = heads(xn[:, g, HW:2 * HW])
                link(v_.tensor_tensor(hg, hg, bc(sml[:, 48 + 4 * g:52 + 4 * g], HD), ALU.mult))

            eng.wait_ge(cs_ok, 2)
            for r in range(2):
                A, B, Dd = spec[:, r, 0, :], spec[:, r, 1, :], spec[:, r, 2, :]
                for g in range(G):
                    n = 2 * r + g
                    eng.wait_ge(fz_mm, n + 1)
                    if n >= 2:
                        eng.wait_ge(iz_mm, n - 1)
                    Pz, Qz, t_ = bank[4 + 2 * g], bank[5 + 2 * g], hyT[g]
                    v_.tensor_tensor(t_[:, 0, :], Pz[:, :], A, ALU.mult)
                    v_.tensor_tensor(t_[:, 1, :], Qz[:, :], B, ALU.mult)
                    v_.tensor_tensor(t_[:, 2, :], Pz[:, :], B, ALU.mult)
                    link(v_.tensor_tensor(t_[:, 3, :], Qz[:, :], Dd, ALU.mult))
                    v_.tensor_tensor(t_[:, 0, :], t_[:, 0, :], t_[:, 1, :], ALU.subtract)
                    v_.tensor_tensor(t_[:, 2, :], t_[:, 2, :], t_[:, 3, :], ALU.add).then_inc(fz_ok, 1)
                    low(54 + 6 * r + g)
                for g in range(G):
                    eng.wait_ge(iz_mm, 2 * r + g + 1)
                    dst = xn[:, g, 0:HW] if r else u[:, g, 0:HW]
                    v_.tensor_tensor(dst, u[:, g, HW * (1 + r):HW * (2 + r)], bank[1 + 2 * g][:, :], ALU.mult
                                     ).then_inc(iz_ok, 1)
                    low(56 + 6 * r + 2 * g, 58 + 6 * r + 2 * g)
            eng.wait_ge(iz_ok, 4)
            for g in range(G):
                eng.sem_inc(rows_ok, 1)
            take_turned(1, None)
            eng.wait_ge(iz_mm, 4)
            gate_source(0)
            mod_columns(1)
            add_projection(0, 0)

            def ffn_low(f, i):
                low_of(eng, f[3] + i, f[1])

            def gated(f, c):
                for g in range(f[0]):
                    b, up, _ = unit_at(f, c, g)
                    eng.wait_ge(h_sa, n_unit(f, c, g))
                    v_.tensor_tensor(grow[b], sa[b], up[:, TW:2 * TW], ALU.mult).then_inc(h_g, 1)

            def hidden_low(f, c):
                for g in range(f[0]):
                    b, _, turn = unit_at(f, c, g)
                    eng.wait_ge(gh_ok, n_unit(f, c, g))
                    v_.tensor_tensor(g_lo[:, b, :], turn[:, 0:TW], g_hi[:, b, :].bitcast(F32), ALU.subtract
                                     ).then_inc(gl_ok, 1)

            def chunk(f, c):
                if c:
                    hidden_low(f, c - 1)
                if c:
                    ffn_low(f, 3 * c + 2)
                if c == 0:
                    ffn_low(f, 3)
                gated(f, c)
                if 0 < c < NCH - 1:
                    ffn_low(f, 3 * c + 3)
                if c < NCH - 1:
                    ffn_low(f, 3 * c + 4)

            norm_rows(1)
            low(FF0 + 2)
            take_turned(2, 2)
            gate_source(1)
            for c in range(NCH):
                chunk(FFN0, c)
            low(QKV0)
            hidden_low(FFN0, NCH - 1)
            eng.wait_ge(gbt, 8)
            for q in range(4):
                if q == 0:
                    eng.wait_ge(ff_g0, 1)
                if q == 2:
                    eng.wait_ge(used, QKV0)
                g, c = q // 2, slice(512 * (q % 2), 512 * (q % 2) + 512)
                link(v_.tensor_tensor(tmpf[:, q % 2, :], bank[4 + q][:, :], Gb[:, g, c], ALU.mult))
                link(v_.tensor_tensor(x[:, g, c], x[:, g, c], tmpf[:, q % 2, :], ALU.add))
                if q % 2:
                    eng.sem_inc(resid, 1)

            norm_rows(2)
            low(QKV0 + 1)
            take_turned(3, 1)
            low(QKV0 + 2)
            gate_source(2)
            stats = sml[:, 0:48].rearrange("p (g n) -> p g n", g=G)
            for b, w in enumerate(QKV_BLOCKS):
                nh = 8 if w < 2 else KV
                c = slice(8 * w, 8 * w + nh)
                if b < 2:
                    low(QKV0 + 3 + 2 * b)
                if b == 0:
                    low(QKV0 + 4)
                eng.wait_ge(tj_t, 15 + 2 * b + 2)
                for g in range(G):
                    ins = v_.tensor_reduce(stats[:, g, c],
                                           sqs[:, g, 512 * w:512 * w + AHD * nh].rearrange("p (h n) -> p h n", n=AHD),
                                           AX, ALU.add)
                ins.then_inc(q_sq, 1)
                eng.wait_ge(q_rt, b + 1)
                if b == 0:
                    eng.wait_ge(ld_at, 16 * 6)
                link(v_.reciprocal(stats[:, :, c], stats[:, :, c]))
                for g in range(G):
                    qk = qkv[:, g, 512 * w:512 * w + AHD * nh].rearrange("p (h n) -> p h n", n=AHD)
                    link(v_.tensor_tensor(qk, qk, bc(stats[:, g, c], AHD), ALU.mult))
                    gain = qkg[:, 0:64] if w < 2 else qkg[:, 64:128]
                    link(v_.tensor_tensor(qk, qk, gain.unsqueeze(1).to_broadcast([P, nh, AHD]), ALU.mult))
                half = qkv[:, 1, 512 * w:512 * w + AHD * nh].rearrange("p (h a b n) -> p h a b n", a=2, b=2, n=16)
                a1, a2 = half[:, :, :, 0, :], half[:, :, :, 1, :]
                cos, sin = (C(n).rearrange("p (a n) -> p a n", a=2).unsqueeze(1).to_broadcast([P, nh, 2, 16])
                            for n in ("cos", "sin"))
                tt = [rtmp[:, i, 0:32 * nh].rearrange("p (h a n) -> p h a n", a=2, n=16) for i in range(4)]
                v_.tensor_tensor(tt[0], a1, cos, ALU.mult)
                v_.tensor_tensor(tt[1], a2, sin, ALU.mult)
                v_.tensor_tensor(tt[2], a1, sin, ALU.mult)
                link(v_.tensor_tensor(tt[3], a2, cos, ALU.mult))
                v_.tensor_tensor(a1, tt[0], tt[1], ALU.subtract)
                link(v_.tensor_tensor(a2, tt[2], tt[3], ALU.add))
                eng.sem_inc(q_ok, 1)
                if b == 0:
                    for d in range(2):
                        ins = v_.tensor_copy(kd[:, :, :, d, :],
                                             qkv[:, :, 1024:1280].rearrange("p g (v n) -> p g v n", v=KV))
                    ins.then_inc(k_dup, 1)
                if b == 1:
                    for q in range(3):
                        eng.wait_ge(at_t, q + 1)
                        for odd in range(2):
                            part = slice(64 * odd, 64 * odd + 64)
                            src = bank[3 + 2 * q][part, :].rearrange("p (v n) -> p v n", v=KV)
                            dst = akT[odd][part, :, T * q:T * q + T] if q < 2 else ckT[odd][part]
                            ins = v_.tensor_copy(dst, src)
                        ins.then_inc(at_td, 1)

            def maxima(v):
                b = 3 * (v % 2)
                eng.wait_ge(sc_mm, v + 1)
                mx = sml[:, 208:220]
                for part in range(3):
                    ins = v_.tensor_reduce(mx[:, 4 * part:4 * part + 4],
                                           bank[b + part][:, :].rearrange("p (h n) -> p h n", h=4), AX, ALU.max)
                link(ins)
                link(v_.tensor_tensor(mx[:, 4:8], mx[:, 4:8], mx[:, 8:12], ALU.max))
                s4 = sinkb[:, 4 * v:4 * v + 4].unsqueeze(1).to_broadcast([P, 2, 4])
                m8 = mx[:, 0:8].rearrange("p (g h) -> p g h", g=2)
                neg = sml[:, 64 + 8 * v:72 + 8 * v]
                link(v_.scalar_tensor_tensor(m8, m8, AHD ** -0.5, s4, ALU.mult, ALU.max))
                link(v_.tensor_scalar(neg, mx[:, 0:8], -1.0, None, ALU.mult))
                link(v_.tensor_tensor(sml[:, 176 + 8 * v:184 + 8 * v].rearrange("p (g h) -> p g h", g=2),
                                      neg.rearrange("p (g h) -> p g h", g=2), s4, ALU.add))
                eng.sem_inc(sc_m, 1)

            def values(v):
                b = 3 * (v % 2)
                eng.wait_ge(sc_e, v + 1)
                sums, sk = sml[:, 96 + 12 * v:108 + 12 * v], sml[:, 144 + 8 * v:152 + 8 * v]
                link(v_.tensor_tensor(sk, sk, sums[:, 0:8], ALU.add))
                link(v_.tensor_tensor(sk[:, 4:8], sk[:, 4:8], sums[:, 8:12], ALU.add))
                link(v_.reciprocal(sk, sk))
                eng.wait_ge(pv_mm, v + 1)
                for g in range(G):
                    ins = v_.tensor_tensor(xn[:, g, TW * v:TW * v + TW].rearrange("p (h n) -> p h n", h=4),
                                           bank[b][:, TW * g:TW * g + TW].rearrange("p (h n) -> p h n", h=4),
                                           bc(sk[:, 4 * g:4 * g + 4], AHD), ALU.mult)
                ins.then_inc(pv_t, 1)

            maxima(0)
            for v in range(KV):
                if v + 1 < KV:
                    maxima(v + 1)
                values(v)
                if v < 3:
                    low(AOUT + v)
            eng.wait_ge(pv_t, KV)
            for g in range(G):
                eng.sem_inc(rows_ok, 1)
            take_turned(4, None)
            add_projection(4, 2)

            norm_rows(3)
            low(MOE0 + 2)
            take_turned(5, 3)
            L, E = rw[:, 0:16].rearrange("p (g e) -> p g e", g=G), rw[:, 16:32].rearrange("p (g e) -> p g e", g=G)
            sel = rw[:, 32:48].rearrange("p (g e) -> p g e", g=G)
            rank = rw[:, 48:64].rearrange("p (g e) -> p g e", g=G)
            top, dsum = rw[:, 64:66], rw[:, 66:68]
            gates = rw[:, 68:88].rearrange("p (g e) -> p g e", g=G)
            place = rw[:, 88:108].rearrange("p (g e) -> p g e", g=G)
            cnt = rw[:, 108:110]
            cmp1 = rw[:, 128:256].rearrange("p (g i j) -> p g i j", g=G, i=NE)
            cmp2 = rw[:, 256:384].rearrange("p (g i j) -> p g i j", g=G, i=NE)
            eng.wait_ge(ld_r, 32)
            eng.wait_ge(r_mm, 1)
            link(v_.tensor_tensor(L, bank[0][:, 0:16].rearrange("p (g e) -> p g e", g=G),
                                  msm[:, 64:72].unsqueeze(1).to_broadcast([P, G, NE]), ALU.add))
            link(v_.tensor_reduce(top, L, AX, ALU.max))
            v_.tensor_tensor(E, L, bc(top, NE), ALU.subtract).then_inc(r_l, 1)
            for g in range(G):
                Li = L[:, g, :].unsqueeze(2).to_broadcast([P, NE, NE])
                Lj = L[:, g, :].unsqueeze(1).to_broadcast([P, NE, NE])
                v_.tensor_tensor(cmp1[:, g], Lj, Li, ALU.is_gt)
                link(v_.tensor_tensor(cmp2[:, g], Lj, Li, ALU.is_equal))
                link(v_.tensor_tensor(cmp2[:, g], cmp2[:, g], C("tri").rearrange("p (i j) -> p i j", i=NE), ALU.mult))
                link(v_.tensor_tensor(cmp1[:, g], cmp1[:, g], cmp2[:, g], ALU.add))
            link(v_.tensor_reduce(rank, cmp1, AX, ALU.add))
            link(v_.tensor_scalar(sel, rank, 1.5, None, ALU.is_lt))
            v_.memset(gates, 0.0)
            link(v_.memset(place, -1.0))
            eng.sem_inc(r_sel, 1)
            eng.wait_ge(hr_t, 4)
            gate_source(3)
            eng.wait_ge(r_e, 1)
            link(v_.tensor_tensor(E, E, sel, ALU.mult))
            link(v_.tensor_reduce(dsum, E, AX, ALU.add))
            link(v_.reciprocal(dsum, dsum))
            link(v_.tensor_tensor(gates[:, :, 1:9], E, bc(dsum, NE), ALU.mult))
            eng.wait_ge(r_pos, 1)
            link(v_.tensor_tensor(place[:, :, 1:9], bank[1][:, 0:16].rearrange("p (g e) -> p g e", g=G), sel, ALU.mult))
            link(v_.tensor_scalar(place[:, :, 1:9], place[:, :, 1:9], 1.0, None, ALU.subtract))
            link(v_.tensor_reduce(cnt[:, 0:1], bank[1][:, 16:24], AX, ALU.max))
            link(v_.tensor_scalar(cnt[:, 1:2], cnt[:, 0:1], float(P) + 0.5, None, ALU.is_gt))
            link(v_.tensor_copy(flag[0:1, 0:1], cnt[0:1, 1:2]))
            v_.memset(acc, 0.0)
            v_.memset(y_hi[:].bitcast(F32), 0.0)
            v_.memset(y_lo[:].bitcast(F32), 0.0)
            link(v_.memset(PselT[1][:].bitcast(F32), 0.0))
            eng.sem_inc(y_a, 1)
            eng.sem_inc(y_d, 1)
            eng.sem_inc(r_ok, 1)

            def selector(par, r, e):
                for g in range(G):
                    ins = v_.tensor_scalar(Psel[par][:, g, :], C("iota")[:, P * r:P * r + P],
                                           place[:, g, bass.ds(e + 1, 1)], None, ALU.is_equal)
                ins.then_inc(p_ok, 1)

            def gather(n0, par, p=None, step=0):
                for q in range(2):
                    eng.wait_ge(x_h, plus(p, 2 * step, X0 + 2 * n0 + q + 1))
                    dst = slice(4 * q, 4 * q + 4), slice(T * par, T * par + T)
                    v_.tensor_tensor(x_lo[:, dst[0], dst[1]], bank[2 + q][:, :].rearrange("p (k n) -> p k n", k=4),
                                     x_hi[:, dst[0], dst[1]].bitcast(F32), ALU.subtract).then_inc(x_l, 1)

            def combined(n0, p, step, e, h):
                for q in (2 * h, 2 * h + 1):
                    c = slice(512 * (q % 2), 512 * (q % 2) + 512)
                    eng.wait_ge(cb, plus(p, 4 * step, 4 * n0 + q + 1))
                    v_.scalar_tensor_tensor(acc[:, h, c], bank[2 + q % 2][:, :], gates[:, h, bass.ds(e, 1)],
                                            acc[:, h, c], ALU.mult, ALU.add).then_inc(cb_t, 1)

            def experts(r):
                if r:
                    eng.wait_ge(gj, 3 * GATHERS * r)
                selector(0, r, 0)
                if r:
                    for n in range(SPL):
                        ffn_low(expert(None, 0, r), n)
                gather(GATHERS * r, 0)
                with eng.Fori(0, NE // XB) as p:
                    for i in range(XB):
                        f = expert(p, i, r)
                        for c in range(NCH):
                            chunk(f, c)
                            if c in (1, 3):
                                combined(GATHERS * r + i, p, XB, p * XB + i, c // 2)
                            if c == 6:
                                eng.wait_ge(gj, p * (3 * XB) + 3 * (GATHERS * r + i + 1))
                                selector(1 - i % 2, r, p * XB + (i + 1))
                        with next_expert(eng, p, i):
                            ffn_low(f, NFW)
                        gather(GATHERS * r + i + 1, 1 - i % 2, p, XB)
                        hidden_low(f, NCH - 1)
                        with next_expert(eng, p, i):
                            ffn_low(f, NFW + 1)
                        eng.wait_ge(y_a, p * XB + (r * NE + i + 2))
                        for h in range(2):
                            c = slice(512 * h, 512 * h + 512)
                            ins = v_.tensor_tensor(y_lo[:, c], bank[4 + h][:, :], y_hi[:, c].bitcast(F32), ALU.subtract)
                        ins.then_inc(y_d, 1)
                        with next_expert(eng, p, i):
                            ffn_low(f, NFW + 2)
                for h in range(G):
                    combined(GATHERS * r + NE, None, 0, NE, h)

            experts(0)
            crowded = eng.value_load(flag[0:1, 0:1], min_val=0, max_val=1)
            with eng.If(crowded > 0):
                experts(1)
            eng.wait_ge(gbt, 16)
            eng.wait_ge(cb_t, 4 * GATHERS)
            for q in range(4):
                g, c = q // 2, slice(512 * (q % 2), 512 * (q % 2) + 512)
                link(v_.tensor_tensor(acc[:, g, c], acc[:, g, c], Gb[:, g, c], ALU.mult))
                link(v_.tensor_tensor(x[:, g, c], x[:, g, c], acc[:, g, c], ALU.add))
            eng.sem_inc(fin, 1)

        @block.tensor
        def _(eng):
            pe = nc.tensor

            def mm(out, lhsT, rhs, start, stop):
                return pe.matmul(out, lhsT, rhs, start=start, stop=stop)

            def split3(out, hi, lo, w_h, w_l, tokens_held, first, last):
                if tokens_held:
                    mm(out, hi, w_h, first, False)
                    mm(out, hi, w_l, False, False)
                    return mm(out, lo, w_h, False, last)
                mm(out, w_h, hi, first, False)
                mm(out, w_h, lo, False, False)
                return mm(out, w_l, hi, False, last)

            def ada_main(i):
                n = i if i < 2 * NB else ADA1 + i - 2 * NB
                m = i // 2
                eng.wait_ge(lo_ok, n + 1)
                if i % 2 == 0 and m >= NB:
                    eng.wait_ge(ada_stg, m)
                elif i % 2 == 0 and m >= 2:
                    eng.wait_ge(ada_stg, m - 1)
                w_h, w_l = split_tile(n, HALFK)
                for kk in range(HALFK):
                    k = HALFK * (i % 2) + kk
                    mm(ada_bank(m)[0:2 * G, :], cond_hl[:, k, :], w_h[:, kk, :], k == 0, False)
                    ins = mm(ada_bank(m)[0:2 * G, :], cond_h0[:, k, :], w_l[:, kk, :], False, k == KD - 1)
                ins.then_inc(used, 1)

            def ada_cols(m):
                l, at = m // NB, m % NB
                eng.wait_ge(ada_stg, m + 1)
                for j in range(4):
                    c = P * l + 2 * (4 * at + j)
                    ins = mm(bank[2][:, c:c + 2], stage[:, m % 2, P * j:P * j + P], C("pair", 2 * G), True, True)
                ins.then_inc(ada_col, 1)

            eng.wait_ge(cond_s, 3)
            for i in range(2 * NB):
                ada_main(i)
                if i == 2:
                    eng.wait_ge(ld_k, 16)
                if i and i % 2 == 0:
                    ada_cols(i // 2 - 1)
                if i == 6:
                    eng.wait_ge(ld_a, 48)
                    pe.transpose(bank[3][:, 3 * P:4 * P], ada_rows, ident).then_inc(ac_mm, 1)
                if i == 9:
                    eng.wait_ge(ld_h, 16 * 6)
                    eng.wait_ge(ac_t, 1)
                    mm(bank[3][0:64, 0:P], hyw1[:], C("zt", 33), True, True).then_inc(f_mm, 1)
                if i == 12:
                    eng.wait_ge(f_sin, 1)
                    mm(bank[3][0:64, P:2 * P], hyp[:, 0:64], sinb[0:64, 4, :], True, True).then_inc(f_mm, 1)
                if i == 15:
                    eng.wait_ge(f_sin, 2)
                    for q in range(4):
                        ins = mm(bank[4 + q][:, :], sinb[0:64, 5, :], hyhw3[:, HW * q:HW * q + HW], True, True)
                    ins.then_inc(f_mm, 1)
                if i == 18:
                    eng.wait_ge(f_abs, 1)
                    eng.wait_ge(pz, 3)
                    for r in range(2):
                        mm(bank[6 + r][:, :], ones[:, :], mags[:, 2 * r, :], True, False)
                        mm(bank[6 + r][:, :], ones[:, :], mags[:, 2 * r + 1, :], False, True).then_inc(f_mm, 1)
                if i >= 20:
                    for q in ((i - 20,) if i < 2 * NB - 1 else (3, 4, 5)):
                        r, k = q // 3, q % 3
                        eng.wait_ge(f_nrm, r + 1)
                        if q >= 2:
                            eng.wait_ge(f_spt, q - 1)
                        mm(bank[4 + q % 2][:, :], C(("fc", "fs0", "fd")[k]), taps[:, 2 * r, :], True, False)
                        mm(bank[4 + q % 2][:, :], C(("gc", "gs0", "gd")[k]), taps[:, 2 * r + 1, :], False, True
                           ).then_inc(f_spec, 1)
            ada_cols(NB - 1)

            def turn_rows(s):
                for q in range(4):
                    g, half = q // 2, q % 2
                    if half == 0:
                        eng.wait_ge(rows_ok, 2 * s + g + 1)
                    for j in range(4):
                        c = 512 * half + P * j
                        ins = pe.transpose(bank[4 + q][:, P * j:P * j + P], xn[:, g, c:c + P], ident)
                    ins.then_inc(turned, 1)

            def wait_inputs(s, i):
                first = 2 if s in MODULATED else 3
                eng.wait_ge(x_l, inputs_split(s) - (0 if i else 4 - first))

            def proj(t, n, width):
                eng.wait_ge(lo_ok, n + 1)
                if t >= 3:
                    eng.wait_ge(tj_t, t - 2)
                b = bank[t % 3]
                if width is None:
                    w_h, w_l = split_tile(n, KD)
                    for h in range(2):
                        c = slice(P * h, P * h + P)
                        for k in range(KD):
                            ins = split3(b[:, TW * h:TW * h + TW], x_hi[:, k, :], x_lo[:, k, :], w_h[:, k, c],
                                         w_l[:, k, c], False, k == 0, k == KD - 1)
                else:
                    w_h, w_l = (t_[:, n % SPL, 0:KD * width].rearrange("p (k n) -> p k n", k=KD) for t_ in (w_hi, w_lo))
                    for k in range(KD):
                        ins = split3(b[0:width, 0:G * T], x_hi[:, k, :], x_lo[:, k, :], w_h[:, k, :], w_l[:, k, :],
                                     False, k == 0, k == KD - 1)
                ins.then_inc(used, 1)

            def proj_pair(s, n, banks, ready):
                for i in range(2):
                    wait_inputs(s, i)
                    eng.wait_ge(lo_ok, n + i + 1)
                    w_h, w_l = split_tile(n + i, HALFK)
                    for g in range(G):
                        if i == 0:
                            ready(g)
                        for kk in range(HALFK):
                            k, c = HALFK * i + kk, slice(T * g, T * g + T)
                            ins = split3(banks[g][:, :], x_hi[:, k, c], x_lo[:, k, c], w_h[:, kk, :], w_l[:, kk, :],
                                         True, k == 0, k == KD - 1)
                    ins.then_inc(used, 1)

            def in_pair(t, n):
                proj_pair(0 if t < 15 else 3, n, [bank[(t + g) % 3] for g in range(G)], lambda g: eng.wait_ge(tj_t, t + g - 2))

            eng.wait_ge(f_spt, 6)
            turn_rows(0)
            eng.wait_ge(modc_ok, 1)
            wait_inputs(0, 1)
            proj(0, IN0, 16)
            proj(1, IN0 + 1, None)
            proj(2, IN0 + 2, None)
            eng.wait_ge(tj_t, 1)
            for f in range(2):
                for g in range(G):
                    c = ROWS * (G * f + g)
                    ins = mm(bank[4][0:ROWS, P * f:P * f + P], C("spread", 16)[:, c:c + ROWS],
                             gcol[:, T * g:T * g + T], g == 0, g == 1)
            ins.then_inc(g_rows, 1)
            proj(3, IN0 + 3, None)
            proj(4, IN0 + 4, None)
            in_pair(5, IN0 + 5)
            eng.wait_ge(tj_t, 5)
            for g in range(G):
                for h in range(NH):
                    ins = mm(bank[6 + g][:, P * h:P * h + P], kT[:, h, T * g:T * g + T], qT[:, h, T * g:T * g + T],
                             True, True)
                ins.then_inc(qk_ok, 1)
            in_pair(7, IN0 + 7)
            eng.wait_ge(g_ex, 1)
            for i, r in enumerate((5, 9, 10, 11)):
                ins = mm(bank[3][:, 64 * i:64 * i + ROWS], rowq[:, r, :], ident[0:ROWS, 0:ROWS], True, True)
            ins.then_inc(g_col, 1)
            for w in range(3):
                in_pair(9 + 2 * w, IN0 + 9 + 2 * w)

            def fill(i):
                if i == 24:
                    eng.wait_ge(tj_t, 15)
                    eng.wait_ge(modc_ok, 1)
                ada_main(i)
                if i > 24 and i % 2 == 0:
                    ada_cols(i // 2 - 1)

            eng.wait_ge(tj_t, 15)
            for c in range(6):
                eng.wait_ge(cw_ok, c + 1)
                if c:
                    eng.wait_ge(cv_ok, c)
                for i in range(2):
                    ins = mm(bank[1][:, :], C("shift")[:, P * i:P * i + P], hyT[0][:, 2 * (c % 2) + i, :],
                             i == 0, i == 1)
                ins.then_inc(cv_mm, 1)
                fill(24 + c)
            eng.wait_ge(sel_ok, 2)
            eng.wait_ge(g_mu, 1)
            for q in range(4):
                if q >= 2:
                    eng.wait_ge(wt_ok, q - 1)
                d, g = q // 2, q % 2
                for h in range(NH):
                    out = bank[4 + q % 2][:, P * h:P * h + P]
                    mm(out, selr[:, 8 * d + 4 * g + h, :], rowq[:, 8, :], True, False)
                    ins = mm(out, ident, C("mask")[:, P * d:P * d + P], False, True)
                ins.then_inc(wt_mm, 1)
                if q % 2:
                    fill(30 + q // 2)
            eng.wait_ge(ld_n, 32)
            for q in range(4):
                d, g = q // 2, q % 2
                if g:
                    eng.wait_ge(ld_C[d], 16)
                eng.wait_ge(st_ok, 4)
                if q >= 2:
                    eng.wait_ge(nu_t, q - 1)
                if q == 3:
                    for h in range(NH):
                        ins = pe.transpose(bank[6][:, P * h:P * h + P], kT[:, h, 0:T], ident)
                    ins.then_inc(kr_ok, 1)
                for h in range(NH):
                    s_, v = ST[:, 4 * q + h, :], vrow[:, g, P * h:P * h + P]
                    mm(bank[4 + q % 2][:, P * h:P * h + P], s_, v, True, True)
                    ins = mm(bank[1 if g else 3][:, 256 + 4 * q + h:257 + 4 * q + h], s_, ones[:, 0:1], True, True)
                    if g:
                        qt = qT[:, h, T:2 * T]
                        mm(bank[6 + d][:, P * h:P * h + P], qt, stateC[d][:, h, :], True, True)
                        ins = mm(bank[1][:, 272 + 4 * d + h:273 + 4 * d + h], qt, nst[:, 4 * d + h:4 * d + h + 1],
                                 True, True)
                ins.then_inc(nu_ok, 1)
                fill(32 + q)
            eng.wait_ge(kw_ok, 1)
            eng.wait_ge(nu_t, 4)
            for d in range(NDIR):
                for h in range(NH):
                    k_ = kw[:, d, h, :]
                    mm(bank[4 + d][:, P * h:P * h + P], k_, vrow[:, 0, P * h:P * h + P], True, True)
                    ins = mm(bank[3][:, 288 + 4 * d + h:289 + 4 * d + h], k_, ones[:, 0:1], True, True)
                ins.then_inc(cs_ok, 1)

            eng.wait_ge(cs_t, 3)
            for r in range(2):
                for g in range(G):
                    if r:
                        eng.wait_ge(iz_ok, g + 1)
                    mm(bank[4 + 2 * g][:, :], C("fc"), u[:, g, 0:HW], True, True)
                    mm(bank[5 + 2 * g][:, :], C("fsn"), u[:, g, 0:HW], True, True).then_inc(fz_mm, 1)
                    fill(36 + 6 * r + g)
                for g in range(G):
                    eng.wait_ge(fz_ok, 2 * r + g + 1)
                    mm(bank[1 + 2 * g][:, :], C("ic"), hyT[g][:, 0, :], True, False)
                    mm(bank[1 + 2 * g][:, :], C("is"), hyT[g][:, 2, :], False, True).then_inc(iz_mm, 1)
                    fill(38 + 6 * r + 2 * g)
                    fill(39 + 6 * r + 2 * g)
            ada_cols(2 * NB - 1)
            turn_rows(1)

            def gate_rows(s):
                eng.wait_ge(gbs, s + 1)
                for q in range(4):
                    for j in range(4):
                        c = 512 * (q % 2) + P * j
                        ins = mm(bank[4 + q][:, P * j:P * j + P], Gb[:, q // 2, c:c + P], ident, True, True)
                    ins.then_inc(gbm, 1)

            def out_proj(n0, w0):
                for i in range(2):
                    n = n0 + 2 * i

                    def ready(g):
                        if n + g >= 4:
                            eng.wait_ge(ro_t, n + g - 3)
                        elif n + g == 2:
                            eng.wait_ge(modc_ok, 2)

                    proj_pair(1 if n0 == 0 else 4, w0 + 2 * i, [out_bank(n + g) for g in range(G)], ready)

            wait_inputs(1, 1)
            gate_rows(0)
            out_proj(0, WOUT)

            def wide(f, c, i):
                n = at_b(c) if i else at_a(c)
                w = (f[3] + n) % SPL
                hi, lo = (t[:, w, :].rearrange("p (k n) -> p k n", k=HALFK) for t in (w_hi, w_lo))
                eng.wait_ge(lo_ok, n_split(f, n))
                if f is FFN0 and c == 0:
                    wait_inputs(2, i)
                for g in range(f[0]):
                    b, up, _ = unit_at(f, c, g)
                    at = g if f is FFN0 else f[2] // NCH % 2
                    if i == 0 and (f is not FFN0 or c > 0):
                        eng.wait_ge(h_g, n_unit(f, c - (1 if f is FFN0 else 2), g))
                    for kk in range(HALFK):
                        k = HALFK * i + kk
                        xh, xl = (t[:, k, T * at:T * at + T] for t in (x_hi, x_lo))
                        mm(up[:, :], xh, hi[:, kk, :], k == 0, False)
                        mm(up[:, :], xh, lo[:, kk, :], False, False)
                        ins = mm(up[:, :], xl, hi[:, kk, :], False, k == KD - 1)
                ins.then_inc(used, 1)

            def turn_hidden(f, c):
                for g in range(f[0]):
                    b, _, turn = unit_at(f, c, g)
                    eng.wait_ge(h_g, n_unit(f, c, g))
                    for j in range(2):
                        ins = pe.transpose(turn[:, P * j:P * j + P], grow[b][:, P * j:P * j + P], ident)
                    ins.then_inc(h_t, 1)

            def down(f, c):
                n = at_w(c)
                w = (f[3] + n) % SPL
                hi, lo = (t[:, w, :].rearrange("p (j n) -> p j n", j=2) for t in (w_hi, w_lo))
                eng.wait_ge(lo_ok, n_split(f, n))
                for g in range(f[0]):
                    b, _, _ = unit_at(f, c, g)
                    eng.wait_ge(gl_ok, n_unit(f, c, g))
                    for j in range(2):
                        gh, gl = (t[:, b, P * j:P * j + P] for t in (g_hi, g_lo))
                        first, last = c == 0 and j == 0, c == NCH - 1 and j == 1
                        outs = [(bank[4 + 2 * g + h][:, :], slice(512 * h, 512 * h + 512)) for h in range(2)]
                        for out, cc in outs:
                            mm(out, gh, hi[:, j, cc], first, False)
                            mm(out, gh, lo[:, j, cc], False, False)
                        for out, cc in outs:
                            ins = mm(out, gl, hi[:, j, cc], False, last)
                    if f is FFN0 and last and g == 0:
                        ins.then_inc(ff_g0, 1)
                ins.then_inc(used, 1)

            turn_rows(2)
            eng.wait_ge(ro_t, 4)
            for c in range(NCH):
                wide(FFN0, c, 0)
                if c:
                    turn_hidden(FFN0, c - 1)
                wide(FFN0, c, 1)
                if c == 0:
                    wait_inputs(2, 1)
                    gate_rows(1)
                if c == 1:
                    eng.wait_ge(gbt, 8)
                if c:
                    down(FFN0, c - 1)
            turn_hidden(FFN0, NCH - 1)
            down(FFN0, NCH - 1)

            turn_rows(3)
            for b in range(3):
                in_pair(15 + 2 * b, QKV0 + 2 * b)
                if b == 0:
                    gate_rows(2)
                if b == 1:
                    eng.wait_ge(gbt, 12)
                    eng.wait_ge(k_dup, 1)
                    eng.wait_ge(ld_at, 16 * 6)
                    for q in range(3):
                        for v in range(KV):
                            src = (kd[:, q, v] if q < 2 else ckd[:, v]).rearrange("p d n -> p (d n)")
                            ins = pe.transpose(bank[3 + 2 * q][:, P * v:P * v + P], src, ident)
                        ins.then_inc(at_t, 1)

            def turn_queries(w):
                eng.wait_ge(q_ok, w + 2)
                for g in range(G):
                    for j in range(4):
                        c = 512 * w + P * j
                        ins = pe.transpose(bank[4 + 2 * g + w][:, P * j:P * j + P], qkv[:, g, c:c + P], ident)
                    ins.then_inc(at_t, 1)

            def scores(v):
                b = 3 * (v % 2)
                if v >= 2:
                    eng.wait_ge(pv_t, v - 1)
                    eng.wait_ge(sc_e, v - 1)
                for part, g in enumerate((0, 1, 1)):
                    for i in range(4):
                        h = 4 * v + i
                        keys = ckT[h % 2][:, v, :] if part == 1 else akT[h % 2][:, v, T * g:T * g + T]
                        ins = mm(bank[b + part][:, P * i:P * i + P], aqT[:, h // 2, T * g:T * g + T], keys, True, True)
                ins.then_inc(sc_mm, 1)

            turn_queries(0)
            eng.wait_ge(az, 4)
            eng.wait_ge(at_td, 3)
            eng.wait_ge(at_ta, 2)
            eng.wait_ge(tj_t, 21)
            scores(0)
            turn_queries(1)
            eng.wait_ge(at_ta, 4)
            for v in range(KV):
                if v + 1 < KV:
                    scores(v + 1)
                b = 3 * (v % 2)
                eng.wait_ge(sc_e, v + 1)
                for q in range(3):
                    n = 3 * v + q
                    if n >= 2:
                        eng.wait_ge(pt_t, n - 1)
                    for j in range(4):
                        i = 4 * q + j
                        ins = pe.transpose(bank[6 + n % 2][:, P * j:P * j + P], Pb[v % 2][:, P * i:P * i + P], ident)
                    ins.then_inc(pt_mm, 1)
                eng.wait_ge(pt_t, 3 * v + 3)
                for h in range(4):
                    own = slice(1280 + AHD * v, 1280 + AHD * v + AHD)
                    PT = [PTb[v % 2][:, P * (4 * q + h):P * (4 * q + h) + P] for q in range(3)]
                    mm(bank[b][:, AHD * h:AHD * h + AHD], PT[0], qkv[:, 0, own], True, True)
                    out = bank[b][:, TW + AHD * h:TW + AHD * h + AHD]
                    mm(out, PT[1], cv[:, AHD * v:AHD * v + AHD], True, False)
                    ins = mm(out, PT[2], qkv[:, 1, own], False, True)
                ins.then_inc(pv_mm, 1)
            turn_rows(4)
            eng.wait_ge(pv_t, 4)
            out_proj(4, AOUT)

            turn_rows(5)
            eng.wait_ge(hT_a, 8)
            eng.wait_ge(hT_d, 8)
            eng.wait_ge(ro_t, 8)
            eng.wait_ge(ld_r, 32)
            for g in range(G):
                for k in range(KD):
                    ins = mm(bank[0][:, NE * g:NE * g + NE], hF[:, k, T * g:T * g + T], msm[:, NE * k:NE * k + NE],
                             k == 0, k == KD - 1)
            ins.then_inc(r_mm, 1)
            for q in range(4):
                g = q // 2
                for j in range(4):
                    k = 4 * (q % 2) + j
                    ins = pe.transpose(bank[4 + q][:, P * j:P * j + P], hF[:, k, T * g:T * g + T], ident)
                ins.then_inc(hr_mm, 1)
            eng.wait_ge(r_sel, 1)
            sel = rw[:, 32:48].rearrange("p (g e) -> p g e", g=G)
            mm(bank[1][:, 0:8], C("prefix"), sel[:, 0, :], True, True)
            mm(bank[1][:, 8:16], C("prefix"), sel[:, 1, :], True, False)
            mm(bank[1][:, 8:16], ones[:, :], sel[:, 0, :], False, True)
            mm(bank[1][:, 16:24], ones[:, :], sel[:, 0, :], True, False)
            mm(bank[1][:, 16:24], ones[:, :], sel[:, 1, :], False, True).then_inc(r_pos, 1)
            eng.wait_ge(hr_t, 4)
            gate_rows(3)

            def gather(n0, par, p=None, step=0):
                eng.wait_ge(p_ok, plus(p, step, n0 + 1))
                if n0:
                    eng.wait_ge(cb_t, plus(p, 4 * step, 4 * n0))
                for q in range(2):
                    for kk in range(4):
                        k = 4 * q + kk
                        for g in range(G):
                            ins = mm(bank[2 + q][:, P * kk:P * kk + P], xn[:, g, P * k:P * k + P],
                                     Psel[par][:, g, :], g == 0, g == 1)
                    ins.then_inc(gj, 1)
                for g in range(G):
                    ins = pe.transpose(bank[7][:, T * g:T * g + T], Psel[par][:, g, :], ident)
                ins.then_inc(gj, 1)

            def combine(n0, p, step, r, par, h):
                if h == 0:
                    eng.wait_ge(gj_t, plus(p, step, (n0 + 1)))
                    eng.wait_ge(x_l, plus(p, 2 * step, X0 + 2 * (n0 + 1)))
                    eng.wait_ge(y_a, plus(p, step, n0 - r + 1))
                    eng.wait_ge(y_d, plus(p, step, n0 - r + 1))
                else:
                    eng.wait_ge(cb_t, plus(p, 4 * step, 4 * n0 + 2))
                for i in range(2):
                    sel_, c = PselT[par][:, T * h:T * h + T], slice(512 * i, 512 * i + 512)
                    mm(bank[2 + i][:, :], sel_, y_hi[:, c], True, False)
                    mm(bank[2 + i][:, :], sel_, y_lo[:, c], False, True).then_inc(cb, 1)

            def experts(r):
                gather(GATHERS * r, 0)
                with eng.Fori(0, NE // XB) as p:
                    for i in range(XB):
                        f = expert(p, i, r)
                        n0 = GATHERS * r + i
                        eng.wait_ge(x_l, p * (2 * XB) + (X0 + 2 * (n0 + 1)))
                        for c in range(NCH):
                            wide(f, c, 0)
                            if c:
                                turn_hidden(f, c - 1)
                            wide(f, c, 1)
                            if c == 1:
                                eng.wait_ge(y_a, p * XB + (n0 - r + 1))
                                eng.wait_ge(y_d, p * XB + (n0 - r + 1))
                            if c:
                                down(f, c - 1)
                            if c in (1, 3):
                                combine(n0, p, XB, r, 1 - i % 2, c // 2)
                        gather(n0 + 1, 1 - i % 2, p, XB)
                        turn_hidden(f, NCH - 1)
                        down(f, NCH - 1)
                for h in range(G):
                    combine(GATHERS * r + NE, None, 0, r, 1, h)

            eng.wait_ge(gbt, 16)
            eng.wait_ge(r_ok, 1)
            experts(0)
            crowded = eng.value_load(flag[0:1, 0:1], min_val=0, max_val=1)
            with eng.If(crowded > 0):
                experts(1)


_INS = ["x_prompt", "x_sample", "state_C", "state_n", "state_m", "cache_k", "cache_v", "c", "c_ctx",
        "norm1_g", "norm2_g", "w_ada", "b_ada", "ev_w_in", "ev_conv", "hy_w1", "hy_b1", "hy_w2", "hy_b2", "hy_w3",
        "hy_freq", "hy_d", "ml_b_gate", "ml_norm_g", "ev_w_out", "ff_w1", "ff_w3", "ff_w2", "at_w_qkv", "at_q_g",
        "at_k_g", "at_sink", "at_w_out", "moe_w_router", "moe_b_router", "moe_w1", "moe_w3", "moe_w2"]
_OUTS = [("y_prompt", (1, T, D)), ("y_sample", (1, T, D)), ("C", (1, 1, NDIR, NH, HD, HD)), ("n", (1, 1, NDIR, NH, HD)),
         ("m", (1, 1, NDIR, NH)), ("k", (1, 1, KV, T, AHD)), ("v", (1, 1, KV, T, AHD))]


def kernel(**inputs):
    import concourse.bacc as bacc
    from concourse.bass_utils import run_bass_kernel_spmd

    nc = bacc.Bacc("TRN2", target_bir_lowering=False, num_devices=1)
    arrays, ins, outs = {}, {}, {}
    for name in _INS + ["constants"]:
        arr = np.ascontiguousarray(inputs[name]) if name != "constants" else constants()
        arrays[f"in_{name}"] = arr
        ins[name] = nc.dram_tensor(f"in_{name}", arr.shape, mybir.dt.from_np(arr.dtype), kind="ExternalInput").ap()
    for name, shape in _OUTS:
        outs[name] = nc.dram_tensor(f"out_{name}", shape, F32, kind="ExternalOutput").ap()
    trunk(nc, ins, outs)
    r = run_bass_kernel_spmd(nc, [arrays], core_ids=[0])
    return tuple(r.results[0][f"out_{name}"] for name, _ in _OUTS)
```
